# Optimizing a Trainium2 kernel written in Bass

```python
import math
import jax
import jax.numpy as jnp
from jax import lax
import numpy as np

D_MODEL = 1024
BATCH = 1
SEQ = 256
DEPTH = 2

HEAD_DIM = 64
MIX_WIDTH = 768
MEM_HEADS = 4
MEM_WIDTH = MEM_HEADS * HEAD_DIM
N_MEM = 256
A_Q_HEADS = MIX_WIDTH // HEAD_DIM
A_KV_HEADS = 4
A_GROUP = A_Q_HEADS // A_KV_HEADS
WINDOW = 128
BLOCK = 128
B_HEADS = MIX_WIDTH // (2 * HEAD_DIM)
B_VDIM = 2 * HEAD_DIM
Q_BLOCK = 128
D_FF = 3584
N_EXPERTS = 8
TOP_K = 2
MOE_BLOCK = 128
EPS = 1e-6
NEG_INF = -1e30
N_EVEN = (DEPTH + 1) // 2
N_ODD = DEPTH // 2
A_QW = A_Q_HEADS * HEAD_DIM
A_KVW = A_KV_HEADS * HEAD_DIM
A_IN = A_QW + 2 * A_KVW + MEM_WIDTH
B_IN = 3 * MIX_WIDTH + MEM_WIDTH
OUT_IN = MIX_WIDTH + MEM_WIDTH

kernel_name = 'hybrid_swa_diffattn_memory_moe_encoder'

def rmsnorm(x, g):
    xf = x.astype(jnp.float32)
    y = xf * lax.rsqrt(jnp.mean(xf * xf, axis=-1, keepdims=True) + EPS)
    return (y * g.astype(jnp.float32)).astype(x.dtype)

def alibi_slopes(n):
    return jnp.exp2(-8.0 * jnp.arange(1, n + 1, dtype=jnp.float32) / n)

def windowed_gqa_sink(q, k, v, sink):
    B, S = q.shape[0], q.shape[1]
    nb = S // BLOCK
    qb = q.reshape(B, nb, BLOCK, A_KV_HEADS, A_GROUP, HEAD_DIM)

    def neighbours(t):
        tp = jnp.pad(t, ((0, 0), (BLOCK, BLOCK), (0, 0), (0, 0)))
        tp = tp.reshape(B, nb + 2, BLOCK, A_KV_HEADS, HEAD_DIM)
        return jnp.concatenate([tp[:, :-2], tp[:, 1:-1], tp[:, 2:]], axis=2)

    kb = neighbours(k)
    vb = neighbours(v)
    s = jnp.einsum('bnqkgd,bnskd->bnkgqs', qb, kb, preferred_element_type=jnp.float32) * HEAD_DIM ** -0.5
    qi = jnp.arange(BLOCK)[:, None]
    kj = jnp.arange(3 * BLOCK)[None, :]
    dist = jnp.abs(BLOCK + qi - kj)
    kpos = (jnp.arange(nb)[:, None] - 1) * BLOCK + jnp.arange(3 * BLOCK)[None, :]
    valid = (dist[None] <= WINDOW) & (kpos[:, None, :] >= 0) & (kpos[:, None, :] < S)
    slopes = alibi_slopes(A_Q_HEADS).reshape(A_KV_HEADS, A_GROUP)
    s = s - slopes[:, :, None, None] * dist.astype(jnp.float32)
    s = jnp.where(valid[None, :, None, None], s, NEG_INF)
    sink_col = jnp.broadcast_to(sink.astype(jnp.float32).reshape(A_KV_HEADS, A_GROUP, 1, 1), s.shape[:-1] + (1,))
    p = jax.nn.softmax(jnp.concatenate([s, sink_col], axis=-1), axis=-1)[..., :-1]
    out = jnp.einsum('bnkgqs,bnskd->bnqkgd', p.astype(v.dtype), vb)
    return out.reshape(B, S, A_QW)

def diff_attention(q, k, v, lam, subln_g, lambda_init):
    B, S = q.shape[0], q.shape[1]
    nq = S // Q_BLOCK
    slopes = alibi_slopes(B_HEADS)
    kpos = jnp.arange(S, dtype=jnp.float32)
    qb = q.reshape(B, nq, Q_BLOCK, B_HEADS, 2, HEAD_DIM).transpose(1, 0, 2, 3, 4, 5)
    starts = jnp.arange(nq, dtype=jnp.int32) * Q_BLOCK

    def one_block(args):
        qblk, start = args
        s = jnp.einsum('bqhcd,bshcd->bhcqs', qblk, k, preferred_element_type=jnp.float32) * HEAD_DIM ** -0.5
        qpos = (start + jnp.arange(Q_BLOCK, dtype=jnp.int32)).astype(jnp.float32)
        dist = jnp.abs(qpos[:, None] - kpos[None, :])
        s = s - slopes[None, :, None, None, None] * dist[None, None, None]
        p = jax.nn.softmax(s, axis=-1)
        w = p[:, :, 0] - lam * p[:, :, 1]
        return jnp.einsum('bhqs,bshe->bqhe', w.astype(v.dtype), v)

    out = lax.map(one_block, (qb, starts))
    out = out.transpose(1, 0, 2, 3, 4).reshape(B, S, B_HEADS, B_VDIM)
    out = rmsnorm(out, subln_g) * (1.0 - lambda_init)
    return out.reshape(B, S, MIX_WIDTH)

def memory_attention(qm, mk, mv):
    s = jnp.einsum('bqhd,bmhd->bhqm', qm, mk, preferred_element_type=jnp.float32) * HEAD_DIM ** -0.5
    p = jax.nn.softmax(s, axis=-1)
    o = jnp.einsum('bhqm,bmhd->bqhd', p.astype(mv.dtype), mv)
    return o.reshape(qm.shape[0], qm.shape[1], MEM_WIDTH)

def swiglu(h, wg, wu, wd):
    return (jax.nn.silu(h @ wg) * (h @ wu)) @ wd

def moe_swiglu(x, w_router, w_gate, w_up, w_down):
    B, S, D = x.shape
    T = B * S
    A = T * TOP_K
    t = x.reshape(T, D)
    logits = jnp.einsum('td,de->te', t, w_router, preferred_element_type=jnp.float32)
    top_v, top_e = lax.top_k(logits, TOP_K)
    gate = jax.nn.softmax(top_v, axis=-1)
    e_flat = top_e.reshape(A)
    tok_flat = jnp.repeat(jnp.arange(T, dtype=jnp.int32), TOP_K)
    g_flat = gate.reshape(A)
    order = jnp.argsort(e_flat)
    e_s = e_flat[order]
    tok_s = tok_flat[order]
    g_s = g_flat[order]
    counts = jnp.bincount(e_flat, length=N_EXPERTS)
    starts = jnp.cumsum(counts) - counts
    padded = (counts + MOE_BLOCK - 1) // MOE_BLOCK * MOE_BLOCK
    pends = jnp.cumsum(padded)
    pstarts = pends - padded
    dest = pstarts[e_s] + (jnp.arange(A, dtype=jnp.int32) - starts[e_s])
    n_blocks = A // MOE_BLOCK + N_EXPERTS
    P = n_blocks * MOE_BLOCK
    tok_p = jnp.zeros((P,), jnp.int32).at[dest].set(tok_s)
    g_p = jnp.zeros((P,), jnp.float32).at[dest].set(g_s)
    blk_e = jnp.minimum(jnp.searchsorted(pends, jnp.arange(n_blocks, dtype=jnp.int32) * MOE_BLOCK, side='right'), N_EXPERTS - 1)

    def expert_block(args):
        idx, e = args
        xb = t[idx]
        return swiglu(xb, w_gate[e], w_up[e], w_down[e])

    yb = lax.map(expert_block, (tok_p.reshape(n_blocks, MOE_BLOCK), blk_e))
    y = jnp.zeros((T, D), jnp.float32).at[tok_p].add(yb.reshape(P, D).astype(jnp.float32) * g_p[:, None])
    return y.astype(x.dtype).reshape(B, S, D)

def setup_inputs(seed: int = 0) -> dict:
    key = jax.random.key(seed)
    ks = jax.random.split(key, 20)
    f32 = jnp.float32

    def w(k, shape, fan_in):
        return jax.random.normal(k, shape, f32) * fan_in ** -0.5

    x = jax.random.normal(ks[0], (BATCH, SEQ, D_MODEL), f32)
    mem = jax.random.normal(ks[1], (BATCH, N_MEM, D_MODEL), f32)
    norm_g = 1.0 + 0.05 * jax.random.normal(ks[2], (DEPTH, 4, D_MODEL), f32)
    mem_norm_g = 1.0 + 0.05 * jax.random.normal(ks[3], (D_MODEL,), f32)
    w_mem_kv = w(ks[4], (D_MODEL, 2 * MEM_WIDTH), D_MODEL)
    a_w_in = w(ks[5], (N_EVEN, D_MODEL, A_IN), D_MODEL)
    a_sink = 0.5 * jax.random.normal(ks[6], (N_EVEN, A_Q_HEADS), f32)
    a_w_out = w(ks[7], (N_EVEN, OUT_IN, D_MODEL), OUT_IN)
    b_w_in = w(ks[8], (N_ODD, D_MODEL, B_IN), D_MODEL)
    b_lambda = 0.1 * jax.random.normal(ks[9], (N_ODD, 4, HEAD_DIM), f32)
    b_subln_g = 1.0 + 0.05 * jax.random.normal(ks[10], (N_ODD, B_VDIM), f32)
    b_w_out = w(ks[11], (N_ODD, OUT_IN, D_MODEL), OUT_IN)
    ffn_w_gate = w(ks[12], (N_EVEN, D_MODEL, D_FF), D_MODEL)
    ffn_w_up = w(ks[13], (N_EVEN, D_MODEL, D_FF), D_MODEL)
    ffn_w_down = w(ks[14], (N_EVEN, D_FF, D_MODEL), D_FF)
    moe_w_router = w(ks[15], (N_ODD, D_MODEL, N_EXPERTS), D_MODEL)
    moe_w_gate = w(ks[16], (N_ODD, N_EXPERTS, D_MODEL, D_FF), D_MODEL)
    moe_w_up = w(ks[17], (N_ODD, N_EXPERTS, D_MODEL, D_FF), D_MODEL)
    moe_w_down = w(ks[18], (N_ODD, N_EXPERTS, D_FF, D_MODEL), D_FF)
    return {'x': x, 'mem': mem, 'norm_g': norm_g, 'mem_norm_g': mem_norm_g, 'w_mem_kv': w_mem_kv,
            'a_w_in': a_w_in, 'a_sink': a_sink, 'a_w_out': a_w_out,
            'b_w_in': b_w_in, 'b_lambda': b_lambda, 'b_subln_g': b_subln_g, 'b_w_out': b_w_out,
            'ffn_w_gate': ffn_w_gate, 'ffn_w_up': ffn_w_up, 'ffn_w_down': ffn_w_down,
            'moe_w_router': moe_w_router, 'moe_w_gate': moe_w_gate, 'moe_w_up': moe_w_up, 'moe_w_down': moe_w_down}

def reference(x, mem, norm_g, mem_norm_g, w_mem_kv,
              a_w_in, a_sink, a_w_out,
              b_w_in, b_lambda, b_subln_g, b_w_out,
              ffn_w_gate, ffn_w_up, ffn_w_down,
              moe_w_router, moe_w_gate, moe_w_up, moe_w_down):
    B, S, _ = x.shape
    memn = rmsnorm(mem, mem_norm_g)
    mkv = memn @ w_mem_kv
    n_mem = mem.shape[1]
    mk = mkv[..., :MEM_WIDTH].reshape(B, n_mem, MEM_HEADS, HEAD_DIM)
    mv = mkv[..., MEM_WIDTH:].reshape(B, n_mem, MEM_HEADS, HEAD_DIM)

    for i in range(DEPTH):
        j = i // 2
        g = norm_g[i]
        h = rmsnorm(x, g[0])
        if i % 2 == 0:
            proj = h @ a_w_in[j]
            q, k, v, qm = jnp.split(proj, [A_QW, A_QW + A_KVW, A_QW + 2 * A_KVW], axis=-1)
            mix = windowed_gqa_sink(q.reshape(B, S, A_Q_HEADS, HEAD_DIM),
                                    k.reshape(B, S, A_KV_HEADS, HEAD_DIM),
                                    v.reshape(B, S, A_KV_HEADS, HEAD_DIM), a_sink[j])
            w_out = a_w_out[j]
        else:
            proj = h @ b_w_in[j]
            q, k, v, qm = jnp.split(proj, [MIX_WIDTH, 2 * MIX_WIDTH, 3 * MIX_WIDTH], axis=-1)
            lambda_init = 0.8 - 0.6 * math.exp(-0.3 * i)
            lp = b_lambda[j].astype(jnp.float32)
            lam = jnp.exp(jnp.sum(lp[0] * lp[1])) - jnp.exp(jnp.sum(lp[2] * lp[3])) + lambda_init
            mix = diff_attention(q.reshape(B, S, B_HEADS, 2, HEAD_DIM),
                                 k.reshape(B, S, B_HEADS, 2, HEAD_DIM),
                                 v.reshape(B, S, B_HEADS, B_VDIM), lam, b_subln_g[j], lambda_init)
            w_out = b_w_out[j]
        mem_out = memory_attention(qm.reshape(B, S, MEM_HEADS, HEAD_DIM), mk, mv)
        o = jnp.concatenate([mix, mem_out], axis=-1) @ w_out
        x = x + rmsnorm(o, g[1])
        h = rmsnorm(x, g[2])
        if i % 2 == 0:
            f = swiglu(h, ffn_w_gate[j], ffn_w_up[j], ffn_w_down[j])
        else:
            f = moe_swiglu(h, moe_w_router[j], moe_w_gate[j], moe_w_up[j], moe_w_down[j])
        x = x + rmsnorm(f, g[3])
    return x


_drawn_inputs = setup_inputs


def setup_inputs(seed=0):
    import zlib

    import numpy as np

    out = dict(_drawn_inputs(seed))
    spreads = {}
    factors = {}
    for name, (base, spread) in spreads.items():
        noise = np.random.default_rng([zlib.crc32(name.encode()), seed]).standard_normal(out[name].shape)
        drawn = base * np.exp(spread * noise) if base else spread * noise
        out[name] = jnp.asarray(drawn.astype(out[name].dtype))
    for name, factor in factors.items():
        out[name] = (out[name] * factor).astype(out[name].dtype)
    return out
```

```python
import math
from contextlib import ExitStack

import concourse.bass as bass
from concourse import mybir

F32 = mybir.dt.float32
F32R = mybir.dt.float32r
I32 = mybir.dt.int32
ACT = mybir.ActivationFunctionType
ALU = mybir.AluOpType
AX = mybir.AxisListType.X

P = 128
D = 1024
T = 256
TT = T // P
KC = D // P
HEAD = 64
MIX = 768
MEMW = 256
A_HEADS, A_KV = 12, 4
B_HEADS = 6
M_HEADS = 4
WINDOW = 128
DFF = 3584
FCH = 512
NCH = DFF // FCH
FT = FCH // P
NE = 8
EPS = 1e-6
CAP = P
ROUNDS = T // CAP
LAMBDA_INIT = 0.8 - 0.6 * math.exp(-0.3)
FAR = 1e32
SCALE = HEAD ** -0.5

RAW_SLOTS = 6
CUT_SLOTS = 3

FFN_H = 14
B_SLAB = 7 + 3 * NCH
MOE_H = 2 * (B_SLAB + 7)
ROUND_H = 6 * NCH * NE


def slopes(n):
    return [2.0 ** (-8.0 * (i + 1) / n) for i in range(n)]


GROUPS = ([("A", h, 0) for h in range(A_HEADS)] + [("M", h, 0) for h in range(M_HEADS)]
          + [("B", h, c) for h in range(B_HEADS) for c in range(2)] + [("M", h, 0) for h in range(M_HEADS)])
PHASES = [(0, A_HEADS + M_HEADS), (A_HEADS + M_HEADS, len(GROUPS))]
ITEM_OF = {}
for _g, (_k, _h, _c) in enumerate(GROUPS):
    if _k != "B" or _c == 1:
        ITEM_OF[_g] = len(ITEM_OF)
GROUP_OF = {v: g for g, v in ITEM_OF.items()}


def block_of(g):
    kind, h, _ = GROUPS[g]
    layer = 0 if g < PHASES[0][1] else 1
    if kind == "B":
        return 8 + h, True
    c = h // 2 if kind == "A" else 6 + h // 2
    return 8 * layer + c, h % 2 == 1


def build_encoder(nc, x, mem, norm_g, mem_norm_g, w_mem_kv, a_w_in, a_sink, a_w_out, b_w_in, b_lambda,
                  b_subln_g, b_w_out, ffn_gate, ffn_up, ffn_down, router, moe_gate, moe_up, moe_down, out):
    ctx = ExitStack()
    with ctx:
        def sb(name, shape, dt=F32):
            return ctx.enter_context(nc.sbuf_tensor(name, shape, dt))

        def sem(name):
            return ctx.enter_context(nc.semaphore(name))

        raw = sb("raw", [P, RAW_SLOTS, 4, 512])
        w_hi = sb("w_hi", [P, CUT_SLOTS, 4, 512], F32R)
        w_lo = sb("w_lo", [P, CUT_SLOTS, 4, 512], F32R)
        x_sb = sb("x_sb", [P, TT, D])
        tok = sb("tok", [P, TT, D])
        act_hi = sb("act_hi", [P, KC, T], F32R)
        act_lo = sb("act_lo", [P, KC, T], F32R)
        at_hi = sb("at_hi", [P, FT, T], F32R)
        at_lo = sb("at_lo", [P, FT, T], F32R)
        g_row = sb("g_row", [P, 2, D])
        mkT = sb("mkT", [P, 2, T])
        mv = sb("mv", [P, TT, MEMW])
        dist_w = sb("dist_w", [P, TT, T])
        dist = sb("dist", [P, TT, T])
        ident = sb("ident", [P, P])
        ones = sb("ones", [P, P])
        before = sb("before", [P, P])
        slot_no = sb("slot_no", [P, P])
        ARENA = 12032
        arena = sb("arena", [P, ARENA])
        g_rows = sb("g_rows", [40, P])
        g_col = sb("g_col", [P, 40])
        router_sb = sb("router_sb", [P, KC, NE])
        router_hi = sb("router_hi", [P, KC, NE], F32R)
        router_lo = sb("router_lo", [P, KC, NE], F32R)
        sink = sb("sink", [P, A_HEADS])
        sink8 = sb("sink8", [P, A_HEADS])
        sub_g = sb("sub_g", [P, 1])
        small = sb("small", [P, 96])
        rt = sb("rt", [P, 16, TT * NE])
        over_i = sb("over_i", [P, 1], I32)

        class Carve:
            def __init__(self):
                self.at = 0

            def __call__(self, *shape):
                n = math.prod(shape)
                v = arena[:, self.at:self.at + n]
                self.at += n
                assert self.at <= ARENA
                if len(shape) == 2:
                    v = v.rearrange("p (a b) -> p a b", a=shape[0])
                elif len(shape) == 3:
                    v = v.rearrange("p (a b c) -> p a b c", a=shape[0], b=shape[1])
                return v

        carve = Carve()
        qT = carve(6, T)
        kT = carve(6, T)
        vv = carve(TT, MIX)
        qmT = carve(2, T)
        s_buf = carve(2, TT, T)
        p_buf = carve(2, TT, T)
        pT = carve(2, TT, T)
        o_raw = carve(6, T)
        o_rs = carve(6, T)
        sq = carve(2, T)
        lam_in = carve(4, HEAD)
        junk = arena[:, 8192:8192 + TT * D].rearrange("p (t d) -> p t d", t=TT)
        mem_sb = arena[:, 6 * T:6 * T + TT * D].rearrange("p (t d) -> p t d", t=TT)
        carve = Carve()
        hid = carve(TT, FCH)
        sil = carve(TT, FCH)
        y = carve(TT, D)
        y_e = carve(D)
        pick = carve(TT, P)
        pick2 = carve(TT, P)
        pickT = carve(TT, P)

        ss = small[:, 0:2]
        ms = small[:, 2:4]
        root = small[:, 4:6]
        rstd = small[:, 6:8]
        mx = small[:, 8:12].rearrange("p (a b) -> p a b", a=2)
        neg = small[:, 12:16].rearrange("p (a b) -> p a b", a=2)
        den = small[:, 16:20].rearrange("p (a b) -> p a b", a=2)
        e_sink = small[:, 20:24].rearrange("p (a b) -> p a b", a=2)
        inv = small[:, 24:28].rearrange("p (a b) -> p a b", a=2)
        tot = small[:, 28:32].rearrange("p (a b) -> p a b", a=2)
        lam_s = small[:, 32:34]
        lam_e = small[:, 34:36]
        neg_lam = small[:, 36:37]
        sub_gs = small[:, 37:38]
        inv_l = small[:, 38:42].rearrange("p (a b) -> p a b", a=2)
        over_f = small[:, 42:43]
        lg = [rt[:, i, :].rearrange("p (t e) -> p t e", t=TT) for i in range(16)]
        (logit, rev, eq1, mask1, logit2, eq2, mask2, gates, chosen, pos, r_tmp, r_tmp2) = lg[:12]
        m1, m2, r1, r2, m_d, m_e, g1, g2 = (rt[:, 12 + i // 4, (i % 4) * 4:(i % 4) * 4 + TT] for i in range(8))
        m_den = rt[:, 14, 0:TT]
        counts = rt[:, 15, 0:NE]

        bank = [ctx.enter_context(nc.psum_tensor(f"bank{i}", [P, 512], F32)) for i in range(8)]

        landed = [sem(f"landed{i}") for i in range(RAW_SLOTS)]
        cut_hi = sem("cut_hi")
        cut_lo = sem("cut_lo")
        w_used = sem("w_used")
        x_in, mem_in, consts_in = sem("x_in"), sem("mem_in"), sem("consts_in")
        g_in = [sem("g_in0"), sem("g_in1")]
        pool_step, consts = sem("pool_step"), sem("consts")
        dve_step = sem("dve_step")
        act_step = sem("act_step")
        g_turned = sem("g_turned")
        squares, mean_sq, rooted = sem("squares"), sem("mean_sq"), sem("rooted")
        normed, turned, act_hi_done, act_done = sem("normed"), sem("turned"), sem("act_hi_done"), sem("act_done")
        evac_act, evac_dve = sem("evac_act"), sem("evac_dve")
        res_done = sem("res_done")
        k_swapped = sem("k_swapped")
        scored, neg_max, exped, prob = sem("scored"), sem("neg_max"), sem("exped"), sem("prob")
        prob_turned, probT, pv_done = sem("prob_turned"), sem("probT"), sem("pv_done")
        blk_hi, blk_done, sq_summed = sem("blk_hi"), sem("blk_done"), sem("sq_summed")
        sub_root, sub_y, sub_hi = sem("sub_root"), sem("sub_y"), sem("sub_hi")
        lam_red, lam_exp = sem("lam_red"), sem("lam_exp")
        silu_done, hid_done = sem("silu_done"), sem("hid_done")
        hid_turned, at_hi_done, at_done = sem("hid_turned"), sem("at_hi_done"), sem("at_done")
        down_ps, y_added = sem("down_ps"), sem("y_added")
        logits_ps, gap, gap_exp, chosen_done = sem("logits_ps"), sem("gap"), sem("gap_exp"), sem("chosen_done")
        pos_ps, routed = sem("pos_ps"), sem("routed")
        picked, gathered, xe_hi, xe_done = sem("picked"), sem("gathered"), sem("xe_hi"), sem("xe_done")
        ye_act, ye_dve = sem("ye_act"), sem("ye_dve")
        picked2, pick_ps, pick_T = sem("picked2"), sem("pick_ps"), sem("pick_T")
        scattered, y_acc = sem("scattered"), sem("y_acc")
        rows_done, moved, y_final = sem("rows_done"), sem("moved"), sem("y_final")
        stored = sem("stored")

        MEM_N, A_N, FFN_N, B_N, MOE_N = range(5)
        gains = [mem_norm_g, norm_g[0, 0], norm_g[0, 2], norm_g[1, 0], norm_g[1, 2]]
        row_gains = [norm_g[0, 1], norm_g[0, 3], norm_g[1, 1], norm_g[1, 2], norm_g[1, 3]]

        def t_job(c0, dst):
            return ("T", c0, dst)

        def r_jobs(c0, w, dst):
            return [("R", c0, w, t, dst(t)) for t in range(TT)]

        slabs = {}
        slabs[0] = (w_mem_kv, 0, 512, [t_job(i * P, mkT[:, i, :]) for i in range(2)]
                    + r_jobs(256, 256, lambda t: mv[:, t, :]))
        slabs[1] = (a_w_in[0], MIX, 512, [t_job(i * P, kT[:, i, :]) for i in range(2)]
                    + r_jobs(256, 256, lambda t: vv[:, t, 0:256]))
        for s in range(2):
            slabs[2 + s] = (a_w_in[0], 384 * s, 384, [t_job(i * P, qT[:, 3 * s + i, :]) for i in range(3)])
        slabs[4] = (a_w_in[0], MIX + 512, 256, [t_job(i * P, qmT[:, i, :]) for i in range(2)])
        for s in range(2):
            slabs[5 + s] = (a_w_out[0], 512 * s, 512, r_jobs(0, 512, lambda t, s=s: tok[:, t, 512 * s:512 * s + 512]))
            slabs[B_SLAB + 5 + s] = (b_w_out[0], 512 * s, 512,
                                     r_jobs(0, 512, lambda t, s=s: tok[:, t, 512 * s:512 * s + 512]))
        for s in range(3):
            blocks = [4 * s + i for i in range(4)]
            slabs[B_SLAB + s] = (b_w_in[0], 512 * s, 512,
                                 [t_job(i * P, (qT[:, b, :] if b < 6 else kT[:, b - 6, :]))
                                  for i, b in enumerate(blocks)])
        slabs[B_SLAB + 3] = (b_w_in[0], 2 * MIX, 512, r_jobs(0, 512, lambda t: vv[:, t, 0:512]))
        slabs[B_SLAB + 4] = (b_w_in[0], 2 * MIX + 512, 512, r_jobs(0, 256, lambda t: vv[:, t, 512:768])
                             + [t_job(256 + i * P, qmT[:, i, :]) for i in range(2)])
        TURNS = {s: n for n, s in enumerate(sorted(slabs))}
        A_PROJ, A_OUT = [1, 2, 3, 4], [5, 6]
        B_PROJ, B_OUT = list(range(B_SLAB, B_SLAB + 5)), [B_SLAB + 5, B_SLAB + 6]

        def first_half(e, j):
            return MOE_H - 2 + 6 * NCH * e + 6 * j

        block = ctx.enter_context(nc.Block())

        @block.sync
        def _(sp):
            def load(h, c, src, view=None):
                slot = c % RAW_SLOTS
                if not isinstance(h, int) or h >= RAW_SLOTS:
                    sp.wait_ge(cut_lo, h - (RAW_SLOTS - 1))
                dst = raw[:, slot, :, :]
                if view is None:
                    dst = dst.rearrange("p a n -> p (a n)").rearrange("p (q n) -> p q n", q=2)
                else:
                    dst = dst[:, :, 0:view]
                sp.dma_start(dst, src).then_inc(landed[slot], 16)

            def load_cols(h, c, w, c0, width):
                v = w.rearrange("(k p) f -> p k f", p=P)
                for i in range(2):
                    load(h + i, c + i, v[:, 4 * i:4 * i + 4, c0:c0 + width], width)

            def load_chunk(h, c, w, j):
                v = w.rearrange("(k p) (j f) -> j p k f", p=P, f=FCH)[j]
                for i in range(2):
                    load(h + i, c + i, v[:, 4 * i:4 * i + 4, :], FCH)

            def load_down(h, c, w, j):
                v = w.rearrange("(j q p) n -> j p q n", q=FT, p=P)[j]
                for i in range(2):
                    load(h + i, c + i, v[:, 2 * i:2 * i + 2, :])

            def load_slab(s):
                w, c0, width, _ = slabs[s]
                load_cols(2 * s, 2 * s, w, c0, width)

            sp.dma_start(mem_sb, mem[0].rearrange("(t p) d -> p t d", p=P)).then_inc(mem_in, 16)
            sp.dma_start(x_sb[:, :, :], x[0].rearrange("(t p) d -> p t d", p=P)).then_inc(x_in, 16)
            for s in range(7):
                load_slab(s)
            load_chunk(FFN_H, FFN_H, ffn_gate[0], 0)
            load_chunk(FFN_H + 2, FFN_H + 2, ffn_up[0], 0)
            with sp.Fori(1, NCH) as j:
                c = FFN_H - 2
                load_chunk(c + 6 * j, c, ffn_gate[0], j)
                load_chunk(c + 6 * j + 2, c + 2, ffn_up[0], j)
                load_down(c + 6 * j + 4, c + 4, ffn_down[0], j - 1)
            load_down(FFN_H + 40, FFN_H + 40, ffn_down[0], NCH - 1)
            for s in B_PROJ + B_OUT:
                load_slab(s)

            def load_experts(base):
                c = MOE_H + base
                load_chunk(c, c, moe_gate[0, 0], 0)
                load_chunk(c + 2, c + 2, moe_up[0, 0], 0)
                c -= 2

                def chunk(h, e, j, e_down, j_down):
                    load_chunk(h, c, moe_gate[0, e], j)
                    load_chunk(h + 2, c + 2, moe_up[0, e], j)
                    load_down(h + 4, c + 4, moe_down[0, e_down], j_down)

                with sp.Fori(1, NCH) as j:
                    chunk(c + 6 * j, 0, j, 0, j - 1)
                with sp.Fori(1, NE) as e:
                    chunk(c + 42 * e, e, 0, e - 1, NCH - 1)
                    with sp.Fori(1, NCH) as j:
                        chunk(c + 42 * e + 6 * j, e, j, e, j - 1)
                load_down(c + ROUND_H, c + ROUND_H, moe_down[0, NE - 1], NCH - 1)

            load_experts(0)
            sp.wait_ge(routed, 1)
            over = sp.value_load(over_i[0:1, 0:1], min_val=0, max_val=T)
            with sp.If(over > CAP):
                load_experts(ROUND_H)
            for t in range(TT):
                sp.wait_ge(res_done, 4 + t)
                sp.dma_start(out[0, t * P:(t + 1) * P, :], x_sb[:, t, :]).then_inc(stored, 16)
            sp.wait_ge(stored, 16 * TT)

        @block.gpsimd
        def _(pool):
            for i, g in enumerate(gains):
                pool.dma_start(g_rows[8 * i:8 * i + 8, :], g.rearrange("(c p) -> c p", p=P)).then_inc(consts_in, 16)
            pool.dma_start(lam_in[:, :, :], b_lambda[0].unsqueeze(0).broadcast_to([P, 4, HEAD])).then_inc(consts_in, 16)
            pool.dma_start(sink[:, :], a_sink.broadcast_to([P, A_HEADS])).then_inc(consts_in, 16)
            pool.dma_start(sub_g[:, :], b_subln_g.rearrange("a p -> p a")).then_inc(consts_in, 16)
            pool.dma_start(router_sb[:, :, :], router[0].rearrange("(k p) e -> p k e", p=P)).then_inc(consts_in, 16)
            nc.gpsimd.memset(ident[:, :], 0.0).then_inc(pool_step, 1)
            nc.gpsimd.memset(ones[:, :], 1.0).then_inc(pool_step, 1)
            nc.gpsimd.iota(slot_no[:, :], [[1, P]], base=0, channel_multiplier=0,
                           allow_small_or_imprecise_dtypes=True).then_inc(consts, 1)
            for t in range(TT):
                nc.gpsimd.iota(rev[:, t, :], [[-1, NE]], base=NE, channel_multiplier=0,
                               allow_small_or_imprecise_dtypes=True).then_inc(consts, 1)
            nc.gpsimd.iota(dist_w[:, :, :], [[P, TT], [-1, T]], base=0, channel_multiplier=1,
                           allow_small_or_imprecise_dtypes=True).then_inc(consts, 1)
            pool.wait_ge(pool_step, 2)
            nc.gpsimd.affine_select(out=ident[:, :], in_=ident[:, :], compare_op=ALU.not_equal, fill=1.0,
                                    base=0, pattern=[[-1, P]], channel_multiplier=1).then_inc(consts, 1)
            nc.gpsimd.affine_select(out=before[:, :], in_=ones[:, :], compare_op=ALU.is_gt, fill=0.0,
                                    base=0, pattern=[[1, P]], channel_multiplier=-1).then_inc(consts, 1)
            pool.wait_ge(evac_act, TURNS[1] + 1)
            pool.wait_ge(evac_dve, TURNS[1] + 1)
            for i in range(2):
                pool.dma_start(kT[HEAD * i:HEAD * i + HEAD, 2:4, :],
                               kT[HEAD * (1 - i):HEAD * (1 - i) + HEAD, 0:2, :]).then_inc(k_swapped, 16)
            for r, g in enumerate(row_gains):
                if r >= 2:
                    pool.wait_ge(*[(res_done, 1), (res_done, 2), (res_done, 3)][r - 2])
                pool.dma_start(g_row[:, r % 2, :], g.unsqueeze(0).broadcast_to([P, D])).then_inc(g_in[r % 2], 16)

        @block.scalar
        def _(act):
            def cut(h, width=512):
                slot, ring = h % RAW_SLOTS, h % CUT_SLOTS
                act.wait_ge(landed[slot], 16 * (h // RAW_SLOTS + 1))
                if h >= CUT_SLOTS:
                    act.wait_ge(w_used, h - (CUT_SLOTS - 1))
                nc.scalar.activation(w_hi[:, ring, :, 0:width], raw[:, slot, :, 0:width],
                                     ACT.Copy).then_inc(cut_hi, 1)

            def cut_at(c, turns, width=512):
                slot, ring = c % RAW_SLOTS, c % CUT_SLOTS
                act.wait_ge(landed[slot], 16 * (c // RAW_SLOTS + 1) + 16 * turns)
                act.wait_ge(w_used, c - (CUT_SLOTS - 1) + 6 * turns)
                nc.scalar.activation(w_hi[:, ring, :, 0:width], raw[:, slot, :, 0:width],
                                     ACT.Copy).then_inc(cut_hi, 1)

            def width_of(h):
                return slabs[h // 2][2] if h // 2 in slabs else 512

            def cut_next(s):
                for h in (2 * s + 2, 2 * s + 3):
                    cut(h, width_of(h))

            def evacuate(s):
                n = TURNS[s]
                jobs = slabs[s][3]
                act.wait_ge(w_used, 2 * s + 2)
                for i in range(0, len(jobs), 2):
                    dst = jobs[i][-1]
                    w = jobs[i][2] if jobs[i][0] == "R" else T
                    last = nc.scalar.activation(dst, bank[4 * (n % 2) + i][:, 0:w], ACT.Copy)
                last.then_inc(evac_act, 1)

            def norm(k, src):
                for t in range(TT):
                    last = nc.scalar.activation(junk[:, t, :], src[:, t, :], ACT.Square, accum_out=ss[:, t:t + 1])
                last.then_inc(squares, 1)
                act.wait_ge(mean_sq, k + 1)
                nc.scalar.activation(root, ms, ACT.Sqrt).then_inc(rooted, 1)

            def turn_rows(k, g, pair_count=4):
                for c in range(KC):
                    if c % 2 == 0:
                        act.wait_ge(turned, 4 * k + c // 2 + 1)
                    last = nc.scalar.activation(act_hi[:, c, :], bank[4 + c // 2][:, (c % 2) * T:(c % 2 + 1) * T],
                                                ACT.Copy, scale=g_col[:, 8 * g + c:8 * g + c + 1])
                    last.then_inc(act_hi_done, 1)

            def exps(g):
                kind, h, _ = GROUPS[g]
                b = g % 2
                act.wait_ge(neg_max, g + 1)
                if g >= 2:
                    if g - 2 in ITEM_OF:
                        act.wait_ge(prob_turned, ITEM_OF[g - 2] + 1)
                    else:
                        act.wait_ge(prob, g)
                for t in range(TT):
                    src = bank[b][:, t * T:(t + 1) * T] if kind == "M" else s_buf[:, b, t, :]
                    last = nc.scalar.activation(p_buf[:, b, t, :], src, ACT.Exp, bias=neg[:, b, t:t + 1],
                                                scale=SCALE, accum_out=den[:, b, t:t + 1])
                if kind == "A":
                    last = nc.scalar.activation(e_sink[:, b, :], neg[:, b, :], ACT.Exp, bias=sink[:, h:h + 1])
                last.then_inc(exped, 1)

            def copy_probT(v):
                act.wait_ge(prob_turned, v + 1)
                if v >= 2:
                    act.wait_ge(pv_done, v - 1)
                nc.scalar.activation(pT[:, v % 2, :, :].rearrange("p a b -> p (a b)"), bank[2 + v % 2][:, :],
                                     ACT.Copy).then_inc(probT, 1)

            def finish_block(v):
                u, complete = block_of(GROUP_OF[v])
                if not complete:
                    return
                act.wait_ge(pv_done, v + 1)
                src = bank[4 + u % 2][:, 0:T]
                if GROUPS[GROUP_OF[v]][0] == "B":
                    h = u - 8
                    if h >= 2:
                        act.wait_ge(sq_summed, h - 1)
                    nc.scalar.activation(o_raw[:, h, :], src, ACT.Copy)
                    nc.scalar.activation(sq[:, h % 2, :], src, ACT.Square).then_inc(blk_hi, 1)
                else:
                    nc.scalar.activation(act_hi[:, u % 8, :], src, ACT.Copy).then_inc(blk_hi, 1)

            def attention(phase):
                g0, g1 = PHASES[phase]
                exps(g0)
                for g in range(g0, g1):
                    if g + 1 < g1:
                        exps(g + 1)
                    if g in ITEM_OF:
                        v = ITEM_OF[g]
                        copy_probT(v)
                        if v - 1 >= 0 and GROUP_OF[v - 1] >= g0:
                            finish_block(v - 1)
                finish_block(ITEM_OF[g1 - 1])

            def first_chunk(c, n, tiles):
                cut(c + 2)
                cut(c + 3)
                silu(n, tiles, c)
                cut(c + 4)
                cut(c + 5)

            def silu(n, tiles, h):
                act.wait_ge(w_used, h + 2)
                if not isinstance(n, int) or n >= 1:
                    act.wait_ge(hid_done, n)
                for t in range(tiles):
                    last = nc.scalar.activation(sil[:, t, :], bank[t][:, :], ACT.Silu)
                last.then_inc(silu_done, 1)

            def hidden_hi(n, tiles):
                act.wait_ge(hid_turned, n + 1)
                for t in range(tiles):
                    last = nc.scalar.activation(at_hi[:, :, t * P:(t + 1) * P],
                                                bank[6 + t][:, :].rearrange("p (f t) -> p f t", f=FT), ACT.Copy)
                last.then_inc(at_hi_done, 1)

            def chunk(c, turns, n, tiles, extra=None):
                cut_at(c + 2, turns)
                cut_at(c + 3, turns)
                silu(n, tiles, c + 6 * turns)
                hidden_hi(n - 1, tiles)
                cut_at(c + 4, turns)
                cut_at(c + 5, turns)
                if extra:
                    extra()
                cut_at(c + 6, turns)
                cut_at(c + 7, turns)

            act.wait_ge(consts_in, 16 * 9)
            nc.scalar.activation(router_hi[:, :, :], router_sb[:, :, :], ACT.Copy).then_inc(act_step, 1)
            act.wait_ge(mem_in, 16)
            norm(0, mem_sb)
            act.wait_ge(x_in, 16)
            cut(0, width_of(0))
            cut(1, width_of(1))
            act.wait_ge(g_turned, 2)
            turn_rows(0, MEM_N)
            norm(1, x_sb)
            cut_next(0)
            evacuate(0)
            turn_rows(1, A_N)
            for s in A_PROJ:
                cut_next(s)
                evacuate(s)
            act.wait_ge(lam_red, 1)
            nc.scalar.activation(lam_e, lam_s, ACT.Exp).then_inc(lam_exp, 1)
            attention(0)
            for s in A_OUT:
                cut_next(s)
                evacuate(s)
            act.wait_ge(evac_dve, TURNS[A_OUT[1]] + 1)
            act.wait_ge(evac_act, TURNS[A_OUT[1]] + 1)
            norm(2, tok)
            act.wait_ge(res_done, 1)
            norm(3, x_sb)
            turn_rows(2, FFN_N)

            first_chunk(FFN_H, 0, TT)
            with act.Fori(1, NCH) as j:
                chunk(FFN_H - 2, j, j, TT)
            hidden_hi(NCH - 1, TT)
            cut(FFN_H + 42)
            cut(FFN_H + 43)
            act.wait_ge(y_added, 4 * NCH + 1)
            norm(4, y)
            act.wait_ge(res_done, 2)
            norm(5, x_sb)
            turn_rows(3, B_N)
            for s in B_PROJ:
                cut_next(s)
                evacuate(s)
            attention(1)
            act.wait_ge(blk_done, 14)
            nc.scalar.activation(o_rs[:, :, :], o_rs[:, :, :], ACT.Sqrt).then_inc(sub_root, 1)
            act.wait_ge(sub_y, 1)
            nc.scalar.activation(act_hi[:, 0:B_HEADS, :], o_raw[:, :, :], ACT.Copy,
                                 scale=sub_gs).then_inc(sub_hi, 1)
            for s in B_OUT:
                cut_next(s)
                evacuate(s)
            act.wait_ge(evac_dve, TURNS[B_OUT[1]] + 1)
            act.wait_ge(evac_act, TURNS[B_OUT[1]] + 1)
            norm(6, tok)
            act.wait_ge(res_done, 3)
            norm(7, x_sb)
            turn_rows(4, MOE_N)
            act.wait_ge(gap, 1)
            nc.scalar.activation(m_e, m_d, ACT.Exp).then_inc(gap_exp, 1)

            def gathered_hi(q):
                act.wait_ge(gathered, q + 1)
                for i in range(2):
                    last = nc.scalar.activation(act_hi[:, 4 * i:4 * i + 4, 0:P],
                                                bank[1 + 2 * i][:, :].rearrange("p (c t) -> p c t", c=4), ACT.Copy)
                last.then_inc(xe_hi, 1)

            def expert_out(h):
                act.wait_ge(w_used, h + 1)
                nc.scalar.activation(y_e[:, 0:512], bank[4][:, :], ACT.Copy).then_inc(ye_act, 1)

            def copy_pickT(q):
                act.wait_ge(pick_ps, q + 1)
                nc.scalar.activation(pickT[:, :, :].rearrange("p a b -> p (a b)"), bank[7][:, 0:T],
                                     ACT.Copy).then_inc(pick_T, 1)

            def experts(r):
                c = MOE_H + r * ROUND_H
                n0 = NCH + r * NCH * NE
                q0 = r * NE
                gathered_hi(q0)
                first_chunk(c, n0, 1)
                c -= 2

                def rest(e):
                    if not isinstance(e, int) or e >= 1:
                        copy_pickT(q0 + e - 1)
                    chunk(c + 6, 7 * e, n0 + 7 * e + 1, 1)
                    with act.Fori(2, NCH - 1) as j:
                        chunk(c, 7 * e + j, n0 + 7 * e + j, 1)
                    last = isinstance(e, int) and e == NE - 1
                    chunk(c + 36, 7 * e, n0 + 7 * e + 6, 1,
                          None if last else (lambda: gathered_hi(q0 + e + 1)))

                rest(0)
                with act.Fori(1, NE - 1) as e:
                    chunk(c, 7 * e, n0 + 7 * e, 1)
                    expert_out(c + 42 * e + 5)
                    rest(e)
                chunk(c, 7 * (NE - 1), n0 + 7 * (NE - 1), 1)
                expert_out(c + 42 * (NE - 1) + 5)
                rest(NE - 1)
                hidden_hi(n0 + NE * NCH - 1, 1)
                expert_out(c + ROUND_H + 1)
                copy_pickT(q0 + NE - 1)

            experts(0)
            act.wait_ge(routed, 1)
            over = act.value_load(over_i[0:1, 0:1], min_val=0, max_val=T)
            with act.If(over > CAP):
                for h in range(2):
                    cut(MOE_H + ROUND_H + h)
                experts(1)
            act.wait_ge(y_final, 1)
            norm(8, y)

        @block.vector
        def _(dve):
            steps = [0]

            def chained(ins):
                steps[0] += 1
                ins.then_inc(dve_step, 1)
                dve.wait_ge(dve_step, steps[0])

            def cut(c, turns=0, width=512):
                slot, ring = c % RAW_SLOTS, c % CUT_SLOTS
                dve.wait_ge(cut_hi, c + 1 + 6 * turns)
                nc.vector.tensor_tensor(w_lo[:, ring, :, 0:width], raw[:, slot, :, 0:width],
                                        w_hi[:, ring, :, 0:width].bitcast(F32), ALU.subtract).then_inc(cut_lo, 1)

            def width_of(h):
                return slabs[h // 2][2] if h // 2 in slabs else 512

            def cut_next(s):
                for h in (2 * s + 2, 2 * s + 3):
                    cut(h, 0, width_of(h))

            def evacuate(s):
                n = TURNS[s]
                jobs = slabs[s][3]
                dve.wait_ge(w_used, 2 * s + 2)
                for i in range(1, len(jobs), 2):
                    w = jobs[i][2] if jobs[i][0] == "R" else T
                    last = nc.vector.tensor_copy(jobs[i][-1], bank[4 * (n % 2) + i][:, 0:w])
                last.then_inc(evac_dve, 1)

            def norm(k):
                dve.wait_ge(squares, k + 1)
                nc.vector.tensor_scalar(ms, ss, 1.0 / D, EPS, ALU.mult, ALU.add).then_inc(mean_sq, 1)
                dve.wait_ge(rooted, k + 1)
                chained(nc.vector.reciprocal(rstd, root))

            def scale_rows(k, src):
                for t in range(TT):
                    last = nc.vector.tensor_scalar(tok[:, t, :], src[:, t, :], rstd[:, t:t + 1], None, ALU.mult)
                last.then_inc(normed, 1)

            def turn_rows(k, g):
                for c in range(KC):
                    dve.wait_ge(act_hi_done, 8 * k + c - c % 2 + 2)
                    last = nc.vector.scalar_tensor_tensor(
                        out=act_lo[:, c, :], in0=bank[4 + c // 2][:, (c % 2) * T:(c % 2 + 1) * T],
                        scalar=g_col[:, 8 * g + c:8 * g + c + 1], in1=act_hi[:, c, :].bitcast(F32),
                        op0=ALU.mult, op1=ALU.subtract)
                last.then_inc(act_done, 1)

            def residual(r, src):
                dve.wait_ge(g_in[r % 2], 16 * (r // 2 + 1))
                for t in range(TT):
                    chained(nc.vector.scalar_tensor_tensor(out=src[:, t, :], in0=src[:, t, :], scalar=rstd[:, t:t + 1],
                                                           in1=g_row[:, r % 2, :], op0=ALU.mult, op1=ALU.mult))
                for t in range(TT):
                    last = nc.vector.tensor_tensor(x_sb[:, t, :], x_sb[:, t, :], src[:, t, :], ALU.add)
                    if r == 4:
                        last.then_inc(res_done, 1)
                if r != 4:
                    last.then_inc(res_done, 1)

            def max_of(g):
                kind, h, c = GROUPS[g]
                b = g % 2
                dve.wait_ge(scored, g + 1)
                src = bank[b][:, :].rearrange("p (t k) -> p t k", t=TT)
                if kind != "M":
                    slope = slopes(A_HEADS if kind == "A" else B_HEADS)[h]
                    d = dist_w if kind == "A" else dist
                    chained(nc.vector.scalar_tensor_tensor(
                        out=s_buf[:, b, :, :], in0=d[:, :, :], scalar=-slope / SCALE, in1=src,
                        op0=ALU.mult, op1=ALU.add))
                    src = s_buf[:, b, :, :]
                chained(nc.vector.reduce_max(mx[:, b, :], src, AX))
                if kind == "A":
                    ins = nc.vector.tensor_scalar(neg[:, b, :], mx[:, b, :], sink8[:, h:h + 1], -SCALE,
                                                  ALU.max, ALU.mult)
                else:
                    ins = nc.vector.tensor_scalar(neg[:, b, :], mx[:, b, :], -SCALE, None, ALU.mult)
                ins.then_inc(neg_max, 1)

            def normalise(g):
                kind, h, c = GROUPS[g]
                b = g % 2
                dve.wait_ge(exped, g + 1)
                d = den[:, b, :]
                if kind == "A":
                    chained(nc.vector.tensor_tensor(tot[:, b, :], d, e_sink[:, b, :], ALU.add))
                    d = tot[:, b, :]
                chained(nc.vector.reciprocal(inv[:, b, :], d))
                if kind == "B" and c == 1:
                    chained(nc.vector.tensor_scalar(inv_l[:, b, :], inv[:, b, :], neg_lam, None, ALU.mult))
                    dve.wait_ge(prob, g)
                    for t in range(TT):
                        last = nc.vector.scalar_tensor_tensor(
                            out=p_buf[:, b, t, :], in0=p_buf[:, b, t, :], scalar=inv_l[:, b, t:t + 1],
                            in1=p_buf[:, 1 - b, t, :], op0=ALU.mult, op1=ALU.add)
                else:
                    for t in range(TT):
                        last = nc.vector.tensor_scalar(p_buf[:, b, t, :], p_buf[:, b, t, :], inv[:, b, t:t + 1],
                                                       None, ALU.mult)
                last.then_inc(prob, 1)

            def finish_block(v):
                u, complete = block_of(GROUP_OF[v])
                if not complete:
                    return
                if GROUPS[GROUP_OF[v]][0] == "B":
                    h = u - 8
                    dve.wait_ge(sq_summed, h + 1)
                    nc.vector.tensor_scalar(o_rs[:, h, :], bank[6 + h % 2][:, 0:T], 1.0 / P, EPS,
                                            ALU.mult, ALU.add).then_inc(blk_done, 1)
                else:
                    dve.wait_ge(blk_hi, u + 1)
                    nc.vector.tensor_tensor(act_lo[:, u % 8, :], bank[4 + u % 2][:, 0:T],
                                            act_hi[:, u % 8, :].bitcast(F32), ALU.subtract).then_inc(blk_done, 1)

            def attention(phase):
                g0, g1 = PHASES[phase]
                max_of(g0)
                for g in range(g0, g1):
                    if g + 1 < g1:
                        max_of(g + 1)
                    normalise(g)
                    if g in ITEM_OF:
                        v = ITEM_OF[g]
                        if v - 2 >= 0 and GROUP_OF[v - 2] >= g0:
                            finish_block(v - 2)
                for v in (ITEM_OF[g1 - 1] - 1, ITEM_OF[g1 - 1]):
                    finish_block(v)

            def hidden(n, tiles, h):
                dve.wait_ge(silu_done, n + 1)
                dve.wait_ge(w_used, h + 4)
                for t in range(tiles):
                    last = nc.vector.tensor_tensor(hid[:, t, :], bank[2 + t][:, :], sil[:, t, :], ALU.mult)
                last.then_inc(hid_done, 1)

            def hidden_lo(n, tiles):
                dve.wait_ge(at_hi_done, n + 1)
                for t in range(tiles):
                    last = nc.vector.tensor_tensor(at_lo[:, :, t * P:(t + 1) * P],
                                                   bank[6 + t][:, :].rearrange("p (f t) -> p f t", f=FT),
                                                   at_hi[:, :, t * P:(t + 1) * P].bitcast(F32), ALU.subtract)
                last.then_inc(at_done, 1)

            def add_down(m, h):
                for i in range(4):
                    t, f = i // 2, i % 2
                    if i < 3:
                        dve.wait_ge(down_ps, 3 * m + i + 1)
                    else:
                        dve.wait_ge(w_used, h + 1)
                    dst = y[:, t, 512 * f:512 * f + 512]
                    dve.wait_ge(y_added, 4 * m + i + 1)
                    nc.vector.tensor_tensor(dst, bank[4 + f][:, :], dst, ALU.add).then_inc(y_added, 1)

            def chunk(c, turns, n, tiles, after_turn=None, after_hidden=None, down=None):
                cut(c + 2, turns)
                cut(c + 3, turns)
                hidden_lo(n - 1, tiles)
                if after_turn:
                    after_turn()
                cut(c + 4, turns)
                cut(c + 5, turns)
                hidden(n, tiles, c + 6 * turns)
                if after_hidden:
                    after_hidden()
                cut(c + 6, turns)
                if down is not None:
                    add_down(down, c + 5 + 6 * turns)
                cut(c + 7, turns)

            def first_chunk(c, n, tiles):
                cut(c + 2)
                cut(c + 3)
                hidden(n, tiles, c)
                cut(c + 4)
                cut(c + 5)

            dve.wait_ge(consts_in, 16 * 9)
            dve.wait_ge(consts, 6)
            nc.vector.tensor_scalar(sink8[:, :], sink[:, :], 1.0 / SCALE, None, ALU.mult)
            nc.vector.tensor_scalar(sub_gs, sub_g[:, :], 1.0 - LAMBDA_INIT, None, ALU.mult)
            dve.wait_ge(act_step, 1)
            nc.vector.tensor_tensor(router_lo[:, :, :], router_sb[:, :, :], router_hi[:, :, :].bitcast(F32),
                                    ALU.subtract)
            dve.wait_ge(g_turned, 1)
            nc.vector.tensor_copy(g_col[:, :], bank[0][:, 0:40]).then_inc(g_turned, 1)
            norm(0)
            scale_rows(0, mem_sb)
            cut(0)
            cut(1)
            turn_rows(0, MEM_N)
            norm(1)
            dve.wait_ge(turned, 4)
            scale_rows(1, x_sb)
            cut_next(0)
            evacuate(0)
            turn_rows(1, A_N)
            chained(nc.vector.scalar_tensor_tensor(out=dist[:, :, :], in0=dist_w[:, :, :], scalar=-1.0,
                                                   in1=dist_w[:, :, :], op0=ALU.mult, op1=ALU.max))
            chained(nc.vector.tensor_scalar(dist_w[:, :, :], dist[:, :, :], float(WINDOW), FAR, ALU.is_gt, ALU.mult))
            chained(nc.vector.tensor_tensor(dist_w[:, :, :], dist_w[:, :, :], dist[:, :, :], ALU.add))
            lam4 = lam_in[:, :, :].rearrange("p (a b) d -> p a b d", b=2)
            chained(nc.vector.tensor_tensor(lam4[:, :, 0, :], lam4[:, :, 0, :], lam4[:, :, 1, :], ALU.mult))
            nc.vector.reduce_sum(lam_s, lam4[:, :, 0, :], AX).then_inc(lam_red, 1)
            for s in A_PROJ:
                cut_next(s)
                evacuate(s)
            dve.wait_ge(lam_exp, 1)
            chained(nc.vector.tensor_tensor(neg_lam, lam_e[:, 1:2], lam_e[:, 0:1], ALU.subtract))
            chained(nc.vector.tensor_scalar(neg_lam, neg_lam, -LAMBDA_INIT, None, ALU.add))
            attention(0)
            for s in A_OUT:
                cut_next(s)
                evacuate(s)
            norm(2)
            dve.wait_ge(evac_act, TURNS[A_OUT[1]] + 1)
            dve.wait_ge(evac_dve, TURNS[A_OUT[1]] + 1)
            residual(0, tok)
            norm(3)
            scale_rows(2, x_sb)
            nc.vector.memset(y[:, :, :], 0.0).then_inc(y_added, 1)
            turn_rows(2, FFN_N)

            first_chunk(FFN_H, 0, TT)
            with dve.Fori(1, NCH) as j:
                chunk(FFN_H - 2, j, j, TT, down=j - 1)
            hidden_lo(NCH - 1, TT)
            cut(FFN_H + 42)
            add_down(NCH - 1, FFN_H + 41)
            cut(FFN_H + 43)
            norm(4)
            residual(1, y)
            norm(5)
            scale_rows(3, x_sb)
            turn_rows(3, B_N)
            for s in B_PROJ:
                cut_next(s)
                evacuate(s)
            attention(1)
            dve.wait_ge(sub_root, 1)
            chained(nc.vector.reciprocal(o_rs[:, :, :], o_rs[:, :, :]))
            nc.vector.tensor_tensor(o_raw[:, :, :], o_raw[:, :, :], o_rs[:, :, :], ALU.mult).then_inc(sub_y, 1)
            dve.wait_ge(sub_hi, 1)
            nc.vector.scalar_tensor_tensor(out=act_lo[:, 0:B_HEADS, :], in0=o_raw[:, :, :], scalar=sub_gs,
                                           in1=act_hi[:, 0:B_HEADS, :].bitcast(F32), op0=ALU.mult,
                                           op1=ALU.subtract).then_inc(sub_hi, 1)
            for s in B_OUT:
                cut_next(s)
                evacuate(s)
            norm(6)
            dve.wait_ge(evac_act, TURNS[B_OUT[1]] + 1)
            dve.wait_ge(evac_dve, TURNS[B_OUT[1]] + 1)
            residual(2, tok)
            norm(7)
            scale_rows(4, x_sb)
            turn_rows(4, MOE_N)
            dve.wait_ge(g_in[1], 32)
            for t in range(TT):
                nc.vector.tensor_tensor(tok[:, t, :], tok[:, t, :], g_row[:, 1, :], ALU.mult).then_inc(rows_done, 1)
            nc.vector.memset(y[:, :, :], 0.0).then_inc(y_acc, 1)

            def per_expert(v):
                return v.unsqueeze(2).broadcast_to([P, TT, NE])

            dve.wait_ge(logits_ps, 1)
            chained(nc.vector.tensor_copy(logit, bank[0][:, 0:TT * NE].rearrange("p (t e) -> p t e", t=TT)))

            def top(src, best, eq, first, mask):
                chained(nc.vector.reduce_max(best, src, AX))
                chained(nc.vector.tensor_tensor(eq, src, per_expert(best), ALU.is_equal))
                chained(nc.vector.tensor_tensor(eq, eq, rev, ALU.mult))
                chained(nc.vector.reduce_max(first, eq, AX))
                chained(nc.vector.tensor_tensor(mask, eq, per_expert(first), ALU.is_equal))

            top(logit, m1, eq1, r1, mask1)
            chained(nc.vector.scalar_tensor_tensor(out=logit2, in0=mask1, scalar=-3e38, in1=logit,
                                                   op0=ALU.mult, op1=ALU.add))
            top(logit2, m2, eq2, r2, mask2)
            nc.vector.tensor_tensor(m_d, m2, m1, ALU.subtract).then_inc(gap, 1)
            nc.vector.tensor_tensor(chosen, mask1, mask2, ALU.add).then_inc(chosen_done, 1)
            dve.wait_ge(gap_exp, 1)
            chained(nc.vector.tensor_scalar(m_den, m_e, 1.0, None, ALU.add))
            chained(nc.vector.reciprocal(g1, m_den))
            chained(nc.vector.tensor_tensor(g2, m_e, g1, ALU.mult))
            chained(nc.vector.tensor_tensor(r_tmp, mask1, per_expert(g1), ALU.mult))
            chained(nc.vector.tensor_tensor(r_tmp2, mask2, per_expert(g2), ALU.mult))
            chained(nc.vector.tensor_tensor(gates, r_tmp, r_tmp2, ALU.add))
            dve.wait_ge(pos_ps, 1)
            chained(nc.vector.tensor_copy(pos, bank[1][:, 0:TT * NE].rearrange("p (t e) -> p t e", t=TT)))
            chained(nc.vector.tensor_copy(counts, bank[1][:, TT * NE:(TT + 1) * NE]))
            chained(nc.vector.reduce_max(over_f, counts, AX))
            nc.vector.tensor_copy(over_i[:, :], over_f).then_inc(routed, 1)

            def pick_rows(dst, e, done):
                for t in range(TT):
                    col = NE * t
                    last = nc.vector.tensor_scalar(dst[:, t, :], slot_no[:, :],
                                                   rt[:, 9, :][:, bass.ds(e + col, 1)],
                                                   rt[:, 8, :][:, bass.ds(e + col, 1)], ALU.is_equal, ALU.mult)
                last.then_inc(done, 1)

            def gathered_lo(q):
                dve.wait_ge(xe_hi, q + 1)
                for i in range(2):
                    last = nc.vector.tensor_tensor(act_lo[:, 4 * i:4 * i + 4, 0:P],
                                                   bank[1 + 2 * i][:, :].rearrange("p (c t) -> p c t", c=4),
                                                   act_hi[:, 4 * i:4 * i + 4, 0:P].bitcast(F32), ALU.subtract)
                last.then_inc(xe_done, 1)

            def expert_out(h, e):
                dve.wait_ge(w_used, h + 1)
                nc.vector.tensor_copy(y_e[:, 512:1024], bank[5][:, :]).then_inc(ye_dve, 1)
                pick_rows(pick2, e, picked2)

            def add_scattered(q, e, t):
                dve.wait_ge(scattered, 2 * q + t + 1)
                dve.wait_ge(y_acc, 2 * q + t + 1)
                for f in range(2):
                    dst = y[:, t, 512 * f:512 * f + 512]
                    last = nc.vector.scalar_tensor_tensor(
                        out=dst, in0=bank[1 + 2 * f][:, :], scalar=rt[:, 7, :][:, bass.ds(e + NE * t, 1)], in1=dst,
                        op0=ALU.mult, op1=ALU.add)
                last.then_inc(y_acc, 1)

            def experts(r):
                c = MOE_H + r * ROUND_H
                n0 = NCH + r * NCH * NE
                q0 = r * NE
                pick_rows(pick, 0, picked)
                gathered_lo(q0)
                first_chunk(c, n0, 1)
                c -= 2

                def rest(e):
                    prev = not isinstance(e, int) or e >= 1
                    q = q0 + e - 1
                    chunk(c + 6, 7 * e, n0 + 7 * e + 1, 1,
                          (lambda: add_scattered(q, e - 1, 0)) if prev else None,
                          (lambda: add_scattered(q, e - 1, 1)) if prev else None)
                    with dve.Fori(2, NCH - 1) as j:
                        chunk(c, 7 * e + j, n0 + 7 * e + j, 1)
                    last = isinstance(e, int) and e == NE - 1
                    chunk(c + 36, 7 * e, n0 + 7 * e + 6, 1,
                          None if last else (lambda: pick_rows(pick, e + 1, picked)),
                          None if last else (lambda: gathered_lo(q0 + e + 1)))

                rest(0)
                with dve.Fori(1, NE - 1) as e:
                    chunk(c, 7 * e, n0 + 7 * e, 1)
                    expert_out(c + 42 * e + 5, e - 1)
                    rest(e)
                chunk(c, 7 * (NE - 1), n0 + 7 * (NE - 1), 1)
                expert_out(c + 42 * (NE - 1) + 5, NE - 2)
                rest(NE - 1)
                hidden_lo(n0 + NE * NCH - 1, 1)
                expert_out(c + ROUND_H + 1, NE - 1)
                for t in range(TT):
                    add_scattered(q0 + NE - 1, NE - 1, t)

            experts(0)
            over = dve.value_load(over_i[0:1, 0:1], min_val=0, max_val=T)
            with dve.If(over > CAP):
                nc.vector.tensor_scalar(pos, pos, -float(CAP), None, ALU.add).then_inc(moved, 1)
                dve.wait_ge(moved, 1)
                for h in range(2):
                    cut(MOE_H + ROUND_H + h)
                experts(1)
            nc.vector.memset(over_f, 0.0).then_inc(y_final, 1)
            norm(8)
            residual(4, y)

        @block.tensor
        def _(pe):
            def three(o, l_hi, l_lo, r_hi, r_lo, start, stop):
                nc.tensor.matmul(o, l_hi, r_hi, start=start, stop=False)
                nc.tensor.matmul(o, l_hi, r_lo, start=False, stop=False)
                return nc.tensor.matmul(o, l_lo, r_hi, start=False, stop=stop)

            def project(s):
                n = TURNS[s]
                if n >= 2:
                    pe.wait_ge(evac_act, n - 1)
                    pe.wait_ge(evac_dve, n - 1)
                jobs = slabs[s][3]
                for i in range(2):
                    h = 2 * s + i
                    ring = h % CUT_SLOTS
                    pe.wait_ge(cut_lo, h + 1)
                    for b, job in enumerate(jobs):
                        for a in range(4):
                            k = 4 * i + a
                            o = bank[4 * (n % 2) + b]
                            if job[0] == "T":
                                c0 = job[1]
                                lh, ll = (m[:, ring, a, c0:c0 + P] for m in (w_hi, w_lo))
                                last = three(o[:, 0:T], lh, ll, act_hi[:, k, :], act_lo[:, k, :], k == 0, k == KC - 1)
                            else:
                                _, c0, w, t, _ = job
                                last = three(o[:, 0:w], act_hi[:, k, t * P:(t + 1) * P], act_lo[:, k, t * P:(t + 1) * P],
                                             w_hi[:, ring, a, c0:c0 + w], w_lo[:, ring, a, c0:c0 + w],
                                             k == 0, k == KC - 1)
                    last.then_inc(w_used, 1)
                return last

            def turn_rows(k):
                pe.wait_ge(normed, k + 1)
                for c in range(KC):
                    for t in range(TT):
                        last = nc.tensor.transpose(bank[4 + c // 2][:, (c % 2) * T + t * P:(c % 2) * T + (t + 1) * P],
                                                   tok[:, t, c * P:(c + 1) * P], ident[:, :])
                    if c % 2 == 1:
                        last.then_inc(turned, 1)

            def scores(g):
                kind, h, c = GROUPS[g]
                if g >= 2:
                    pe.wait_ge(exped, g - 1)
                if kind == "A":
                    kv = h // 3
                    half, q = h % 2, qT[:, h // 2, :]
                    k = kT[:, kv // 2 if kv % 2 == half else 2 + kv // 2, :]
                elif kind == "B":
                    half, q, k = c, qT[:, h, :], kT[:, h, :]
                else:
                    half, q, k = h % 2, qmT[:, h // 2, :], mkT[:, h // 2, :]
                rows = slice(half * HEAD, half * HEAD + HEAD)
                for t in range(TT):
                    last = nc.tensor.matmul(bank[g % 2][:, t * T:(t + 1) * T], q[rows, t * P:(t + 1) * P], k[rows, :],
                                            start=True, stop=True)
                last.then_inc(scored, 1)

            def turn_probs(v):
                g = GROUP_OF[v]
                pe.wait_ge(prob, g + 1)
                if v >= 2:
                    pe.wait_ge(probT, v - 1)
                for kt in range(TT):
                    for t in range(TT):
                        last = nc.tensor.transpose(bank[2 + v % 2][:, kt * T + t * P:kt * T + (t + 1) * P],
                                                   p_buf[:, g % 2, t, kt * P:(kt + 1) * P], ident[:, :])
                last.then_inc(prob_turned, 1)

            def values(v):
                g = GROUP_OF[v]
                kind, h, _ = GROUPS[g]
                u, _ = block_of(g)
                pe.wait_ge(probT, v + 1)
                if u >= 2:
                    pe.wait_ge(blk_done, u - 1)
                for kt in range(TT):
                    if kind == "A":
                        val, rows = vv[:, kt, (h // 3) * HEAD:(h // 3 + 1) * HEAD], slice((h % 2) * HEAD, (h % 2 + 1) * HEAD)
                    elif kind == "B":
                        val, rows = vv[:, kt, h * P:(h + 1) * P], slice(0, P)
                    else:
                        val, rows = mv[:, kt, h * HEAD:(h + 1) * HEAD], slice((h % 2) * HEAD, (h % 2 + 1) * HEAD)
                    last = nc.tensor.matmul(bank[4 + u % 2][rows, 0:T], val, pT[:, v % 2, kt, :],
                                            start=(kt == 0), stop=(kt == TT - 1))
                last.then_inc(pv_done, 1)

            def sum_squares(v):
                g = GROUP_OF[v]
                if GROUPS[g][0] != "B":
                    return
                h = GROUPS[g][1]
                pe.wait_ge(blk_hi, 8 + h + 1)
                nc.tensor.matmul(bank[6 + h % 2][:, 0:T], ones[:, :], sq[:, h % 2, :],
                                 start=True, stop=True).then_inc(sq_summed, 1)

            def attention(phase):
                g0, g1 = PHASES[phase]
                scores(g0)
                scores(g0 + 1)
                v0 = min(v for v, g in GROUP_OF.items() if g >= g0)
                for g in range(g0, g1):
                    if g in ITEM_OF:
                        v = ITEM_OF[g]
                        turn_probs(v)
                        if v - 2 >= v0:
                            sum_squares(v - 2)
                        if v - 1 >= v0:
                            values(v - 1)
                    if g + 2 < g1:
                        scores(g + 2)
                v = ITEM_OF[g1 - 1]
                values(v)
                for w in (v - 1, v):
                    sum_squares(w)

            def gate_or_up(h, c, first_bank, tiles):
                for i in range(2):
                    ring = (c + i) % CUT_SLOTS
                    pe.wait_ge(cut_lo, h + i + 1)
                    for t in range(tiles):
                        for a in range(4):
                            k = 4 * i + a
                            last = three(bank[first_bank + t][:, :], act_hi[:, k, t * P:(t + 1) * P],
                                         act_lo[:, k, t * P:(t + 1) * P], w_hi[:, ring, a, :], w_lo[:, ring, a, :],
                                         k == 0, k == KC - 1)
                    last.then_inc(w_used, 1)
                return last

            def turn_hidden(n, tiles):
                pe.wait_ge(hid_done, n + 1)
                for t in range(tiles):
                    for f in range(FT):
                        last = nc.tensor.transpose(bank[6 + t][:, f * P:(f + 1) * P], hid[:, t, f * P:(f + 1) * P],
                                                   ident[:, :])
                last.then_inc(hid_turned, 1)

            def dense_down(h, c, n):
                pe.wait_ge(at_done, n + 1)
                pe.wait_ge(cut_lo, h + 2)
                for i in range(4):
                    t, f = i // 2, i % 2
                    pe.wait_ge(y_added, 4 * n + max(i, 1))
                    for a in range(FT):
                        ring = (c + a // 2) % CUT_SLOTS
                        col = (a % 2) * D + 512 * f
                        r_hi, r_lo = (m[:, ring, :, :].rearrange("p a n -> p (a n)")[:, col:col + 512]
                                      for m in (w_hi, w_lo))
                        last = three(bank[4 + f][:, :], at_hi[:, a, t * P:(t + 1) * P], at_lo[:, a, t * P:(t + 1) * P],
                                     r_hi, r_lo, a == 0, a == FT - 1)
                        if i == 3 and a % 2 == 1:
                            last.then_inc(w_used, 1)
                    if i < 3:
                        last.then_inc(down_ps, 1)

            def expert_down(h, c, n, first, last_chunk):
                pe.wait_ge(at_done, n + 1)
                for i in range(2):
                    ring = (c + i) % CUT_SLOTS
                    pe.wait_ge(cut_lo, h + i + 1)
                    for a in range(2):
                        for f in range(2):
                            col = a * D + 512 * f
                            r_hi, r_lo = (m[:, ring, :, :].rearrange("p a n -> p (a n)")[:, col:col + 512]
                                          for m in (w_hi, w_lo))
                            last = three(bank[4 + f][:, :], at_hi[:, 2 * i + a, 0:P], at_lo[:, 2 * i + a, 0:P],
                                         r_hi, r_lo, first and i == 0 and a == 0, last_chunk and i == 1 and a == 1)
                    last.then_inc(w_used, 1)
                return last

            pe.wait_ge(consts, 6)
            pe.wait_ge(consts_in, 16 * 9)
            nc.tensor.transpose(bank[0][:, 0:40], g_rows[:, :], ident[0:40, 0:40]).then_inc(g_turned, 1)
            pe.wait_ge(g_turned, 2)
            turn_rows(0)
            pe.wait_ge(act_done, 1)
            project(0)
            turn_rows(1)
            pe.wait_ge(act_done, 2)
            for s in A_PROJ:
                project(s)
            pe.wait_ge(evac_act, TURNS[4] + 1)
            pe.wait_ge(evac_dve, TURNS[4] + 1)
            pe.wait_ge(k_swapped, 32)
            attention(0)
            pe.wait_ge(blk_done, 8)
            for s in A_OUT:
                project(s)
            turn_rows(2)
            pe.wait_ge(act_done, 3)

            gate_or_up(FFN_H, FFN_H, 0, TT)
            gate_or_up(FFN_H + 2, FFN_H + 2, 2, TT)
            with pe.Fori(1, NCH) as j:
                c = FFN_H - 2
                pe.wait_ge(silu_done, j)
                gate_or_up(c + 6 * j, c, 0, TT)
                turn_hidden(j - 1, TT)
                gate_or_up(c + 6 * j + 2, c + 2, 2, TT)
                dense_down(c + 6 * j + 4, c + 4, j - 1)
            turn_hidden(NCH - 1, TT)
            dense_down(FFN_H + 40, FFN_H + 40, NCH - 1)

            turn_rows(3)
            pe.wait_ge(act_done, 4)
            for s in B_PROJ:
                project(s)
            pe.wait_ge(evac_act, TURNS[B_PROJ[-1]] + 1)
            pe.wait_ge(evac_dve, TURNS[B_PROJ[-1]] + 1)
            attention(1)
            pe.wait_ge(blk_done, 16)
            pe.wait_ge(sub_hi, 2)
            for s in B_OUT:
                project(s)
            turn_rows(4)
            pe.wait_ge(act_done, 5)

            for t in range(TT):
                for k in range(KC):
                    for i, (l, r) in enumerate(((act_hi, router_hi), (act_hi, router_lo), (act_lo, router_hi),
                                                (act_lo, router_lo))):
                        last = nc.tensor.matmul(bank[0][:, NE * t:NE * t + NE], l[:, k, t * P:(t + 1) * P], r[:, k, :],
                                                start=(k == 0 and i == 0), stop=(k == KC - 1 and i == 3))
            last.then_inc(logits_ps, 1)
            pe.wait_ge(chosen_done, 1)
            ch = [rt[:, 8, NE * t:NE * t + NE] for t in range(TT)]
            nc.tensor.matmul(bank[1][:, 0:NE], before[:, :], ch[0], start=True, stop=True)
            nc.tensor.matmul(bank[1][:, NE:2 * NE], ones[:, :], ch[0], start=True, stop=False)
            nc.tensor.matmul(bank[1][:, NE:2 * NE], before[:, :], ch[1], start=False, stop=True)
            nc.tensor.matmul(bank[1][:, 2 * NE:3 * NE], ones[:, :], ch[0], start=True, stop=False)
            nc.tensor.matmul(bank[1][:, 2 * NE:3 * NE], ones[:, :], ch[1], start=False, stop=True).then_inc(pos_ps, 1)
            pe.wait_ge(rows_done, 2)

            def gather(q):
                pe.wait_ge(picked, q + 1)
                for k in range(KC):
                    for t in range(TT):
                        last = nc.tensor.matmul(bank[1 + 2 * (k // 4)][:, (k % 4) * P:(k % 4 + 1) * P],
                                                tok[:, t, k * P:(k + 1) * P], pick[:, t, :],
                                                start=(t == 0), stop=(t == TT - 1))
                last.then_inc(gathered, 1)

            def turn_pick(q):
                pe.wait_ge(picked2, q + 1)
                for t in range(TT):
                    last = nc.tensor.transpose(bank[7][:, t * P:(t + 1) * P], pick2[:, t, :], ident[:, :])
                last.then_inc(pick_ps, 1)

            def scatter(q, t):
                if t == 0:
                    pe.wait_ge(pick_T, q + 1)
                    pe.wait_ge(ye_act, q + 1)
                    pe.wait_ge(ye_dve, q + 1)
                else:
                    pe.wait_ge(y_acc, 2 * q + 2)
                for f in range(2):
                    last = nc.tensor.matmul(bank[1 + 2 * f][:, :], pickT[:, t, :], y_e[:, 512 * f:512 * f + 512],
                                            start=True, stop=True)
                last.then_inc(scattered, 1)

            def experts(r):
                c = MOE_H + r * ROUND_H
                n0 = NCH + r * NCH * NE
                q0 = r * NE
                if r >= 1:
                    pe.wait_ge(y_acc, 2 * q0 + 1)
                gather(q0)
                pe.wait_ge(xe_done, q0 + 1)
                pe.wait_ge(silu_done, n0)
                gate_or_up(c, c, 0, 1)
                gate_or_up(c + 2, c + 2, 2, 1)
                c -= 2

                def chunk(h, n, first=False, last=False, mid=None, late=None):
                    pe.wait_ge(silu_done, n)
                    gate_or_up(h, c, 0, 1)
                    turn_hidden(n - 1, 1)
                    if mid:
                        mid()
                    gate_or_up(h + 2, c + 2, 2, 1)
                    if late:
                        late()
                    expert_down(h + 4, c + 4, n - 1, first, last)

                def rest(e):
                    prev = not isinstance(e, int) or e >= 1
                    q = q0 + e - 1
                    if prev:
                        turn_pick(q)
                    chunk(c + 42 * e + 6, n0 + 7 * e + 1, True, False,
                          (lambda: scatter(q, 0)) if prev else None,
                          (lambda: scatter(q, 1)) if prev else None)
                    with pe.Fori(2, NCH - 1) as j:
                        chunk(c + 42 * e + 6 * j, n0 + 7 * e + j)
                    last = isinstance(e, int) and e == NE - 1

                    def next_rows():
                        if prev:
                            pe.wait_ge(y_acc, 2 * q + 3)
                        gather(q0 + e + 1)

                    chunk(c + 42 * e + 36, n0 + 7 * e + 6, late=None if last else next_rows)

                rest(0)
                with pe.Fori(1, NE - 1) as e:
                    pe.wait_ge(xe_done, q0 + e + 1)
                    chunk(c + 42 * e, n0 + 7 * e, last=True)
                    rest(e)
                e = NE - 1
                pe.wait_ge(xe_done, q0 + e + 1)
                chunk(c + 42 * e, n0 + 7 * e, last=True)
                rest(e)
                turn_hidden(n0 + NE * NCH - 1, 1)
                expert_down(c + ROUND_H, c + ROUND_H, n0 + NE * NCH - 1, False, True)
                turn_pick(q0 + NE - 1)
                for t in range(TT):
                    scatter(q0 + NE - 1, t)

            experts(0)
            pe.wait_ge(routed, 1)
            over = pe.value_load(over_i[0:1, 0:1], min_val=0, max_val=T)
            with pe.If(over > CAP):
                experts(1)


_INS = ['x', 'mem', 'norm_g', 'mem_norm_g', 'w_mem_kv', 'a_w_in', 'a_sink', 'a_w_out', 'b_w_in', 'b_lambda',
        'b_subln_g', 'b_w_out', 'ffn_w_gate', 'ffn_w_up', 'ffn_w_down', 'moe_w_router', 'moe_w_gate', 'moe_w_up',
        'moe_w_down']
_OUTS = [((1, T, D), 'float32')]


def kernel(**inputs):
    import numpy as _np
    import concourse.bacc as _bacc
    from concourse import mybir as _mybir
    from concourse.bass_utils import run_bass_kernel_spmd as _run

    nc = _bacc.Bacc("TRN2", target_bir_lowering=False, num_devices=1)
    arrays, args = {}, []
    for name in _INS:
        a = _np.ascontiguousarray(inputs[name])
        arrays[f"in_{name}_dram"] = a
        args.append(nc.dram_tensor(f"in_{name}_dram", a.shape, _mybir.dt.from_np(a.dtype), kind="ExternalInput").ap())
    for i, (shape, dtype) in enumerate(_OUTS):
        dt = _mybir.dt.from_np(_np.dtype(dtype))
        args.append(nc.dram_tensor(f"out_{i}_dram", shape, dt, kind="ExternalOutput").ap())
    build_encoder(nc, *args)
    r = _run(nc, [arrays], core_ids=[0])
    return r.results[0]["out_0_dram"]
```

```python
import math
from contextlib import ExitStack

import concourse.bass as bass
from concourse import mybir

F32 = mybir.dt.float32
F32R = mybir.dt.float32r
I32 = mybir.dt.int32
ACT = mybir.ActivationFunctionType
ALU = mybir.AluOpType
AX = mybir.AxisListType.X

P = 128
D = 1024
T = 256
TT = T // P
KC = D // P
HEAD = 64
MIX = 768
MEMW = 256
A_HEADS, A_KV = 12, 4
B_HEADS = 6
M_HEADS = 4
WINDOW = 128
DFF = 3584
FCH = 512
NCH = DFF // FCH
FT = FCH // P
NE = 8
EPS = 1e-6
CAP = P
ROUNDS = T // CAP
LAMBDA_INIT = 0.8 - 0.6 * math.exp(-0.3)
FAR = 1e32
SCALE = HEAD ** -0.5

RAW_SLOTS = 6
CUT_SLOTS = 3

FFN_H = 14
B_SLAB = 7 + 3 * NCH
MOE_H = 2 * (B_SLAB + 7)
ROUND_H = 6 * NCH * NE


def slopes(n):
    return [2.0 ** (-8.0 * (i + 1) / n) for i in range(n)]


GROUPS = ([("A", h, 0) for h in range(A_HEADS)] + [("M", h, 0) for h in range(M_HEADS)]
          + [("B", h, c) for h in range(B_HEADS) for c in range(2)] + [("M", h, 0) for h in range(M_HEADS)])
PHASES = [(0, A_HEADS + M_HEADS), (A_HEADS + M_HEADS, len(GROUPS))]
ITEM_OF = {}
for _g, (_k, _h, _c) in enumerate(GROUPS):
    if _k != "B" or _c == 1:
        ITEM_OF[_g] = len(ITEM_OF)
GROUP_OF = {v: g for g, v in ITEM_OF.items()}


def block_of(g):
    kind, h, _ = GROUPS[g]
    layer = 0 if g < PHASES[0][1] else 1
    if kind == "B":
        return 8 + h, True
    c = h // 2 if kind == "A" else 6 + h // 2
    return 8 * layer + c, h % 2 == 1


def build_encoder(nc, x, mem, norm_g, mem_norm_g, w_mem_kv, a_w_in, a_sink, a_w_out, b_w_in, b_lambda,
                  b_subln_g, b_w_out, ffn_gate, ffn_up, ffn_down, router, moe_gate, moe_up, moe_down, out):
    ctx = ExitStack()
    with ctx:
        def sb(name, shape, dt=F32):
            return ctx.enter_context(nc.sbuf_tensor(name, shape, dt))

        def sem(name):
            return ctx.enter_context(nc.semaphore(name))

        raw = sb("raw", [P, RAW_SLOTS, 4, 512])
        w_hi = sb("w_hi", [P, CUT_SLOTS, 4, 512], F32R)
        w_lo = sb("w_lo", [P, CUT_SLOTS, 4, 512], F32R)
        x_sb = sb("x_sb", [P, TT, D])
        tok = sb("tok", [P, TT, D])
        act_hi = sb("act_hi", [P, KC, T], F32R)
        act_lo = sb("act_lo", [P, KC, T], F32R)
        at_hi = sb("at_hi", [P, FT, T], F32R)
        at_lo = sb("at_lo", [P, FT, T], F32R)
        g_row = sb("g_row", [P, 2, D])
        mkT = sb("mkT", [P, 2, T])
        mv = sb("mv", [P, TT, MEMW])
        dist_w = sb("dist_w", [P, TT, T])
        dist = sb("dist", [P, TT, T])
        ident = sb("ident", [P, P])
        ones = sb("ones", [P, P])
        before = sb("before", [P, P])
        slot_no = sb("slot_no", [P, P])
        ARENA = 12032
        arena = sb("arena", [P, ARENA])
        g_rows = sb("g_rows", [40, P])
        g_col = sb("g_col", [P, 40])
        router_sb = sb("router_sb", [P, KC, NE])
        router2 = sb("router2", [P, KC, 2 * NE], F32R)
        cell = sb("cell", [P, 2])
        sink = sb("sink", [P, A_HEADS])
        sink8 = sb("sink8", [P, A_HEADS])
        sub_g = sb("sub_g", [P, 1])
        small = sb("small", [P, 96])
        rt = sb("rt", [P, 16, TT * NE])
        logitT = sb("logitT", [2 * NE, T])
        one_col = sb("one_col", [P, 12])
        over_i = sb("over_i", [P, 1], I32)

        class Carve:
            def __init__(self):
                self.at = 0

            def __call__(self, *shape):
                n = math.prod(shape)
                v = arena[:, self.at:self.at + n]
                self.at += n
                assert self.at <= ARENA
                if len(shape) == 2:
                    v = v.rearrange("p (a b) -> p a b", a=shape[0])
                elif len(shape) == 3:
                    v = v.rearrange("p (a b c) -> p a b c", a=shape[0], b=shape[1])
                return v

        carve = Carve()
        qT = carve(6, T)
        kT = carve(6, T)
        vv = carve(TT, MIX)
        qmT = carve(2, T)
        s_buf = carve(2, TT, T)
        p_buf = carve(2, TT, T)
        pT = carve(2, TT, T)
        o_raw = carve(6, T)
        sub_r = carve(6, T)[0:B_HEADS, 0, :]
        sq = carve(2, T)
        lam_in = carve(4, HEAD)
        junk = arena[:, 8192:8192 + TT * D].rearrange("p (t d) -> p t d", t=TT)
        mem_sb = arena[:, 6 * T:6 * T + TT * D].rearrange("p (t d) -> p t d", t=TT)
        carve = Carve()
        hid = carve(TT, FCH)
        sil = carve(TT, FCH)
        y = carve(TT, D)
        y_e = carve(D)
        pick = carve(TT, P)
        pick2 = carve(TT, P)
        pickT = carve(TT, P)

        ss = small[:, 0:2]
        ss4 = small[:, 44:48].rearrange("p (a b) -> p a b", a=2)
        ms = small[:, 2:4]
        root = small[:, 4:6]
        rstd = small[:, 6:8]
        mx = small[:, 8:12].rearrange("p (a b) -> p a b", a=2)
        neg = small[:, 12:16].rearrange("p (a b) -> p a b", a=2)
        den = small[:, 16:20].rearrange("p (a b) -> p a b", a=2)
        e_sink = small[:, 20:24].rearrange("p (a b) -> p a b", a=2)
        inv = small[:, 24:28].rearrange("p (a b) -> p a b", a=2)
        tot = small[:, 28:32].rearrange("p (a b) -> p a b", a=2)
        lam_s = small[:, 32:34]
        lam_e = small[:, 34:36]
        neg_lam = small[:, 36:37]
        sub_gs = small[:, 37:38]
        inv_l = small[:, 38:42].rearrange("p (a b) -> p a b", a=2)
        over_f = small[:, 42:43]
        lg = [rt[:, i, :].rearrange("p (t e) -> p t e", t=TT) for i in range(16)]
        (logit, rev, eq1, mask1, logit2, eq2, mask2, gates, chosen, pos, r_tmp, r_tmp2) = lg[:12]
        m1, m2, r1, r2, m_d, m_e, g1, g2 = (rt[:, 12 + i // 4, (i % 4) * 4:(i % 4) * 4 + TT] for i in range(8))
        m_den = rt[:, 14, 0:TT]
        counts = rt[:, 15, 0:NE]

        bank = [ctx.enter_context(nc.psum_tensor(f"bank{i}", [P, 512], F32)) for i in range(8)]

        landed = [sem(f"landed{i}") for i in range(RAW_SLOTS)]
        cut_hi = sem("cut_hi")
        cut_lo = sem("cut_lo")
        w_used = sem("w_used")
        x_in, mem_in, gains_in, consts_in = sem("x_in"), sem("mem_in"), sem("gains_in"), sem("consts_in")
        cell_set = sem("cell_set")
        g_in = [sem("g_in0"), sem("g_in1")]
        pool_step, consts = sem("pool_step"), sem("consts")
        dve_step = sem("dve_step")
        act_step = sem("act_step")
        g_turned = sem("g_turned")
        squares, mean_sq, rooted = sem("squares"), sem("mean_sq"), sem("rooted")
        normed, turned, act_hi_done, act_done = sem("normed"), sem("turned"), sem("act_hi_done"), sem("act_done")
        evac_act, evac_dve = sem("evac_act"), sem("evac_dve")
        res_done = sem("res_done")
        k_swapped = sem("k_swapped")
        scored, neg_max, exped, prob = sem("scored"), sem("neg_max"), sem("exped"), sem("prob")
        prob_turned, probT, pv_done = sem("prob_turned"), sem("probT"), sem("pv_done")
        blk_hi, blk_done, sq_summed = sem("blk_hi"), sem("blk_done"), sem("sq_summed")
        sub_ms, sub_root, sub_spread = sem("sub_ms"), sem("sub_root"), sem("sub_spread")
        sub_y, sub_hi, sub_lo = sem("sub_y"), sem("sub_hi"), sem("sub_lo")
        out_sq = sem("out_sq")
        lam_red, lam_exp = sem("lam_red"), sem("lam_exp")
        silu_done, hid_done = sem("silu_done"), sem("hid_done")
        hid_turned, at_hi_done, at_done = sem("hid_turned"), sem("at_hi_done"), sem("at_done")
        down_ps, y_added = sem("down_ps"), sem("y_added")
        logits_sb = sem("logits_sb")
        logits_ps, gap, gap_exp, chosen_done = sem("logits_ps"), sem("gap"), sem("gap_exp"), sem("chosen_done")
        pos_ps, routed = sem("pos_ps"), sem("routed")
        picked, gathered, xe_hi, xe_done = sem("picked"), sem("gathered"), sem("xe_hi"), sem("xe_done")
        ye_act, ye_dve = sem("ye_act"), sem("ye_dve")
        picked2, pick_ps, pick_T = sem("picked2"), sem("pick_ps"), sem("pick_T")
        scattered, y_acc = sem("scattered"), sem("y_acc")
        rows_done, moved, y_final = sem("rows_done"), sem("moved"), sem("y_final")
        stored = sem("stored")

        MEM_N, A_N, FFN_N, B_N, MOE_N = range(5)
        row_gains = [norm_g[0, 1], norm_g[0, 3], norm_g[1, 1], norm_g[1, 2], norm_g[1, 3]]

        def t_job(c0, dst):
            return ("T", c0, dst)

        def r_jobs(c0, w, dst):
            return [("R", c0, w, t, dst(t)) for t in range(TT)]

        slabs = {}
        slabs[0] = (w_mem_kv, 0, 512, [t_job(i * P, mkT[:, i, :]) for i in range(2)]
                    + r_jobs(256, 256, lambda t: mv[:, t, :]))
        slabs[1] = (a_w_in[0], MIX, 512, [t_job(i * P, kT[:, i, :]) for i in range(2)]
                    + r_jobs(256, 256, lambda t: vv[:, t, 0:256]))
        for s in range(2):
            slabs[2 + s] = (a_w_in[0], 384 * s, 384, [t_job(i * P, qT[:, 3 * s + i, :]) for i in range(3)])
        slabs[4] = (a_w_in[0], MIX + 512, 256, [t_job(i * P, qmT[:, i, :]) for i in range(2)])
        for s in range(2):
            slabs[5 + s] = (a_w_out[0], 512 * s, 512, r_jobs(0, 512, lambda t, s=s: tok[:, t, 512 * s:512 * s + 512]))
            slabs[B_SLAB + 5 + s] = (b_w_out[0], 512 * s, 512,
                                     r_jobs(0, 512, lambda t, s=s: tok[:, t, 512 * s:512 * s + 512]))
        for s in range(3):
            blocks = [4 * s + i for i in range(4)]
            slabs[B_SLAB + s] = (b_w_in[0], 512 * s, 512,
                                 [t_job(i * P, (qT[:, b, :] if b < 6 else kT[:, b - 6, :]))
                                  for i, b in enumerate(blocks)])
        slabs[B_SLAB + 3] = (b_w_in[0], 2 * MIX, 512, r_jobs(0, 512, lambda t: vv[:, t, 0:512]))
        slabs[B_SLAB + 4] = (b_w_in[0], 2 * MIX + 512, 512, r_jobs(0, 256, lambda t: vv[:, t, 512:768])
                             + [t_job(256 + i * P, qmT[:, i, :]) for i in range(2)])
        TURNS = {s: n for n, s in enumerate(sorted(slabs))}
        A_PROJ, A_OUT = [1, 2, 3, 4], [5, 6]
        B_PROJ, B_OUT = list(range(B_SLAB, B_SLAB + 5)), [B_SLAB + 5, B_SLAB + 6]

        def score_bank(g):
            return bank[(0, 1, 7)[g % 3]]

        block = ctx.enter_context(nc.Block())

        @block.sync
        def _(sp):
            def load(h, c, src, view=None):
                slot = c % RAW_SLOTS
                if not isinstance(h, int) or h >= RAW_SLOTS:
                    sp.wait_ge(cut_lo, h - (RAW_SLOTS - 1))
                dst = raw[:, slot, :, :]
                if view is None:
                    dst = dst.rearrange("p a n -> p (a n)").rearrange("p (q n) -> p q n", q=2)
                else:
                    dst = dst[:, :, 0:view]
                sp.dma_start(dst, src).then_inc(landed[slot], 16)

            def load_cols(h, c, w, c0, width):
                v = w.rearrange("(k p) f -> p k f", p=P)
                for i in range(2):
                    load(h + i, c + i, v[:, 4 * i:4 * i + 4, c0:c0 + width], width)

            def load_chunk(h, c, w, j):
                v = w.rearrange("(k p) (j f) -> j p k f", p=P, f=FCH)[j]
                for i in range(2):
                    load(h + i, c + i, v[:, 4 * i:4 * i + 4, :], FCH)

            def load_down(h, c, w, j):
                v = w.rearrange("(j q p) n -> j p q n", q=FT, p=P)[j]
                for i in range(2):
                    load(h + i, c + i, v[:, 2 * i:2 * i + 2, :])

            def load_slab(s):
                w, c0, width, _ = slabs[s]
                load_cols(2 * s, 2 * s, w, c0, width)

            sp.dma_start(g_rows[0:8, :], mem_norm_g.rearrange("(c p) -> c p", p=P)).then_inc(gains_in, 16)
            for i in range(2):
                sp.dma_start(g_rows[8 + 16 * i:24 + 16 * i, :],
                             norm_g[i, 0:4:2, :].rearrange("a (c p) -> a c p", p=P)).then_inc(gains_in, 16)
            sp.dma_start(mem_sb, mem[0].rearrange("(t p) d -> p t d", p=P)).then_inc(mem_in, 16)
            load_slab(0)
            sp.dma_start(x_sb[:, :, :], x[0].rearrange("(t p) d -> p t d", p=P)).then_inc(x_in, 16)
            for s in range(1, 7):
                load_slab(s)
            load_chunk(FFN_H, FFN_H, ffn_gate[0], 0)
            load_chunk(FFN_H + 2, FFN_H + 2, ffn_up[0], 0)
            with sp.Fori(1, NCH) as j:
                c = FFN_H - 2
                load_chunk(c + 6 * j, c, ffn_gate[0], j)
                load_chunk(c + 6 * j + 2, c + 2, ffn_up[0], j)
                load_down(c + 6 * j + 4, c + 4, ffn_down[0], j - 1)
            load_down(FFN_H + 40, FFN_H + 40, ffn_down[0], NCH - 1)
            for s in B_PROJ + B_OUT:
                load_slab(s)

            def load_experts(base):
                c = MOE_H + base
                load_chunk(c, c, moe_gate[0, 0], 0)
                load_chunk(c + 2, c + 2, moe_up[0, 0], 0)
                c -= 2

                def chunk(h, e, j, e_down, j_down):
                    load_chunk(h, c, moe_gate[0, e], j)
                    load_chunk(h + 2, c + 2, moe_up[0, e], j)
                    load_down(h + 4, c + 4, moe_down[0, e_down], j_down)

                with sp.Fori(1, NCH) as j:
                    chunk(c + 6 * j, 0, j, 0, j - 1)
                with sp.Fori(1, NE) as e:
                    chunk(c + 42 * e, e, 0, e - 1, NCH - 1)
                    with sp.Fori(1, NCH) as j:
                        chunk(c + 42 * e + 6 * j, e, j, e, j - 1)
                load_down(c + ROUND_H, c + ROUND_H, moe_down[0, NE - 1], NCH - 1)

            load_experts(0)
            sp.wait_ge(routed, 1)
            over = sp.value_load(over_i[0:1, 0:1], min_val=0, max_val=T)
            with sp.If(over > CAP):
                load_experts(ROUND_H)
            for t in range(TT):
                sp.wait_ge(res_done, 7 + t)
                sp.dma_start(out[0, t * P:(t + 1) * P, :], x_sb[:, t, :]).then_inc(stored, 16)
            sp.wait_ge(stored, 16 * TT)

        @block.gpsimd
        def _(pool):
            pool.dma_start(lam_in[:, :, :], b_lambda[0].unsqueeze(0).broadcast_to([P, 4, HEAD])).then_inc(consts_in, 16)
            pool.dma_start(sink[:, :], a_sink.broadcast_to([P, A_HEADS])).then_inc(consts_in, 16)
            pool.dma_start(sub_g[:, :], b_subln_g.rearrange("a p -> p a")).then_inc(consts_in, 16)
            pool.dma_start(router_sb[:, :, :], router[0].rearrange("(k p) e -> p k e", p=P)).then_inc(consts_in, 16)
            nc.gpsimd.memset(ident[:, :], 0.0).then_inc(pool_step, 1)
            nc.gpsimd.memset(ones[:, :], 1.0).then_inc(pool_step, 1)
            nc.gpsimd.iota(slot_no[:, :], [[1, P]], base=0, channel_multiplier=0,
                           allow_small_or_imprecise_dtypes=True).then_inc(consts, 1)
            for t in range(TT):
                nc.gpsimd.iota(rev[:, t, :], [[-1, NE]], base=NE, channel_multiplier=0,
                               allow_small_or_imprecise_dtypes=True).then_inc(consts, 1)
            nc.gpsimd.iota(dist_w[:, :, :], [[P, TT], [-1, T]], base=0, channel_multiplier=1,
                           allow_small_or_imprecise_dtypes=True).then_inc(consts, 1)
            pool.wait_ge(pool_step, 2)
            nc.gpsimd.affine_select(out=ident[:, :], in_=ident[:, :], compare_op=ALU.not_equal, fill=1.0,
                                    base=0, pattern=[[-1, P]], channel_multiplier=1).then_inc(consts, 1)
            nc.gpsimd.affine_select(out=before[:, :], in_=ones[:, :], compare_op=ALU.is_gt, fill=0.0,
                                    base=0, pattern=[[1, P]], channel_multiplier=-1).then_inc(consts, 1)
            pool.wait_ge(evac_act, TURNS[1] + 1)
            pool.wait_ge(evac_dve, TURNS[1] + 1)
            for i in range(2):
                pool.dma_start(kT[HEAD * i:HEAD * i + HEAD, 2:4, :],
                               kT[HEAD * (1 - i):HEAD * (1 - i) + HEAD, 0:2, :]).then_inc(k_swapped, 16)
            def load_gain(r):
                if r >= 2:
                    pool.wait_ge(res_done, 2 * (r - 1))
                pool.dma_start(g_row[:, r % 2, :], row_gains[r].unsqueeze(0).broadcast_to([P, D])).then_inc(g_in[r % 2], 16)

            load_gain(0)
            load_gain(1)
            pool.wait_ge(blk_done, 8)
            nc.gpsimd.memset(y[:, :, :], 0.0).then_inc(y_added, 1)
            for r in range(2, 5):
                load_gain(r)
            nc.gpsimd.memset(y[:, :, :], 0.0).then_inc(y_acc, 1)
            pool.wait_ge(g_in[1], 32)
            pool.wait_ge(normed, 5)
            pool.wait_ge(turned, 20)
            for t in range(TT):
                nc.gpsimd.tensor_tensor(tok[:, t, :], tok[:, t, :], g_row[:, 1, :], ALU.mult).then_inc(rows_done, 1)

        @block.scalar
        def _(act):
            def cut(h, width=512):
                slot, ring = h % RAW_SLOTS, h % CUT_SLOTS
                act.wait_ge(landed[slot], 16 * (h // RAW_SLOTS + 1))
                if h >= CUT_SLOTS:
                    act.wait_ge(w_used, h - (CUT_SLOTS - 1))
                nc.scalar.activation(w_hi[:, ring, :, 0:width], raw[:, slot, :, 0:width],
                                     ACT.Copy).then_inc(cut_hi, 1)

            def cut_at(c, turns, width=512):
                slot, ring = c % RAW_SLOTS, c % CUT_SLOTS
                act.wait_ge(landed[slot], 16 * (c // RAW_SLOTS + 1) + 16 * turns)
                act.wait_ge(w_used, c - (CUT_SLOTS - 1) + 6 * turns)
                nc.scalar.activation(w_hi[:, ring, :, 0:width], raw[:, slot, :, 0:width],
                                     ACT.Copy).then_inc(cut_hi, 1)

            def load_table(func):
                nc.scalar.activation(cell[:, 1:2], cell[:, 0:1], func)

            def width_of(h):
                return slabs[h // 2][2] if h // 2 in slabs else 512

            def cut_next(s):
                for h in (2 * s + 2, 2 * s + 3):
                    cut(h, width_of(h))

            def evacuate(s):
                n = TURNS[s]
                jobs = slabs[s][3]
                act.wait_ge(w_used, 2 * s + 2)
                for i in range(0, len(jobs), 2):
                    dst = jobs[i][-1]
                    w = jobs[i][2] if jobs[i][0] == "R" else T
                    last = nc.scalar.activation(dst, bank[4 * (n % 2) + i][:, 0:w], ACT.Copy)
                last.then_inc(evac_act, 1)

            def norm(k, src, tiles_done=None):
                for t in range(TT):
                    if tiles_done:
                        act.wait_ge(tiles_done[0], tiles_done[1] + t)
                    last = nc.scalar.activation(junk[:, t, :], src[:, t, :], ACT.Square, accum_out=ss[:, t:t + 1])
                last.then_inc(squares, 1)
                root_of(k)

            def out_squares(s, i):
                b = 4 * (TURNS[s] % 2)
                act.wait_ge(w_used, 2 * s + 2)
                nc.scalar.activation(junk[:, 0, 512 * i:512 * i + 512], bank[b][:, :], ACT.Square,
                                     accum_out=ss4[:, i, 0:1]).then_inc(evac_act, 1)
                act.wait_ge(evac_dve, TURNS[s] + 1)
                nc.scalar.activation(junk[:, 1, 512 * i:512 * i + 512], bank[b + 1][:, :], ACT.Square,
                                     accum_out=ss4[:, i, 1:2]).then_inc(out_sq, 1)

            def root_of(k):
                act.wait_ge(mean_sq, k + 1)
                nc.scalar.activation(root, ms, ACT.Sqrt).then_inc(rooted, 1)

            def turn_rows(k, g, pair_count=4):
                for c in range(KC):
                    if c % 2 == 0:
                        act.wait_ge(turned, 4 * k + c // 2 + 1)
                    last = nc.scalar.activation(act_hi[:, c, :], bank[4 + c // 2][:, (c % 2) * T:(c % 2 + 1) * T],
                                                ACT.Copy, scale=g_col[:, 8 * g + c:8 * g + c + 1])
                    last.then_inc(act_hi_done, 1)

            def exps(g):
                kind, h, _ = GROUPS[g]
                b = g % 2
                act.wait_ge(neg_max, g + 1)
                if g >= 2:
                    if g - 2 in ITEM_OF:
                        act.wait_ge(prob_turned, ITEM_OF[g - 2] + 1)
                    else:
                        act.wait_ge(prob, g)
                for t in range(TT):
                    src = score_bank(g)[:, t * T:(t + 1) * T] if kind == "M" else s_buf[:, b, t, :]
                    last = nc.scalar.activation(p_buf[:, b, t, :], src, ACT.Exp, bias=neg[:, b, t:t + 1],
                                                scale=SCALE, accum_out=den[:, b, t:t + 1])
                if kind == "A":
                    last = nc.scalar.activation(e_sink[:, b, :], neg[:, b, :], ACT.Exp, bias=sink[:, h:h + 1])
                last.then_inc(exped, 1)

            def copy_probT(v):
                act.wait_ge(prob_turned, v + 1)
                if v >= 2:
                    act.wait_ge(pv_done, v - 1)
                nc.scalar.activation(pT[:, v % 2, :, :].rearrange("p a b -> p (a b)"), bank[2 + v % 2][:, :],
                                     ACT.Copy).then_inc(probT, 1)

            def finish_block(v):
                u, complete = block_of(GROUP_OF[v])
                if not complete:
                    return
                act.wait_ge(pv_done, v + 1)
                src = bank[4 + u % 2][:, 0:T]
                if GROUPS[GROUP_OF[v]][0] == "B":
                    h = u - 8
                    if h >= 2:
                        act.wait_ge(sq_summed, h - 1)
                    nc.scalar.activation(o_raw[:, h, :], src, ACT.Copy)
                    nc.scalar.activation(sq[:, h % 2, :], src, ACT.Square).then_inc(blk_hi, 1)
                else:
                    nc.scalar.activation(act_hi[:, u % 8, :], src, ACT.Copy).then_inc(blk_hi, 1)

            def attention(phase):
                g0, g1 = PHASES[phase]
                exps(g0)
                for g in range(g0, g1):
                    if g + 1 < g1:
                        exps(g + 1)
                    if g in ITEM_OF:
                        v = ITEM_OF[g]
                        copy_probT(v)
                        if v - 1 >= 0 and GROUP_OF[v - 1] >= g0:
                            finish_block(v - 1)
                finish_block(ITEM_OF[g1 - 1])

            def first_chunk(c, n, tiles):
                cut(c + 2)
                cut(c + 3)
                silu(n, tiles, c)
                cut(c + 4)
                cut(c + 5)

            def silu(n, tiles, h):
                act.wait_ge(w_used, h + 2)
                if not isinstance(n, int) or n >= 1:
                    act.wait_ge(hid_done, n)
                for t in range(tiles):
                    last = nc.scalar.activation(sil[:, t, :], bank[t][:, :], ACT.Silu)
                last.then_inc(silu_done, 1)

            def hidden_hi(n, tiles):
                act.wait_ge(hid_turned, n + 1)
                for t in range(tiles):
                    last = nc.scalar.activation(at_hi[:, :, t * P:(t + 1) * P],
                                                bank[6 + t][:, :].rearrange("p (f t) -> p f t", f=FT), ACT.Copy)
                last.then_inc(at_hi_done, 1)

            def chunk(c, turns, n, tiles, extra=None):
                cut_at(c + 2, turns)
                cut_at(c + 3, turns)
                silu(n, tiles, c + 6 * turns)
                hidden_hi(n - 1, tiles)
                cut_at(c + 4, turns)
                cut_at(c + 5, turns)
                if extra:
                    extra()
                cut_at(c + 6, turns)
                cut_at(c + 7, turns)

            act.wait_ge(cell_set, 1)
            load_table(ACT.Sqrt)
            act.wait_ge(mem_in, 16)
            norm(0, mem_sb)
            cut(0, width_of(0))
            act.wait_ge(g_turned, 2)
            turn_rows(0, MEM_N)
            cut(1, width_of(1))
            act.wait_ge(x_in, 16)
            norm(1, x_sb)
            cut_next(0)
            evacuate(0)
            turn_rows(1, A_N)
            act.wait_ge(consts_in, 16 * 4)
            nc.scalar.activation(router2[:, :, 0:NE], router_sb[:, :, :], ACT.Copy).then_inc(act_step, 1)
            for s in A_PROJ:
                cut_next(s)
                evacuate(s)
            act.wait_ge(lam_red, 1)
            nc.scalar.activation(lam_e, lam_s, ACT.Exp).then_inc(lam_exp, 1)
            attention(0)
            load_table(ACT.Sqrt)
            for i, s in enumerate(A_OUT):
                cut_next(s)
                out_squares(s, i)
            root_of(2)
            norm(3, x_sb, (res_done, 1))
            load_table(ACT.Silu)
            turn_rows(2, FFN_N)

            first_chunk(FFN_H, 0, TT)
            with act.Fori(1, NCH) as j:
                chunk(FFN_H - 2, j, j, TT)
            hidden_hi(NCH - 1, TT)
            cut(FFN_H + 42)
            cut(FFN_H + 43)
            load_table(ACT.Sqrt)
            act.wait_ge(y_added, 4 * NCH + 1)
            norm(4, y)
            norm(5, x_sb, (res_done, 3))
            load_table(ACT.Exp)
            turn_rows(3, B_N)
            for s in B_PROJ:
                cut_next(s)
                evacuate(s)
            attention(1)
            load_table(ACT.Sqrt)
            act.wait_ge(sub_ms, 1)
            nc.scalar.activation(sub_r[:, :], sub_r[:, :], ACT.Sqrt).then_inc(sub_root, 1)
            for i in range(B_HEADS // 2):
                act.wait_ge(sub_y, i + 1)
                nc.scalar.activation(act_hi[:, 2 * i:2 * i + 2, :], o_raw[:, 2 * i:2 * i + 2, :], ACT.Copy,
                                     scale=sub_gs).then_inc(sub_hi, 1)
            for i, s in enumerate(B_OUT):
                cut_next(s)
                out_squares(s, i)
            root_of(6)
            norm(7, x_sb, (res_done, 5))
            load_table(ACT.Exp)
            turn_rows(4, MOE_N)
            act.wait_ge(gap, 1)
            nc.scalar.activation(m_e, m_d, ACT.Exp).then_inc(gap_exp, 1)
            load_table(ACT.Silu)

            def gathered_hi(q):
                act.wait_ge(gathered, q + 1)
                for i in range(2):
                    last = nc.scalar.activation(act_hi[:, 4 * i:4 * i + 4, 0:P],
                                                bank[1 + 2 * i][:, :].rearrange("p (c t) -> p c t", c=4), ACT.Copy)
                last.then_inc(xe_hi, 1)

            def expert_out(h):
                act.wait_ge(w_used, h + 1)
                nc.scalar.activation(y_e[:, 0:512], bank[4][:, :], ACT.Copy).then_inc(ye_act, 1)

            def copy_pickT(q):
                act.wait_ge(pick_ps, q + 1)
                nc.scalar.activation(pickT[:, :, :].rearrange("p a b -> p (a b)"), bank[7][:, 0:T],
                                     ACT.Copy).then_inc(pick_T, 1)

            def experts(r):
                c = MOE_H + r * ROUND_H
                n0 = NCH + r * NCH * NE
                q0 = r * NE
                gathered_hi(q0)
                first_chunk(c, n0, 1)
                c -= 2

                def rest(e):
                    if not isinstance(e, int) or e >= 1:
                        copy_pickT(q0 + e - 1)
                    chunk(c + 6, 7 * e, n0 + 7 * e + 1, 1)
                    with act.Fori(2, NCH - 1) as j:
                        chunk(c, 7 * e + j, n0 + 7 * e + j, 1)
                    last = isinstance(e, int) and e == NE - 1
                    chunk(c + 36, 7 * e, n0 + 7 * e + 6, 1,
                          None if last else (lambda: gathered_hi(q0 + e + 1)))

                rest(0)
                with act.Fori(1, NE - 1) as e:
                    chunk(c, 7 * e, n0 + 7 * e, 1)
                    expert_out(c + 42 * e + 5)
                    rest(e)
                chunk(c, 7 * (NE - 1), n0 + 7 * (NE - 1), 1)
                expert_out(c + 42 * (NE - 1) + 5)
                rest(NE - 1)
                hidden_hi(n0 + NE * NCH - 1, 1)
                expert_out(c + ROUND_H + 1)
                copy_pickT(q0 + NE - 1)

            experts(0)
            act.wait_ge(routed, 1)
            over = act.value_load(over_i[0:1, 0:1], min_val=0, max_val=T)
            with act.If(over > CAP):
                for h in range(2):
                    cut(MOE_H + ROUND_H + h)
                experts(1)
            load_table(ACT.Sqrt)
            act.wait_ge(y_final, 1)
            norm(8, y)

        @block.vector
        def _(dve):
            steps = [0]
            squares_seen = [0]

            def chained(ins):
                steps[0] += 1
                ins.then_inc(dve_step, 1)
                dve.wait_ge(dve_step, steps[0])

            def cut(c, turns=0, width=512):
                slot, ring = c % RAW_SLOTS, c % CUT_SLOTS
                dve.wait_ge(cut_hi, c + 1 + 6 * turns)
                nc.vector.tensor_tensor(w_lo[:, ring, :, 0:width], raw[:, slot, :, 0:width],
                                        w_hi[:, ring, :, 0:width].bitcast(F32), ALU.subtract).then_inc(cut_lo, 1)

            def width_of(h):
                return slabs[h // 2][2] if h // 2 in slabs else 512

            def cut_next(s):
                for h in (2 * s + 2, 2 * s + 3):
                    cut(h, 0, width_of(h))

            def evacuate(s):
                n = TURNS[s]
                jobs = slabs[s][3]
                dve.wait_ge(w_used, 2 * s + 2)
                for i in range(1, len(jobs), 2):
                    w = jobs[i][2] if jobs[i][0] == "R" else T
                    last = nc.vector.tensor_copy(jobs[i][-1], bank[4 * (n % 2) + i][:, 0:w])
                last.then_inc(evac_dve, 1)

            def norm(k, from_act=True):
                if from_act:
                    squares_seen[0] += 1
                    dve.wait_ge(squares, squares_seen[0])
                nc.vector.tensor_scalar(ms, ss, 1.0 / D, EPS, ALU.mult, ALU.add).then_inc(mean_sq, 1)
                dve.wait_ge(rooted, k + 1)
                chained(nc.vector.reciprocal(rstd, root))

            def scale_rows(k, src):
                for t in range(TT):
                    last = nc.vector.tensor_scalar(tok[:, t, :], src[:, t, :], rstd[:, t:t + 1], None, ALU.mult)
                last.then_inc(normed, 1)

            def turn_rows(k, g):
                for c in range(KC):
                    dve.wait_ge(act_hi_done, 8 * k + c - c % 2 + 2)
                    last = nc.vector.scalar_tensor_tensor(
                        out=act_lo[:, c, :], in0=bank[4 + c // 2][:, (c % 2) * T:(c % 2 + 1) * T],
                        scalar=g_col[:, 8 * g + c:8 * g + c + 1], in1=act_hi[:, c, :].bitcast(F32),
                        op0=ALU.mult, op1=ALU.subtract)
                last.then_inc(act_done, 1)

            def out_gains(s, i, r):
                dve.wait_ge(g_in[r % 2], 16 * (r // 2 + 1))
                dve.wait_ge(w_used, 2 * s + 2)
                b = 4 * (TURNS[s] % 2)
                cols = slice(512 * i, 512 * i + 512)
                nc.vector.tensor_tensor(tok[:, 1, cols], bank[b + 1][:, :], g_row[:, r % 2, cols],
                                        ALU.mult).then_inc(evac_dve, 1)
                dve.wait_ge(evac_act, TURNS[s] + 1)
                chained(nc.vector.tensor_tensor(tok[:, 0, cols], bank[b][:, :], g_row[:, r % 2, cols], ALU.mult))

            def y_gains(r):
                dve.wait_ge(g_in[r % 2], 16 * (r // 2 + 1))
                for t in range(TT):
                    chained(nc.vector.tensor_tensor(tok[:, t, :], y[:, t, :], g_row[:, r % 2, :], ALU.mult))

            def residual(r):
                for t in range(TT):
                    nc.vector.scalar_tensor_tensor(out=x_sb[:, t, :], in0=tok[:, t, :], scalar=rstd[:, t:t + 1],
                                                   in1=x_sb[:, t, :], op0=ALU.mult,
                                                   op1=ALU.add).then_inc(res_done, 1)

            def max_of(g):
                kind, h, c = GROUPS[g]
                b = g % 2
                dve.wait_ge(scored, g + 1)
                src = score_bank(g)[:, :].rearrange("p (t k) -> p t k", t=TT)
                if kind != "M":
                    slope = slopes(A_HEADS if kind == "A" else B_HEADS)[h]
                    d = dist_w if kind == "A" else dist
                    chained(nc.vector.scalar_tensor_tensor(
                        out=s_buf[:, b, :, :], in0=d[:, :, :], scalar=-slope / SCALE, in1=src,
                        op0=ALU.mult, op1=ALU.add))
                    src = s_buf[:, b, :, :]
                chained(nc.vector.reduce_max(mx[:, b, :], src, AX))
                if kind == "A":
                    ins = nc.vector.tensor_scalar(neg[:, b, :], mx[:, b, :], sink8[:, h:h + 1], -SCALE,
                                                  ALU.max, ALU.mult)
                else:
                    ins = nc.vector.tensor_scalar(neg[:, b, :], mx[:, b, :], -SCALE, None, ALU.mult)
                ins.then_inc(neg_max, 1)

            def normalise(g):
                kind, h, c = GROUPS[g]
                b = g % 2
                dve.wait_ge(exped, g + 1)
                d = den[:, b, :]
                if kind == "A":
                    chained(nc.vector.tensor_tensor(tot[:, b, :], d, e_sink[:, b, :], ALU.add))
                    d = tot[:, b, :]
                chained(nc.vector.reciprocal(inv[:, b, :], d))
                if kind == "B" and c == 1:
                    chained(nc.vector.tensor_scalar(inv_l[:, b, :], inv[:, b, :], neg_lam, None, ALU.mult))
                    dve.wait_ge(prob, g)
                    for t in range(TT):
                        last = nc.vector.scalar_tensor_tensor(
                            out=p_buf[:, b, t, :], in0=p_buf[:, b, t, :], scalar=inv_l[:, b, t:t + 1],
                            in1=p_buf[:, 1 - b, t, :], op0=ALU.mult, op1=ALU.add)
                else:
                    for t in range(TT):
                        last = nc.vector.tensor_scalar(p_buf[:, b, t, :], p_buf[:, b, t, :], inv[:, b, t:t + 1],
                                                       None, ALU.mult)
                last.then_inc(prob, 1)

            def finish_block(v):
                u, complete = block_of(GROUP_OF[v])
                if not complete:
                    return
                if GROUPS[GROUP_OF[v]][0] == "B":
                    return
                else:
                    dve.wait_ge(blk_hi, u + 1)
                    nc.vector.tensor_tensor(act_lo[:, u % 8, :], bank[4 + u % 2][:, 0:T],
                                            act_hi[:, u % 8, :].bitcast(F32), ALU.subtract).then_inc(blk_done, 1)

            def attention(phase):
                g0, g1 = PHASES[phase]
                max_of(g0)
                for g in range(g0, g1):
                    if g + 1 < g1:
                        max_of(g + 1)
                    normalise(g)
                    if g in ITEM_OF:
                        v = ITEM_OF[g]
                        if v - 2 >= 0 and GROUP_OF[v - 2] >= g0:
                            finish_block(v - 2)
                for v in (ITEM_OF[g1 - 1] - 1, ITEM_OF[g1 - 1]):
                    finish_block(v)

            def hidden(n, tiles, h):
                dve.wait_ge(silu_done, n + 1)
                dve.wait_ge(w_used, h + 4)
                for t in range(tiles):
                    last = nc.vector.tensor_tensor(hid[:, t, :], bank[2 + t][:, :], sil[:, t, :], ALU.mult)
                last.then_inc(hid_done, 1)

            def hidden_lo(n, tiles):
                dve.wait_ge(at_hi_done, n + 1)
                for t in range(tiles):
                    last = nc.vector.tensor_tensor(at_lo[:, :, t * P:(t + 1) * P],
                                                   bank[6 + t][:, :].rearrange("p (f t) -> p f t", f=FT),
                                                   at_hi[:, :, t * P:(t + 1) * P].bitcast(F32), ALU.subtract)
                last.then_inc(at_done, 1)

            def add_down(m, h):
                for i in range(4):
                    t, f = i // 2, i % 2
                    if i < 3:
                        dve.wait_ge(down_ps, 3 * m + i + 1)
                    else:
                        dve.wait_ge(w_used, h + 1)
                    dst = y[:, t, 512 * f:512 * f + 512]
                    dve.wait_ge(y_added, 4 * m + i + 1)
                    nc.vector.tensor_tensor(dst, bank[4 + f][:, :], dst, ALU.add).then_inc(y_added, 1)

            def chunk(c, turns, n, tiles, after_turn=None, after_hidden=None, down=None):
                cut(c + 2, turns)
                cut(c + 3, turns)
                hidden_lo(n - 1, tiles)
                if after_turn:
                    after_turn()
                cut(c + 4, turns)
                cut(c + 5, turns)
                hidden(n, tiles, c + 6 * turns)
                if after_hidden:
                    after_hidden()
                cut(c + 6, turns)
                if down is not None:
                    add_down(down, c + 5 + 6 * turns)
                cut(c + 7, turns)

            def first_chunk(c, n, tiles):
                cut(c + 2)
                cut(c + 3)
                hidden(n, tiles, c)
                cut(c + 4)
                cut(c + 5)

            nc.vector.memset(cell[:, 0:1], 1.0).then_inc(cell_set, 1)
            chained(nc.vector.memset(one_col[:, :], 0.0))
            nc.vector.memset(one_col[:, B_HEADS:B_HEADS + 1], 1.0)
            dve.wait_ge(g_turned, 1)
            nc.vector.tensor_copy(g_col[:, :], bank[0][:, 0:40]).then_inc(g_turned, 1)
            norm(0)
            scale_rows(0, mem_sb)
            cut(0)
            turn_rows(0, MEM_N)
            cut(1)
            norm(1)
            dve.wait_ge(turned, 4)
            scale_rows(1, x_sb)
            cut_next(0)
            evacuate(0)
            turn_rows(1, A_N)
            dve.wait_ge(consts_in, 16 * 4)
            nc.vector.tensor_scalar(sink8[:, :], sink[:, :], 1.0 / SCALE, None, ALU.mult)
            nc.vector.tensor_scalar(sub_gs, sub_g[:, :], 1.0 - LAMBDA_INIT, None, ALU.mult)
            dve.wait_ge(act_step, 1)
            nc.vector.tensor_tensor(router2[:, :, NE:2 * NE], router_sb[:, :, :],
                                    router2[:, :, 0:NE].bitcast(F32), ALU.subtract).then_inc(act_step, 1)
            dve.wait_ge(consts, 6)
            chained(nc.vector.scalar_tensor_tensor(out=dist[:, :, :], in0=dist_w[:, :, :], scalar=-1.0,
                                                   in1=dist_w[:, :, :], op0=ALU.mult, op1=ALU.max))
            chained(nc.vector.tensor_scalar(dist_w[:, :, :], dist[:, :, :], float(WINDOW), FAR, ALU.is_gt, ALU.mult))
            chained(nc.vector.tensor_tensor(dist_w[:, :, :], dist_w[:, :, :], dist[:, :, :], ALU.add))
            lam4 = lam_in[:, :, :].rearrange("p (a b) d -> p a b d", b=2)
            chained(nc.vector.tensor_tensor(lam4[:, :, 0, :], lam4[:, :, 0, :], lam4[:, :, 1, :], ALU.mult))
            nc.vector.reduce_sum(lam_s, lam4[:, :, 0, :], AX).then_inc(lam_red, 1)
            for s in A_PROJ:
                cut_next(s)
                evacuate(s)
            dve.wait_ge(lam_exp, 1)
            chained(nc.vector.tensor_tensor(neg_lam, lam_e[:, 1:2], lam_e[:, 0:1], ALU.subtract))
            chained(nc.vector.tensor_scalar(neg_lam, neg_lam, -LAMBDA_INIT, None, ALU.add))
            attention(0)
            for i, s in enumerate(A_OUT):
                cut_next(s)
                out_gains(s, i, 0)
            dve.wait_ge(out_sq, 2)
            chained(nc.vector.tensor_tensor(ss, ss4[:, 0, :], ss4[:, 1, :], ALU.add))
            norm(2, False)
            residual(0)
            norm(3)
            scale_rows(2, x_sb)
            turn_rows(2, FFN_N)

            first_chunk(FFN_H, 0, TT)
            with dve.Fori(1, NCH) as j:
                chunk(FFN_H - 2, j, j, TT, down=j - 1)
            hidden_lo(NCH - 1, TT)
            cut(FFN_H + 42)
            add_down(NCH - 1, FFN_H + 41)
            cut(FFN_H + 43)
            dve.wait_ge(y_added, 4 * NCH + 1)
            y_gains(1)
            norm(4)
            residual(1)
            norm(5)
            scale_rows(3, x_sb)
            turn_rows(3, B_N)
            for s in B_PROJ:
                cut_next(s)
                evacuate(s)
            attention(1)
            dve.wait_ge(sq_summed, B_HEADS)
            nc.vector.tensor_scalar(sub_r[:, :], bank[6][0:B_HEADS, 0:T], 1.0 / P, EPS,
                                    ALU.mult, ALU.add).then_inc(sub_ms, 1)
            dve.wait_ge(sub_root, 1)
            nc.vector.reciprocal(sub_r[:, :], sub_r[:, :]).then_inc(sub_ms, 1)
            for i in range(B_HEADS // 2):
                dve.wait_ge(sub_spread, i + 1)
                nc.vector.tensor_tensor(o_raw[:, 2 * i:2 * i + 2, :], o_raw[:, 2 * i:2 * i + 2, :],
                                        bank[i][:, :].rearrange("p (h t) -> p h t", h=2), ALU.mult).then_inc(sub_y, 1)
                dve.wait_ge(sub_hi, i + 1)
                dve.wait_ge(sub_y, i + 1)
                nc.vector.scalar_tensor_tensor(out=act_lo[:, 2 * i:2 * i + 2, :], in0=o_raw[:, 2 * i:2 * i + 2, :],
                                               scalar=sub_gs, in1=act_hi[:, 2 * i:2 * i + 2, :].bitcast(F32),
                                               op0=ALU.mult, op1=ALU.subtract).then_inc(sub_lo, 1)
            for i, s in enumerate(B_OUT):
                cut_next(s)
                out_gains(s, i, 2)
            dve.wait_ge(out_sq, 4)
            chained(nc.vector.tensor_tensor(ss, ss4[:, 0, :], ss4[:, 1, :], ALU.add))
            norm(6, False)
            residual(2)
            norm(7)
            scale_rows(4, x_sb)
            turn_rows(4, MOE_N)

            def per_expert(v):
                return v.unsqueeze(2).broadcast_to([P, TT, NE])

            dve.wait_ge(logits_ps, 1)
            nc.vector.tensor_copy(logitT[:, :], bank[2][0:2 * NE, 0:T]).then_inc(logits_sb, 1)
            dve.wait_ge(logits_ps, 2)
            logit_parts = bank[0][:, 0:TT * 2 * NE].rearrange("p (t x e) -> p x t e", t=TT, x=2)
            chained(nc.vector.tensor_copy(r_tmp, logit_parts[:, 0]))
            chained(nc.vector.tensor_tensor(logit, logit_parts[:, 1], r_tmp, ALU.add))

            def top(src, best, eq, first, mask):
                chained(nc.vector.reduce_max(best, src, AX))
                chained(nc.vector.tensor_tensor(eq, src, per_expert(best), ALU.is_equal))
                chained(nc.vector.tensor_tensor(eq, eq, rev, ALU.mult))
                chained(nc.vector.reduce_max(first, eq, AX))
                chained(nc.vector.tensor_tensor(mask, eq, per_expert(first), ALU.is_equal))

            top(logit, m1, eq1, r1, mask1)
            chained(nc.vector.scalar_tensor_tensor(out=logit2, in0=mask1, scalar=-3e38, in1=logit,
                                                   op0=ALU.mult, op1=ALU.add))
            top(logit2, m2, eq2, r2, mask2)
            nc.vector.tensor_tensor(m_d, m2, m1, ALU.subtract).then_inc(gap, 1)
            nc.vector.tensor_tensor(chosen, mask1, mask2, ALU.add).then_inc(chosen_done, 1)
            dve.wait_ge(gap_exp, 1)
            chained(nc.vector.tensor_scalar(m_den, m_e, 1.0, None, ALU.add))
            chained(nc.vector.reciprocal(g1, m_den))
            chained(nc.vector.tensor_tensor(g2, m_e, g1, ALU.mult))
            chained(nc.vector.tensor_tensor(r_tmp, mask1, per_expert(g1), ALU.mult))
            chained(nc.vector.tensor_tensor(r_tmp2, mask2, per_expert(g2), ALU.mult))
            chained(nc.vector.tensor_tensor(gates, r_tmp, r_tmp2, ALU.add))
            dve.wait_ge(pos_ps, 1)
            chained(nc.vector.tensor_copy(pos, bank[1][:, 0:TT * NE].rearrange("p (t e) -> p t e", t=TT)))
            chained(nc.vector.tensor_copy(counts, bank[1][:, TT * NE:(TT + 1) * NE]))
            chained(nc.vector.reduce_max(over_f, counts, AX))
            nc.vector.tensor_copy(over_i[:, :], over_f).then_inc(routed, 1)

            def pick_rows(dst, e, done):
                for t in range(TT):
                    col = NE * t
                    last = nc.vector.tensor_scalar(dst[:, t, :], slot_no[:, :],
                                                   rt[:, 9, :][:, bass.ds(e + col, 1)],
                                                   rt[:, 8, :][:, bass.ds(e + col, 1)], ALU.is_equal, ALU.mult)
                last.then_inc(done, 1)

            def gathered_lo(q):
                dve.wait_ge(xe_hi, q + 1)
                for i in range(2):
                    last = nc.vector.tensor_tensor(act_lo[:, 4 * i:4 * i + 4, 0:P],
                                                   bank[1 + 2 * i][:, :].rearrange("p (c t) -> p c t", c=4),
                                                   act_hi[:, 4 * i:4 * i + 4, 0:P].bitcast(F32), ALU.subtract)
                last.then_inc(xe_done, 1)

            def expert_out(h, e):
                dve.wait_ge(w_used, h + 1)
                nc.vector.tensor_copy(y_e[:, 512:1024], bank[5][:, :]).then_inc(ye_dve, 1)
                pick_rows(pick2, e, picked2)

            def add_scattered(q, e, t):
                dve.wait_ge(scattered, 2 * q + t + 1)
                dve.wait_ge(y_acc, 2 * q + t + 1)
                for f in range(2):
                    dst = y[:, t, 512 * f:512 * f + 512]
                    last = nc.vector.scalar_tensor_tensor(
                        out=dst, in0=bank[1 + 2 * f][:, :], scalar=rt[:, 7, :][:, bass.ds(e + NE * t, 1)], in1=dst,
                        op0=ALU.mult, op1=ALU.add)
                last.then_inc(y_acc, 1)

            def experts(r):
                c = MOE_H + r * ROUND_H
                n0 = NCH + r * NCH * NE
                q0 = r * NE
                pick_rows(pick, 0, picked)
                gathered_lo(q0)
                first_chunk(c, n0, 1)
                c -= 2

                def rest(e):
                    prev = not isinstance(e, int) or e >= 1
                    q = q0 + e - 1
                    chunk(c + 6, 7 * e, n0 + 7 * e + 1, 1,
                          (lambda: add_scattered(q, e - 1, 0)) if prev else None,
                          (lambda: add_scattered(q, e - 1, 1)) if prev else None)
                    with dve.Fori(2, NCH - 1) as j:
                        chunk(c, 7 * e + j, n0 + 7 * e + j, 1)
                    last = isinstance(e, int) and e == NE - 1
                    chunk(c + 36, 7 * e, n0 + 7 * e + 6, 1,
                          None if last else (lambda: pick_rows(pick, e + 1, picked)),
                          None if last else (lambda: gathered_lo(q0 + e + 1)))

                rest(0)
                with dve.Fori(1, NE - 1) as e:
                    chunk(c, 7 * e, n0 + 7 * e, 1)
                    expert_out(c + 42 * e + 5, e - 1)
                    rest(e)
                chunk(c, 7 * (NE - 1), n0 + 7 * (NE - 1), 1)
                expert_out(c + 42 * (NE - 1) + 5, NE - 2)
                rest(NE - 1)
                hidden_lo(n0 + NE * NCH - 1, 1)
                expert_out(c + ROUND_H + 1, NE - 1)
                for t in range(TT):
                    add_scattered(q0 + NE - 1, NE - 1, t)
                dve.wait_ge(y_acc, 2 * NE * (r + 1) + 1)

            experts(0)
            over = dve.value_load(over_i[0:1, 0:1], min_val=0, max_val=T)
            with dve.If(over > CAP):
                nc.vector.tensor_scalar(pos, pos, -float(CAP), None, ALU.add).then_inc(moved, 1)
                dve.wait_ge(moved, 1)
                for h in range(2):
                    cut(MOE_H + ROUND_H + h)
                experts(1)
            nc.vector.memset(over_f, 0.0).then_inc(y_final, 1)
            y_gains(4)
            norm(8)
            residual(4)

        @block.tensor
        def _(pe):
            def three(o, l_hi, l_lo, r_hi, r_lo, start, stop):
                nc.tensor.matmul(o, l_hi, r_hi, start=start, stop=False)
                nc.tensor.matmul(o, l_hi, r_lo, start=False, stop=False)
                return nc.tensor.matmul(o, l_lo, r_hi, start=False, stop=stop)

            def project(s):
                n = TURNS[s]
                if n >= 2:
                    pe.wait_ge(evac_act, n - 1)
                    pe.wait_ge(evac_dve, n - 1)
                jobs = slabs[s][3]
                for i in range(2):
                    h = 2 * s + i
                    ring = h % CUT_SLOTS
                    pe.wait_ge(cut_lo, h + 1)
                    for b, job in enumerate(jobs):
                        for a in range(4):
                            k = 4 * i + a
                            o = bank[4 * (n % 2) + b]
                            if job[0] == "T":
                                c0 = job[1]
                                lh, ll = (m[:, ring, a, c0:c0 + P] for m in (w_hi, w_lo))
                                last = three(o[:, 0:T], lh, ll, act_hi[:, k, :], act_lo[:, k, :], k == 0, k == KC - 1)
                            else:
                                _, c0, w, t, _ = job
                                last = three(o[:, 0:w], act_hi[:, k, t * P:(t + 1) * P], act_lo[:, k, t * P:(t + 1) * P],
                                             w_hi[:, ring, a, c0:c0 + w], w_lo[:, ring, a, c0:c0 + w],
                                             k == 0, k == KC - 1)
                    last.then_inc(w_used, 1)
                return last

            def turn_rows(k):
                pe.wait_ge(normed, k + 1)
                for c in range(KC):
                    for t in range(TT):
                        last = nc.tensor.transpose(bank[4 + c // 2][:, (c % 2) * T + t * P:(c % 2) * T + (t + 1) * P],
                                                   tok[:, t, c * P:(c + 1) * P], ident[:, :])
                    if c % 2 == 1:
                        last.then_inc(turned, 1)

            def scores(g):
                kind, h, c = GROUPS[g]
                if g >= 3:
                    pe.wait_ge(*((exped, g - 2) if GROUPS[g - 3][0] == "M" else (neg_max, g - 2)))
                if kind == "A":
                    kv = h // 3
                    half, q = h % 2, qT[:, h // 2, :]
                    k = kT[:, kv // 2 if kv % 2 == half else 2 + kv // 2, :]
                elif kind == "B":
                    half, q, k = c, qT[:, h, :], kT[:, h, :]
                else:
                    half, q, k = h % 2, qmT[:, h // 2, :], mkT[:, h // 2, :]
                rows = slice(half * HEAD, half * HEAD + HEAD)
                for t in range(TT):
                    last = nc.tensor.matmul(score_bank(g)[:, t * T:(t + 1) * T], q[rows, t * P:(t + 1) * P], k[rows, :],
                                            start=True, stop=True)
                last.then_inc(scored, 1)

            def turn_probs(v):
                g = GROUP_OF[v]
                pe.wait_ge(prob, g + 1)
                if v >= 2:
                    pe.wait_ge(probT, v - 1)
                for kt in range(TT):
                    for t in range(TT):
                        last = nc.tensor.transpose(bank[2 + v % 2][:, kt * T + t * P:kt * T + (t + 1) * P],
                                                   p_buf[:, g % 2, t, kt * P:(kt + 1) * P], ident[:, :])
                last.then_inc(prob_turned, 1)

            def values(v):
                g = GROUP_OF[v]
                kind, h, _ = GROUPS[g]
                u, _ = block_of(g)
                pe.wait_ge(probT, v + 1)
                if u >= 2:
                    done, n = (blk_hi, u - 1) if u - 2 >= 8 else (blk_done, u - 1)
                    pe.wait_ge(done, n)
                for kt in range(TT):
                    if kind == "A":
                        val, rows = vv[:, kt, (h // 3) * HEAD:(h // 3 + 1) * HEAD], slice((h % 2) * HEAD, (h % 2 + 1) * HEAD)
                    elif kind == "B":
                        val, rows = vv[:, kt, h * P:(h + 1) * P], slice(0, P)
                    else:
                        val, rows = mv[:, kt, h * HEAD:(h + 1) * HEAD], slice((h % 2) * HEAD, (h % 2 + 1) * HEAD)
                    last = nc.tensor.matmul(bank[4 + u % 2][rows, 0:T], val, pT[:, v % 2, kt, :],
                                            start=(kt == 0), stop=(kt == TT - 1))
                last.then_inc(pv_done, 1)

            def sum_squares(v):
                g = GROUP_OF[v]
                if GROUPS[g][0] != "B":
                    return
                h = GROUPS[g][1]
                pe.wait_ge(blk_hi, 8 + h + 1)
                nc.tensor.matmul(bank[6][0:B_HEADS, 0:T], one_col[:, B_HEADS - h:2 * B_HEADS - h], sq[:, h % 2, :],
                                 start=(h == 0), stop=(h == B_HEADS - 1)).then_inc(sq_summed, 1)

            def attention(phase):
                g0, g1 = PHASES[phase]
                for g in range(g0, g0 + 3):
                    scores(g)
                v0 = min(v for v, g in GROUP_OF.items() if g >= g0)
                for g in range(g0, g1):
                    if g + 3 < g1:
                        scores(g + 3)
                    if g in ITEM_OF:
                        v = ITEM_OF[g]
                        if v - 2 >= v0:
                            sum_squares(v - 2)
                        if v - 1 >= v0:
                            values(v - 1)
                        turn_probs(v)
                v = ITEM_OF[g1 - 1]
                values(v)
                for w in (v - 1, v):
                    sum_squares(w)

            def gate_or_up(h, c, first_bank, tiles):
                for i in range(2):
                    ring = (c + i) % CUT_SLOTS
                    pe.wait_ge(cut_lo, h + i + 1)
                    for t in range(tiles):
                        for a in range(4):
                            k = 4 * i + a
                            last = three(bank[first_bank + t][:, :], act_hi[:, k, t * P:(t + 1) * P],
                                         act_lo[:, k, t * P:(t + 1) * P], w_hi[:, ring, a, :], w_lo[:, ring, a, :],
                                         k == 0, k == KC - 1)
                    last.then_inc(w_used, 1)
                return last

            def turn_hidden(n, tiles):
                pe.wait_ge(hid_done, n + 1)
                for t in range(tiles):
                    for f in range(FT):
                        last = nc.tensor.transpose(bank[6 + t][:, f * P:(f + 1) * P], hid[:, t, f * P:(f + 1) * P],
                                                   ident[:, :])
                last.then_inc(hid_turned, 1)

            def dense_down(h, c, n):
                pe.wait_ge(at_done, n + 1)
                pe.wait_ge(cut_lo, h + 2)
                for i in range(4):
                    t, f = i // 2, i % 2
                    pe.wait_ge(y_added, 4 * n + max(i, 1))
                    for a in range(FT):
                        ring = (c + a // 2) % CUT_SLOTS
                        col = (a % 2) * D + 512 * f
                        r_hi, r_lo = (m[:, ring, :, :].rearrange("p a n -> p (a n)")[:, col:col + 512]
                                      for m in (w_hi, w_lo))
                        last = three(bank[4 + f][:, :], at_hi[:, a, t * P:(t + 1) * P], at_lo[:, a, t * P:(t + 1) * P],
                                     r_hi, r_lo, a == 0, a == FT - 1)
                        if i == 3 and a % 2 == 1:
                            last.then_inc(w_used, 1)
                    if i < 3:
                        last.then_inc(down_ps, 1)

            def expert_down(h, c, n, first, last_chunk):
                pe.wait_ge(at_done, n + 1)
                for i in range(2):
                    ring = (c + i) % CUT_SLOTS
                    pe.wait_ge(cut_lo, h + i + 1)
                    for a in range(2):
                        for f in range(2):
                            col = a * D + 512 * f
                            r_hi, r_lo = (m[:, ring, :, :].rearrange("p a n -> p (a n)")[:, col:col + 512]
                                          for m in (w_hi, w_lo))
                            last = three(bank[4 + f][:, :], at_hi[:, 2 * i + a, 0:P], at_lo[:, 2 * i + a, 0:P],
                                         r_hi, r_lo, first and i == 0 and a == 0, last_chunk and i == 1 and a == 1)
                    last.then_inc(w_used, 1)
                return last

            pe.wait_ge(consts, 6)
            pe.wait_ge(gains_in, 16 * 3)
            nc.tensor.transpose(bank[0][:, 0:40], g_rows[:, :], ident[0:40, 0:40]).then_inc(g_turned, 1)
            pe.wait_ge(g_turned, 2)
            turn_rows(0)
            pe.wait_ge(act_done, 1)
            project(0)
            turn_rows(1)
            pe.wait_ge(act_done, 2)
            for s in A_PROJ:
                project(s)
            pe.wait_ge(evac_act, TURNS[4] + 1)
            pe.wait_ge(evac_dve, TURNS[4] + 1)
            pe.wait_ge(k_swapped, 32)
            attention(0)
            pe.wait_ge(blk_done, 8)
            for s in A_OUT:
                project(s)
            turn_rows(2)
            pe.wait_ge(act_done, 3)

            gate_or_up(FFN_H, FFN_H, 0, TT)
            gate_or_up(FFN_H + 2, FFN_H + 2, 2, TT)
            with pe.Fori(1, NCH) as j:
                c = FFN_H - 2
                pe.wait_ge(silu_done, j)
                gate_or_up(c + 6 * j, c, 0, TT)
                turn_hidden(j - 1, TT)
                gate_or_up(c + 6 * j + 2, c + 2, 2, TT)
                dense_down(c + 6 * j + 4, c + 4, j - 1)
            turn_hidden(NCH - 1, TT)
            dense_down(FFN_H + 40, FFN_H + 40, NCH - 1)

            turn_rows(3)
            pe.wait_ge(act_done, 4)
            for s in B_PROJ:
                project(s)
            pe.wait_ge(evac_act, TURNS[B_PROJ[-1]] + 1)
            pe.wait_ge(evac_dve, TURNS[B_PROJ[-1]] + 1)
            attention(1)
            pe.wait_ge(blk_done, 10)
            pe.wait_ge(sub_ms, 2)
            for i in range(B_HEADS // 2):
                for f in range(2):
                    h = 2 * i + f
                    last = nc.tensor.matmul(bank[i][:, f * T:(f + 1) * T],
                                            ident[0:B_HEADS, h:h + 1].broadcast_to([B_HEADS, P]), sub_r[:, :],
                                            start=True, stop=True)
                last.then_inc(sub_spread, 1)
            pe.wait_ge(sub_lo, B_HEADS // 2)
            for s in B_OUT:
                project(s)
            turn_rows(4)
            pe.wait_ge(act_done, 5)

            pe.wait_ge(act_step, 2)
            for k in range(KC):
                for a in (act_hi, act_lo):
                    last = nc.tensor.matmul(bank[2][0:2 * NE, 0:T], router2[:, k, :], a[:, k, :],
                                            start=(k == 0 and a is act_hi), stop=(k == KC - 1 and a is act_lo))
            last.then_inc(logits_ps, 1)
            pe.wait_ge(logits_sb, 1)
            for t in range(TT):
                last = nc.tensor.transpose(bank[0][:, 2 * NE * t:2 * NE * (t + 1)], logitT[:, t * P:(t + 1) * P],
                                           ident[0:2 * NE, 0:2 * NE])
            last.then_inc(logits_ps, 1)
            pe.wait_ge(chosen_done, 1)
            ch = [rt[:, 8, NE * t:NE * t + NE] for t in range(TT)]
            nc.tensor.matmul(bank[1][:, 0:NE], before[:, :], ch[0], start=True, stop=True)
            nc.tensor.matmul(bank[1][:, NE:2 * NE], ones[:, :], ch[0], start=True, stop=False)
            nc.tensor.matmul(bank[1][:, NE:2 * NE], before[:, :], ch[1], start=False, stop=True)
            nc.tensor.matmul(bank[1][:, 2 * NE:3 * NE], ones[:, :], ch[0], start=True, stop=False)
            nc.tensor.matmul(bank[1][:, 2 * NE:3 * NE], ones[:, :], ch[1], start=False, stop=True).then_inc(pos_ps, 1)
            pe.wait_ge(rows_done, 2)

            def gather(q):
                pe.wait_ge(picked, q + 1)
                for k in range(KC):
                    for t in range(TT):
                        last = nc.tensor.matmul(bank[1 + 2 * (k // 4)][:, (k % 4) * P:(k % 4 + 1) * P],
                                                tok[:, t, k * P:(k + 1) * P], pick[:, t, :],
                                                start=(t == 0), stop=(t == TT - 1))
                last.then_inc(gathered, 1)

            def turn_pick(q):
                pe.wait_ge(picked2, q + 1)
                for t in range(TT):
                    last = nc.tensor.transpose(bank[7][:, t * P:(t + 1) * P], pick2[:, t, :], ident[:, :])
                last.then_inc(pick_ps, 1)

            def scatter(q, t):
                if t == 0:
                    pe.wait_ge(pick_T, q + 1)
                    pe.wait_ge(ye_act, q + 1)
                    pe.wait_ge(ye_dve, q + 1)
                else:
                    pe.wait_ge(y_acc, 2 * q + 2)
                for f in range(2):
                    last = nc.tensor.matmul(bank[1 + 2 * f][:, :], pickT[:, t, :], y_e[:, 512 * f:512 * f + 512],
                                            start=True, stop=True)
                last.then_inc(scattered, 1)

            def experts(r):
                c = MOE_H + r * ROUND_H
                n0 = NCH + r * NCH * NE
                q0 = r * NE
                if r >= 1:
                    pe.wait_ge(y_acc, 2 * q0 + 1)
                gather(q0)
                pe.wait_ge(xe_done, q0 + 1)
                pe.wait_ge(silu_done, n0)
                gate_or_up(c, c, 0, 1)
                gate_or_up(c + 2, c + 2, 2, 1)
                c -= 2

                def chunk(h, n, first=False, last=False, mid=None, late=None):
                    pe.wait_ge(silu_done, n)
                    gate_or_up(h, c, 0, 1)
                    turn_hidden(n - 1, 1)
                    if mid:
                        mid()
                    gate_or_up(h + 2, c + 2, 2, 1)
                    if late:
                        late()
                    expert_down(h + 4, c + 4, n - 1, first, last)

                def rest(e):
                    prev = not isinstance(e, int) or e >= 1
                    q = q0 + e - 1
                    if prev:
                        turn_pick(q)
                    chunk(c + 42 * e + 6, n0 + 7 * e + 1, True, False,
                          (lambda: scatter(q, 0)) if prev else None,
                          (lambda: scatter(q, 1)) if prev else None)
                    with pe.Fori(2, NCH - 1) as j:
                        chunk(c + 42 * e + 6 * j, n0 + 7 * e + j)
                    last = isinstance(e, int) and e == NE - 1

                    def next_rows():
                        if prev:
                            pe.wait_ge(y_acc, 2 * q + 3)
                        gather(q0 + e + 1)

                    chunk(c + 42 * e + 36, n0 + 7 * e + 6, late=None if last else next_rows)

                rest(0)
                with pe.Fori(1, NE - 1) as e:
                    pe.wait_ge(xe_done, q0 + e + 1)
                    chunk(c + 42 * e, n0 + 7 * e, last=True)
                    rest(e)
                e = NE - 1
                pe.wait_ge(xe_done, q0 + e + 1)
                chunk(c + 42 * e, n0 + 7 * e, last=True)
                rest(e)
                turn_hidden(n0 + NE * NCH - 1, 1)
                expert_down(c + ROUND_H, c + ROUND_H, n0 + NE * NCH - 1, False, True)
                turn_pick(q0 + NE - 1)
                for t in range(TT):
                    scatter(q0 + NE - 1, t)

            experts(0)
            pe.wait_ge(routed, 1)
            over = pe.value_load(over_i[0:1, 0:1], min_val=0, max_val=T)
            with pe.If(over > CAP):
                experts(1)


_INS = ['x', 'mem', 'norm_g', 'mem_norm_g', 'w_mem_kv', 'a_w_in', 'a_sink', 'a_w_out', 'b_w_in', 'b_lambda',
        'b_subln_g', 'b_w_out', 'ffn_w_gate', 'ffn_w_up', 'ffn_w_down', 'moe_w_router', 'moe_w_gate', 'moe_w_up',
        'moe_w_down']
_OUTS = [((1, T, D), 'float32')]


def kernel(**inputs):
    import numpy as _np
    import concourse.bacc as _bacc
    from concourse import mybir as _mybir
    from concourse.bass_utils import run_bass_kernel_spmd as _run

    nc = _bacc.Bacc("TRN2", target_bir_lowering=False, num_devices=1)
    arrays, args = {}, []
    for name in _INS:
        a = _np.ascontiguousarray(inputs[name])
        arrays[f"in_{name}_dram"] = a
        args.append(nc.dram_tensor(f"in_{name}_dram", a.shape, _mybir.dt.from_np(a.dtype), kind="ExternalInput").ap())
    for i, (shape, dtype) in enumerate(_OUTS):
        dt = _mybir.dt.from_np(_np.dtype(dtype))
        args.append(nc.dram_tensor(f"out_{i}_dram", shape, dt, kind="ExternalOutput").ap())
    build_encoder(nc, *args)
    r = _run(nc, [arrays], core_ids=[0])
    return r.results[0]["out_0_dram"]
```

```python
import math
from contextlib import ExitStack

import concourse.bass as bass
from concourse import mybir

F32 = mybir.dt.float32
F32R = mybir.dt.float32r
I32 = mybir.dt.int32
ACT = mybir.ActivationFunctionType
ALU = mybir.AluOpType
AX = mybir.AxisListType.X

P = 128
D = 1024
T = 256
TT = T // P
KC = D // P
HEAD = 64
MIX = 768
MEMW = 256
A_HEADS = 12
B_HEADS = 6
M_HEADS = 4
WINDOW = 128
DFF = 3584
FCH = 512
NCH = DFF // FCH
FT = FCH // P
NE = 8
EPS = 1e-6
CAP = P
LAMBDA_INIT = 0.8 - 0.6 * math.exp(-0.3)
FAR = 1e32
SCALE = HEAD ** -0.5

RAW_SLOTS = 6
EARLY = 5
CUT_SLOTS = 3

FFN_H = 14
B_SLAB = 7 + 3 * NCH
MOE_H = 2 * (B_SLAB + 7)
EARLY_H = MOE_H + RAW_SLOTS
ROUND_H = 6 * NCH * NE


def slopes(n):
    return [2.0 ** (-8.0 * (i + 1) / n) for i in range(n)]


GROUPS = ([("A", h, 0) for h in range(A_HEADS)] + [("M", h, 0) for h in range(M_HEADS)]
          + [("B", h, c) for h in range(B_HEADS) for c in range(2)] + [("M", h, 0) for h in range(M_HEADS)])
PHASES = [(0, A_HEADS + M_HEADS), (A_HEADS + M_HEADS, len(GROUPS))]
ITEM_OF = {}
for _g, (_k, _h, _c) in enumerate(GROUPS):
    if _k != "B" or _c == 1:
        ITEM_OF[_g] = len(ITEM_OF)
GROUP_OF = {v: g for g, v in ITEM_OF.items()}
PR = 4


def combines(g):
    return GROUPS[g][0] == "B" and GROUPS[g][2] == 1


def scaled_upto(g):
    return sum(not combines(i) for i in range(g + 1))


def combined_upto(g):
    return sum(combines(i) for i in range(g + 1))


def block_of(g):
    kind, h, _ = GROUPS[g]
    layer = 0 if g < PHASES[0][1] else 1
    if kind == "B":
        return 8 + h, True
    c = h // 2 if kind == "A" else 6 + h // 2
    return 8 * layer + c, h % 2 == 1


def build_encoder(nc, x, mem, norm_g, mem_norm_g, w_mem_kv, a_w_in, a_sink, a_w_out, b_w_in, b_lambda,
                  b_subln_g, b_w_out, ffn_gate, ffn_up, ffn_down, router, moe_gate, moe_up, moe_down, out):
    ctx = ExitStack()
    with ctx:
        def sb(name, shape, dt=F32):
            return ctx.enter_context(nc.sbuf_tensor(name, shape, dt))

        def sem(name):
            return ctx.enter_context(nc.semaphore(name))

        raw = sb("raw", [P, RAW_SLOTS, 4, 512])
        w_hi = sb("w_hi", [P, CUT_SLOTS, 4, 512], F32R)
        w_lo = sb("w_lo", [P, CUT_SLOTS, 4, 512], F32R)
        x_sb = sb("x_sb", [P, TT, D])
        tok = sb("tok", [P, TT, D])
        act_hi = sb("act_hi", [P, KC, T], F32R)
        act_lo = sb("act_lo", [P, KC, T], F32R)
        at_hi = sb("at_hi", [P, FT, T], F32R)
        at_lo = sb("at_lo", [P, FT, T], F32R)
        g_row = sb("g_row", [P, 2, D])
        ident = sb("ident", [P, P])
        ones = sb("ones", [P, P])
        before = sb("before", [P, P])
        slot_no = sb("slot_no", [P, P])
        ARENA = 14336
        arena = sb("arena", [P, ARENA])
        g_rows = sb("g_rows", [40, P])
        g_col = sb("g_col", [P, 40])
        router_sb = sb("router_sb", [P, KC, NE])
        router2 = sb("router2", [P, KC, 2 * NE], F32R)
        cell = sb("cell", [P, 2])
        sink = sb("sink", [P, A_HEADS])
        sink8 = sb("sink8", [P, A_HEADS])
        sub_g = sb("sub_g", [P, 1])
        small = sb("small", [P, 48])
        per_group = sb("per_group", [P, 7, PR, TT])
        rt = sb("rt", [P, 16, TT * NE])
        logitT = sb("logitT", [2 * NE, T])
        one_col = sb("one_col", [P, 12])
        pickT = sb("pickT", [P, TT, P], F32R)
        over_i = sb("over_i", [P, 1], I32)

        class Carve:
            def __init__(self):
                self.at = 0

            def __call__(self, *shape):
                n = math.prod(shape)
                v = arena[:, self.at:self.at + n]
                self.at += n
                assert self.at <= ARENA
                if len(shape) == 2:
                    v = v.rearrange("p (a b) -> p a b", a=shape[0])
                elif len(shape) == 3:
                    v = v.rearrange("p (a b c) -> p a b c", a=shape[0], b=shape[1])
                return v

        carve = Carve()
        qT = carve(6, T)
        kT = carve(6, T)
        vv = carve(TT, MIX)
        qmT = carve(2, T)
        s_buf = carve(2, TT, T)
        p_buf = carve(PR, TT, T)
        pT = carve(2, TT, T)
        o_raw = carve(6, T)
        sub_r = carve(T)[0:B_HEADS, :]
        sq = carve(2, T)
        lam_in = carve(4, HEAD)
        dist_w = carve(TT, T)
        dist = carve(TT, T)
        mkT = carve(2, T)
        mv = carve(TT, MEMW)
        junk = arena[:, 0:TT * D].rearrange("p (t d) -> p t d", t=TT)
        mem_sb = arena[:, 8192:8192 + TT * D].rearrange("p (t d) -> p t d", t=TT)
        carve = Carve()
        hid = carve(TT, FCH)
        sil = carve(TT, FCH)
        y = carve(TT, D)
        pick = hid[:, 1, 0:TT * P].rearrange("p (t c) -> p t c", t=TT)
        ye_hi, ye_lo = act_hi[:, :, P:2 * P], act_lo[:, :, P:2 * P]
        early = carve(EARLY, 4, 512)

        ss = small[:, 0:2]
        ss4 = small[:, 44:48].rearrange("p (a b) -> p a b", a=2)
        ms = small[:, 2:4]
        root = small[:, 4:6]
        rstd = small[:, 6:8]
        mx, neg, den, e_sink, inv, tot, inv_l = (per_group[:, i, :, :] for i in range(7))
        lam_s = small[:, 32:34]
        lam_e = small[:, 34:36]
        neg_lam = small[:, 36:37]
        sub_gs = small[:, 37:38]
        over_f = small[:, 42:43]
        lg = [rt[:, i, :].rearrange("p (t e) -> p t e", t=TT) for i in range(16)]
        (logit, rev, eq1, mask1, logit2, eq2, mask2, gates, chosen, pos, r_tmp, r_tmp2) = lg[:12]
        m1, m2, r1, r2, m_d, m_e, g1, g2 = (rt[:, 12 + i // 4, (i % 4) * 4:(i % 4) * 4 + TT] for i in range(8))
        m_den = rt[:, 14, 0:TT]
        counts = rt[:, 15, 0:NE]

        bank = [ctx.enter_context(nc.psum_tensor(f"bank{i}", [P, 512], F32)) for i in range(8)]

        landed = [sem(f"landed{i}") for i in range(RAW_SLOTS)]
        early_in = [sem(f"early_in{i}") for i in range(EARLY)]
        cut_hi = sem("cut_hi")
        cut_lo = sem("cut_lo")
        w_used = sem("w_used")
        x_in, mem_in, gains_in, consts_in = sem("x_in"), sem("mem_in"), sem("gains_in"), sem("consts_in")
        cell_set = sem("cell_set")
        g_in = [sem("g_in0"), sem("g_in1")]
        pool_step, consts = sem("pool_step"), sem("consts")
        dve_step = sem("dve_step")
        act_step = sem("act_step")
        g_turned = sem("g_turned")
        squares, mean_sq, rooted = sem("squares"), sem("mean_sq"), sem("rooted")
        normed, turned, act_hi_done, act_done = sem("normed"), sem("turned"), sem("act_hi_done"), sem("act_done")
        evac_act, evac_dve = sem("evac_act"), sem("evac_dve")
        res_done = sem("res_done")
        k_swapped = sem("k_swapped")
        scored, neg_max, exped, inverted = sem("scored"), sem("neg_max"), sem("exped"), sem("inverted")
        scaled0, scaled1, combined = sem("scaled0"), sem("scaled1"), sem("combined")
        prob_turned, probT, pv_done = sem("prob_turned"), sem("probT"), sem("pv_done")
        blk_hi, blk_done, sq_summed = sem("blk_hi"), sem("blk_done"), sem("sq_summed")
        sub_ms, sub_root, sub_spread = sem("sub_ms"), sem("sub_root"), sem("sub_spread")
        sub_y, sub_hi, sub_lo = sem("sub_y"), sem("sub_hi"), sem("sub_lo")
        out_sq = sem("out_sq")
        lam_red, lam_exp = sem("lam_red"), sem("lam_exp")
        silu_done, hid_done = sem("silu_done"), sem("hid_done")
        hid_turned, at_hi_done, at_done = sem("hid_turned"), sem("at_hi_done"), sem("at_done")
        last_hi, last_at = sem("last_hi"), sem("last_at")
        down_ps, y_added = sem("down_ps"), sem("y_added")
        logits_sb = sem("logits_sb")
        logits_ps, gap, gap_exp, chosen_done = sem("logits_ps"), sem("gap"), sem("gap_exp"), sem("chosen_done")
        pos_ps, routed = sem("pos_ps"), sem("routed")
        picked, gathered, xe_hi, xe_done = sem("picked"), sem("gathered"), sem("xe_hi"), sem("xe_done")
        ye_hi_done, ye_done = sem("ye_hi_done"), sem("ye_done")
        pick_ps, pick_T = sem("pick_ps"), sem("pick_T")
        scattered, y_acc = sem("scattered"), sem("y_acc")
        rows_done, moved, y_final = sem("rows_done"), sem("moved"), sem("y_final")
        stored = sem("stored")

        MEM_N, A_N, FFN_N, B_N, MOE_N = range(5)
        row_gains = [norm_g[0, 1], norm_g[0, 3], norm_g[1, 1], norm_g[1, 2], norm_g[1, 3]]

        def t_job(c0, dst):
            return ("T", c0, dst)

        def r_jobs(c0, w, dst):
            return [("R", c0, w, t, dst(t)) for t in range(TT)]

        slabs = {}
        slabs[0] = (w_mem_kv, 0, 512, [t_job(i * P, mkT[:, i, :]) for i in range(2)]
                    + r_jobs(256, 256, lambda t: mv[:, t, :]))
        slabs[1] = (a_w_in[0], MIX, 512, [t_job(i * P, kT[:, i, :]) for i in range(2)]
                    + r_jobs(256, 256, lambda t: vv[:, t, 0:256]))
        for s in range(2):
            slabs[2 + s] = (a_w_in[0], 384 * s, 384, [t_job(i * P, qT[:, 3 * s + i, :]) for i in range(3)])
        slabs[4] = (a_w_in[0], MIX + 512, 256, [t_job(i * P, qmT[:, i, :]) for i in range(2)])
        for s in range(2):
            slabs[5 + s] = (a_w_out[0], 512 * s, 512, r_jobs(0, 512, lambda t, s=s: tok[:, t, 512 * s:512 * s + 512]))
            slabs[B_SLAB + 5 + s] = (b_w_out[0], 512 * s, 512,
                                     r_jobs(0, 512, lambda t, s=s: tok[:, t, 512 * s:512 * s + 512]))
        for s in range(3):
            blocks = [4 * s + i for i in range(4)]
            slabs[B_SLAB + s] = (b_w_in[0], 512 * s, 512,
                                 [t_job(i * P, (qT[:, b, :] if b < 6 else kT[:, b - 6, :]))
                                  for i, b in enumerate(blocks)])
        slabs[B_SLAB + 3] = (b_w_in[0], 2 * MIX, 512, r_jobs(0, 512, lambda t: vv[:, t, 0:512]))
        slabs[B_SLAB + 4] = (b_w_in[0], 2 * MIX + 512, 512, r_jobs(0, 256, lambda t: vv[:, t, 512:768])
                             + [t_job(256 + i * P, qmT[:, i, :]) for i in range(2)])
        TURNS = {s: n for n, s in enumerate(sorted(slabs))}
        A_PROJ, A_OUT = [1, 2, 3, 4], [5, 6]

        def first_bank(s):
            return 4 * ((TURNS[s] + (s in A_OUT)) % 2)

        B_PROJ, B_OUT = list(range(B_SLAB, B_SLAB + 5)), [B_SLAB + 5, B_SLAB + 6]

        def raw_at(c, turns=0):
            if isinstance(turns, int) and EARLY_H <= c + 6 * turns < EARLY_H + EARLY:
                i = c + 6 * turns - EARLY_H
                return early[:, i, :, :], early_in[i], 16
            if (c + 6 * turns >= EARLY_H + EARLY) if isinstance(turns, int) else (c >= MOE_H - 2):
                c -= EARLY
            slot = c % RAW_SLOTS
            return raw[:, slot, :, :], landed[slot], 16 * (c // RAW_SLOTS + 1) + 16 * turns

        def spread_bank(i):
            return (bank[7], score_bank(len(GROUPS) - 3), score_bank(len(GROUPS) - 2))[i]

        LAST_BANKS = [(1, 3), (0, 2)]

        def turn_bank(k, c):
            return bank[(0 if k == B_N else 4) + c // 2]

        def score_bank(g):
            return bank[(2, 3, 6)[(g - PHASES[g >= PHASES[1][0]][0]) % 3]]

        block = ctx.enter_context(nc.Block())

        @block.sync
        def _(sp):
            def load(h, c, src, view=None, moe=False):
                if moe and isinstance(h, int) and EARLY_H <= h < EARLY_H + EARLY:
                    i = h - EARLY_H
                    sp.wait_ge(sub_lo, B_HEADS // 2)
                    dst, here = early[:, i, :, :], early_in[i]
                else:
                    behind = moe and not (isinstance(h, int) and h < EARLY_H)
                    slot = (c - (EARLY if behind else 0)) % RAW_SLOTS
                    if not isinstance(h, int) or h >= RAW_SLOTS:
                        first = behind and isinstance(h, int) and h < EARLY_H + EARLY + RAW_SLOTS
                        sp.wait_ge(cut_lo, h - (RAW_SLOTS - 1) - (EARLY if first else 0))
                    dst, here = raw[:, slot, :, :], landed[slot]
                if view is None:
                    dst = dst.rearrange("p a n -> p (a n)").rearrange("p (q n) -> p q n", q=2)
                else:
                    dst = dst[:, :, 0:view]
                sp.dma_start(dst, src).then_inc(here, 16)

            def load_cols(h, c, w, c0, width):
                v = w.rearrange("(k p) f -> p k f", p=P)
                for i in range(2):
                    load(h + i, c + i, v[:, 4 * i:4 * i + 4, c0:c0 + width], width)

            def load_chunk(h, c, w, j, moe=False, halves=range(2)):
                v = w.rearrange("(k p) (j f) -> j p k f", p=P, f=FCH)[j]
                for i in halves:
                    load(h + i, c + i, v[:, 4 * i:4 * i + 4, :], FCH, moe)

            def load_down(h, c, w, j, moe=False):
                v = w.rearrange("(j q p) n -> j p q n", q=FT, p=P)[j]
                for i in range(2):
                    load(h + i, c + i, v[:, 2 * i:2 * i + 2, :], None, moe)

            def load_slab(s):
                w, c0, width, _ = slabs[s]
                load_cols(2 * s, 2 * s, w, c0, width)

            sp.dma_start(g_rows[0:8, :], mem_norm_g.rearrange("(c p) -> c p", p=P)).then_inc(gains_in, 16)
            for i in range(2):
                sp.dma_start(g_rows[8 + 16 * i:24 + 16 * i, :],
                             norm_g[i, 0:4:2, :].rearrange("a (c p) -> a c p", p=P)).then_inc(gains_in, 16)
            sp.dma_start(mem_sb, mem[0].rearrange("(t p) d -> p t d", p=P)).then_inc(mem_in, 16)
            load_slab(0)
            sp.dma_start(x_sb[:, :, :], x[0].rearrange("(t p) d -> p t d", p=P)).then_inc(x_in, 16)
            for s in range(1, 7):
                load_slab(s)
            load_chunk(FFN_H, FFN_H, ffn_gate[0], 0)
            load_chunk(FFN_H + 2, FFN_H + 2, ffn_up[0], 0)
            with sp.Fori(1, NCH) as j:
                c = FFN_H - 2
                load_chunk(c + 6 * j, c, ffn_gate[0], j)
                load_chunk(c + 6 * j + 2, c + 2, ffn_up[0], j)
                load_down(c + 6 * j + 4, c + 4, ffn_down[0], j - 1)
            load_down(FFN_H + 40, FFN_H + 40, ffn_down[0], NCH - 1)
            for s in B_PROJ + B_OUT:
                load_slab(s)

            def load_experts(base):
                c = MOE_H + base
                load_chunk(c, c, moe_gate[0, 0], 0, True)
                load_chunk(c + 2, c + 2, moe_up[0, 0], 0, True)
                c -= 2

                def chunk(h, e, j, e_down, j_down):
                    load_chunk(h, c, moe_gate[0, e], j, True)
                    load_chunk(h + 2, c + 2, moe_up[0, e], j, True)
                    load_down(h + 4, c + 4, moe_down[0, e_down], j_down, True)

                if base:
                    for j in (1, 2):
                        chunk(c + 6 * j, 0, j, 0, j - 1)
                else:
                    load_chunk(c + 6, c, moe_gate[0, 0], 1, True, [0])
                    load_chunk(c + 8, c + 2, moe_up[0, 0], 1, True)
                    load_down(c + 10, c + 4, moe_down[0, 0], 0, True)
                    load_chunk(c + 12, c, moe_gate[0, 0], 2, True, [0])
                    load_chunk(c + 6, c, moe_gate[0, 0], 1, True, [1])
                    load_chunk(c + 12, c, moe_gate[0, 0], 2, True, [1])
                    load_chunk(c + 14, c + 2, moe_up[0, 0], 2, True)
                    load_down(c + 16, c + 4, moe_down[0, 0], 1, True)
                chunk(c + 18, 0, 3, 0, 2)
                with sp.Fori(4, NCH) as j:
                    chunk(c + 6 * j, 0, j, 0, j - 1)
                with sp.Fori(1, NE) as e:
                    chunk(c + 42 * e, e, 0, e - 1, NCH - 1)
                    with sp.Fori(1, NCH) as j:
                        chunk(c + 42 * e + 6 * j, e, j, e, j - 1)
                load_down(c + ROUND_H, c + ROUND_H, moe_down[0, NE - 1], NCH - 1, True)

            load_experts(0)
            sp.wait_ge(routed, 1)
            over = sp.value_load(over_i[0:1, 0:1], min_val=0, max_val=T)
            with sp.If(over > CAP):
                load_experts(ROUND_H)
            for t in range(TT):
                sp.wait_ge(res_done, 7 + t)
                sp.dma_start(out[0, t * P:(t + 1) * P, :], x_sb[:, t, :]).then_inc(stored, 16)
            sp.wait_ge(stored, 16 * TT)

        @block.gpsimd
        def _(pool):
            pool.dma_start(lam_in[:, :, :], b_lambda[0].unsqueeze(0).broadcast_to([P, 4, HEAD])).then_inc(consts_in, 16)
            pool.dma_start(sink[:, :], a_sink.broadcast_to([P, A_HEADS])).then_inc(consts_in, 16)
            pool.dma_start(sub_g[:, :], b_subln_g.rearrange("a p -> p a")).then_inc(consts_in, 16)
            pool.dma_start(router_sb[:, :, :], router[0].rearrange("(k p) e -> p k e", p=P)).then_inc(consts_in, 16)
            nc.gpsimd.memset(ident[:, :], 0.0).then_inc(pool_step, 1)
            nc.gpsimd.memset(ones[:, :], 1.0).then_inc(pool_step, 1)
            nc.gpsimd.iota(slot_no[:, :], [[1, P]], base=0, channel_multiplier=0,
                           allow_small_or_imprecise_dtypes=True).then_inc(consts, 1)
            for t in range(TT):
                nc.gpsimd.iota(rev[:, t, :], [[-1, NE]], base=NE, channel_multiplier=0,
                               allow_small_or_imprecise_dtypes=True).then_inc(consts, 1)
            nc.gpsimd.iota(dist_w[:, :, :], [[P, TT], [-1, T]], base=0, channel_multiplier=1,
                           allow_small_or_imprecise_dtypes=True).then_inc(consts, 1)
            pool.wait_ge(pool_step, 2)
            nc.gpsimd.affine_select(out=ident[:, :], in_=ident[:, :], compare_op=ALU.not_equal, fill=1.0,
                                    base=0, pattern=[[-1, P]], channel_multiplier=1).then_inc(consts, 1)
            nc.gpsimd.affine_select(out=before[:, :], in_=ones[:, :], compare_op=ALU.is_gt, fill=0.0,
                                    base=0, pattern=[[1, P]], channel_multiplier=-1).then_inc(consts, 1)
            pool.wait_ge(evac_act, TURNS[1] + 1)
            pool.wait_ge(evac_dve, TURNS[1] + 1)
            for i in range(2):
                pool.dma_start(kT[HEAD * i:HEAD * i + HEAD, 2:4, :],
                               kT[HEAD * (1 - i):HEAD * (1 - i) + HEAD, 0:2, :]).then_inc(k_swapped, 16)
            def load_gain(r):
                if r >= 2:
                    pool.wait_ge(res_done, 2 * (r - 1))
                pool.dma_start(g_row[:, r % 2, :], row_gains[r].unsqueeze(0).broadcast_to([P, D])).then_inc(g_in[r % 2], 16)

            load_gain(0)
            load_gain(1)
            def scale_probs(g):
                b = g % PR
                pool.wait_ge(inverted, scaled_upto(g))
                nc.gpsimd.tensor_scalar(p_buf[:, b, 1, :], p_buf[:, b, 1, :], inv[:, b, 1:2],
                                        None, ALU.mult).then_inc(scaled1, 1)

            def attention(phase):
                for g in range(*PHASES[phase]):
                    if not combines(g):
                        scale_probs(g)

            attention(0)
            pool.wait_ge(blk_done, 8)
            nc.gpsimd.memset(y[:, :, :], 0.0).then_inc(y_added, 1)
            load_gain(2)
            load_gain(3)
            attention(1)
            load_gain(4)
            nc.gpsimd.memset(y[:, :, :], 0.0).then_inc(y_acc, 1)
            pool.wait_ge(g_in[1], 32)
            pool.wait_ge(normed, 5 * TT)
            pool.wait_ge(turned, 20)
            for t in range(TT):
                nc.gpsimd.tensor_tensor(tok[:, t, :], tok[:, t, :], g_row[:, 1, :], ALU.mult).then_inc(rows_done, 1)

        @block.scalar
        def _(act):
            def cut(h, width=512):
                src, here, n = raw_at(h)
                ring = h % CUT_SLOTS
                act.wait_ge(here, n)
                if h >= CUT_SLOTS:
                    act.wait_ge(w_used, h - (CUT_SLOTS - 1))
                nc.scalar.activation(w_hi[:, ring, :, 0:width], src[:, :, 0:width],
                                     ACT.Copy).then_inc(cut_hi, 1)

            def cut_at(c, turns, width=512):
                src, here, n = raw_at(c, turns)
                ring = c % CUT_SLOTS
                act.wait_ge(here, n)
                act.wait_ge(w_used, c - (CUT_SLOTS - 1) + 6 * turns)
                nc.scalar.activation(w_hi[:, ring, :, 0:width], src[:, :, 0:width],
                                     ACT.Copy).then_inc(cut_hi, 1)

            def load_table(func):
                nc.scalar.activation(cell[:, 1:2], cell[:, 0:1], func)

            def width_of(h):
                return slabs[h // 2][2] if h // 2 in slabs else 512

            def cut_next(s):
                for h in (2 * s + 2, 2 * s + 3):
                    cut(h, width_of(h))

            def evacuate(s):
                jobs = slabs[s][3]
                act.wait_ge(w_used, 2 * s + 2)
                for i in range(0, len(jobs), 2):
                    dst = jobs[i][-1]
                    w = jobs[i][2] if jobs[i][0] == "R" else T
                    last = nc.scalar.activation(dst, bank[first_bank(s) + i][:, 0:w], ACT.Copy)
                last.then_inc(evac_act, 1)

            roots = [0]

            def squares_of(src, t):
                nc.scalar.activation(junk[:, t, :], src[:, t, :], ACT.Square,
                                     accum_out=ss[:, t:t + 1]).then_inc(squares, 1)

            def root_of(t0, t1):
                roots[0] += 1
                act.wait_ge(mean_sq, roots[0])
                nc.scalar.activation(root[:, t0:t1], ms[:, t0:t1], ACT.Sqrt).then_inc(rooted, 1)

            def norm(src, tiles_done=None):
                for t in range(TT):
                    if tiles_done:
                        act.wait_ge(tiles_done[0], tiles_done[1] + t)
                    squares_of(src, t)
                    root_of(t, t + 1)

            def out_squares(s, i):
                b = first_bank(s)
                act.wait_ge(w_used, 2 * s + 2)
                nc.scalar.activation(junk[:, 0, 512 * i:512 * i + 512], bank[b][:, :], ACT.Square,
                                     accum_out=ss4[:, i, 0:1]).then_inc(evac_act, 1)
                act.wait_ge(evac_dve, TURNS[s] + 1)
                nc.scalar.activation(junk[:, 1, 512 * i:512 * i + 512], bank[b + 1][:, :], ACT.Square,
                                     accum_out=ss4[:, i, 1:2]).then_inc(out_sq, 1)

            def turn_rows(k, g, blocks=range(KC)):
                for c in blocks:
                    if c % 2 == 0:
                        act.wait_ge(turned, 4 * k + c // 2 + 1)
                    last = nc.scalar.activation(act_hi[:, c, :], turn_bank(k, c)[:, (c % 2) * T:(c % 2 + 1) * T],
                                                ACT.Copy, scale=g_col[:, 8 * g + c:8 * g + c + 1])
                    last.then_inc(act_hi_done, 1)

            def exps(g):
                kind, h, _ = GROUPS[g]
                b = g % PR
                act.wait_ge(neg_max, g + 1)
                if g >= PR:
                    if g - PR in ITEM_OF:
                        act.wait_ge(prob_turned, ITEM_OF[g - PR] + 1)
                    else:
                        act.wait_ge(combined, combined_upto(g - PR + 1))
                for t in range(TT):
                    src = score_bank(g)[:, t * T:(t + 1) * T] if kind == "M" else s_buf[:, g % 2, t, :]
                    last = nc.scalar.activation(p_buf[:, b, t, :], src, ACT.Exp, bias=neg[:, b, t:t + 1],
                                                scale=SCALE, accum_out=den[:, b, t:t + 1])
                if kind == "A":
                    last = nc.scalar.activation(e_sink[:, b, :], neg[:, b, :], ACT.Exp, bias=sink[:, h:h + 1])
                last.then_inc(exped, 1)

            def copy_probT(v):
                act.wait_ge(prob_turned, v + 1)
                if v >= 2:
                    act.wait_ge(pv_done, v - 1)
                nc.scalar.activation(pT[:, v % 2, :, :].rearrange("p a b -> p (a b)"), bank[v % 2][:, :],
                                     ACT.Copy).then_inc(probT, 1)

            def finish_block(v):
                u, complete = block_of(GROUP_OF[v])
                if not complete:
                    return
                act.wait_ge(pv_done, v + 1)
                src = bank[4 + u % 2][:, 0:T]
                if GROUPS[GROUP_OF[v]][0] == "B":
                    h = u - 8
                    if h >= 2:
                        act.wait_ge(sq_summed, h - 1)
                    nc.scalar.activation(o_raw[:, h, :], src, ACT.Copy)
                    nc.scalar.activation(sq[:, h % 2, :], src, ACT.Square).then_inc(blk_hi, 1)
                else:
                    nc.scalar.activation(act_hi[:, u % 8, :], src, ACT.Copy).then_inc(blk_hi, 1)

            def attention(phase):
                g0, g1 = PHASES[phase]
                exps(g0 + 1)
                for g in range(g0, g1):
                    if g + 2 < g1:
                        exps(g + 2)
                    if g in ITEM_OF:
                        v = ITEM_OF[g]
                        copy_probT(v)
                        if v - 1 >= 0 and GROUP_OF[v - 1] >= g0:
                            finish_block(v - 1)
                    if phase == 1 and g == g1 - 3:
                        load_table(ACT.Sqrt)
                        act.wait_ge(sub_ms, 1)
                        nc.scalar.activation(sub_r[:, :], sub_r[:, :], ACT.Sqrt).then_inc(sub_root, 1)
                if phase == 0:
                    finish_block(ITEM_OF[g1 - 1])

            def sub_his(i):
                act.wait_ge(sub_y, i + 1)
                nc.scalar.activation(act_hi[:, 2 * i:2 * i + 2, :], o_raw[:, 2 * i:2 * i + 2, :], ACT.Copy,
                                     scale=sub_gs).then_inc(sub_hi, 1)

            def first_chunk(c, n, tiles):
                cut(c + 3)
                silu(n, tiles, c)
                cut(c + 4)
                cut(c + 5)

            def silu(n, tiles, h):
                act.wait_ge(w_used, h + 2)
                if not isinstance(n, int) or n >= 1:
                    act.wait_ge(hid_done, n)
                for t in range(tiles):
                    last = nc.scalar.activation(sil[:, t, :], bank[t][:, :], ACT.Silu)
                last.then_inc(silu_done, 1)

            def hi_of_hidden(t, place):
                return nc.scalar.activation(at_hi[:, :, place * P:(place + 1) * P],
                                            bank[6 + t][:, :].rearrange("p (f t) -> p f t", f=FT), ACT.Copy)

            def hidden_hi(n, tiles, place=0):
                act.wait_ge(hid_turned, n + 1)
                for t in range(tiles):
                    last = hi_of_hidden(t, place + t)
                last.then_inc(at_hi_done, 1)

            def chunk(c, turns, n, tiles, extra=None, last_cut=True):
                cut_at(c + 2, turns)
                cut_at(c + 3, turns)
                silu(n, tiles, c + 6 * turns)
                hidden_hi(n - 1, tiles)
                cut_at(c + 4, turns)
                cut_at(c + 5, turns)
                if extra:
                    extra()
                cut_at(c + 6, turns)
                if last_cut:
                    cut_at(c + 7, turns)

            act.wait_ge(cell_set, 1)
            load_table(ACT.Sqrt)
            act.wait_ge(mem_in, 16)
            norm(mem_sb)
            cut(0, width_of(0))
            act.wait_ge(g_turned, 2)
            turn_rows(0, MEM_N)
            cut(1, width_of(1))
            act.wait_ge(x_in, 16)
            norm(x_sb)
            cut_next(0)
            turn_rows(1, A_N, range(KC // 2))
            evacuate(0)
            turn_rows(1, A_N, range(KC // 2, KC))
            act.wait_ge(consts_in, 16 * 4)
            nc.scalar.activation(router2[:, :, 0:NE], router_sb[:, :, :], ACT.Copy).then_inc(act_step, 1)
            for s in A_PROJ[:-1]:
                cut_next(s)
                evacuate(s)
            act.wait_ge(lam_red, 1)
            nc.scalar.activation(lam_e, lam_s, ACT.Exp).then_inc(lam_exp, 1)
            cut_next(A_PROJ[-1])
            exps(PHASES[0][0])
            evacuate(A_PROJ[-1])
            attention(0)
            load_table(ACT.Sqrt)
            for i, s in enumerate(A_OUT):
                cut_next(s)
                out_squares(s, i)
            root_of(0, TT)
            norm(x_sb, (res_done, 1))
            load_table(ACT.Silu)
            turn_rows(2, FFN_N)

            cut(FFN_H + 2)
            first_chunk(FFN_H, 0, TT)
            with act.Fori(1, NCH - 1) as j:
                chunk(FFN_H - 2, j, j, TT)
            chunk(FFN_H - 2, NCH - 1, NCH - 1, TT, last_cut=False)
            act.wait_ge(hid_turned, NCH)
            act.wait_ge(down_ps, 3 * (NCH - 2) + 2)
            hi_of_hidden(0, 0).then_inc(last_hi, 1)
            cut(FFN_H + 41)
            act.wait_ge(w_used, FFN_H + 40)
            hi_of_hidden(1, 1).then_inc(at_hi_done, 1)
            load_table(ACT.Sqrt)
            cut(FFN_H + 42)
            act.wait_ge(y_added, 4 * NCH - 1)
            squares_of(y, 0)
            cut(FFN_H + 43)
            root_of(0, 1)
            act.wait_ge(y_added, 4 * NCH + 1)
            squares_of(y, 1)
            root_of(1, 2)
            norm(x_sb, (res_done, 3))
            load_table(ACT.Exp)
            turn_rows(3, B_N)
            for s in B_PROJ[:-1]:
                cut_next(s)
                evacuate(s)
            cut_next(B_PROJ[-1])
            exps(PHASES[1][0])
            evacuate(B_PROJ[-1])
            attention(1)
            load_table(ACT.Sqrt)
            sub_his(0)
            sub_his(1)
            finish_block(len(GROUP_OF) - 1)
            sub_his(2)
            for i, s in enumerate(B_OUT):
                cut_next(s)
                out_squares(s, i)
            root_of(0, TT)
            norm(x_sb, (res_done, 5))
            load_table(ACT.Exp)
            turn_rows(4, MOE_N)
            cut(MOE_H + 2)
            act.wait_ge(gap, 1)
            nc.scalar.activation(m_e, m_d, ACT.Exp).then_inc(gap_exp, 1)
            load_table(ACT.Silu)

            def gathered_hi(q):
                for i in range(2):
                    act.wait_ge(gathered, 2 * q + i + 1)
                    nc.scalar.activation(act_hi[:, 4 * i:4 * i + 4, 0:P],
                                         bank[1 + 2 * i][:, :].rearrange("p (c t) -> p c t", c=4),
                                         ACT.Copy).then_inc(xe_hi, 1)

            def expert_out(h):
                act.wait_ge(w_used, h + 1)
                for f in range(2):
                    nc.scalar.activation(ye_hi[:, 4 * f:4 * f + 4, :],
                                         bank[4 + f][:, :].rearrange("p (c t) -> p c t", c=4),
                                         ACT.Copy).then_inc(ye_hi_done, 1)

            def copy_pickT(q):
                act.wait_ge(pick_ps, q + 1)
                nc.scalar.activation(pickT[:, :, :].rearrange("p a b -> p (a b)"), bank[7][:, 0:T],
                                     ACT.Copy).then_inc(pick_T, 1)

            def experts(r):
                c = MOE_H + r * ROUND_H
                n0 = NCH + r * NCH * NE
                q0 = r * NE
                gathered_hi(q0)
                first_chunk(c, n0, 1)
                c -= 2

                def rest(e):
                    chunk(c + 6, 7 * e, n0 + 7 * e + 1, 1)
                    with act.Fori(2, NCH - 1) as j:
                        chunk(c, 7 * e + j, n0 + 7 * e + j, 1)
                    last = isinstance(e, int) and e == NE - 1
                    chunk(c + 36, 7 * e, n0 + 7 * e + 6, 1,
                          lambda: (copy_pickT(q0 + e), None if last else gathered_hi(q0 + e + 1)),
                          last_cut=not last)

                rest(0)
                with act.Fori(1, NE - 1) as e:
                    chunk(c, 7 * e, n0 + 7 * e, 1)
                    expert_out(c + 42 * e + 5)
                    rest(e)
                chunk(c, 7 * (NE - 1), n0 + 7 * (NE - 1), 1)
                expert_out(c + 42 * (NE - 1) + 5)
                rest(NE - 1)
                hidden_hi(n0 + NE * NCH - 1, 1, 1)
                cut(c + ROUND_H + 1)
                expert_out(c + ROUND_H + 1)

            experts(0)
            act.wait_ge(routed, 1)
            over = act.value_load(over_i[0:1, 0:1], min_val=0, max_val=T)
            with act.If(over > CAP):
                for h in range(3):
                    cut(MOE_H + ROUND_H + h)
                experts(1)
            load_table(ACT.Sqrt)
            act.wait_ge(y_final, 1)
            norm(y)

        @block.vector
        def _(dve):
            steps = [0]
            squares_seen = [0]

            def chained(ins):
                steps[0] += 1
                ins.then_inc(dve_step, 1)
                dve.wait_ge(dve_step, steps[0])

            def cut(c, turns=0, width=512):
                ring = c % CUT_SLOTS
                dve.wait_ge(cut_hi, c + 1 + 6 * turns)
                nc.vector.tensor_tensor(w_lo[:, ring, :, 0:width], raw_at(c, turns)[0][:, :, 0:width],
                                        w_hi[:, ring, :, 0:width].bitcast(F32), ALU.subtract).then_inc(cut_lo, 1)

            def width_of(h):
                return slabs[h // 2][2] if h // 2 in slabs else 512

            def cut_next(s):
                for h in (2 * s + 2, 2 * s + 3):
                    cut(h, 0, width_of(h))

            def evacuate(s):
                jobs = slabs[s][3]
                dve.wait_ge(w_used, 2 * s + 2)
                for i in range(1, len(jobs), 2):
                    w = jobs[i][2] if jobs[i][0] == "R" else T
                    last = nc.vector.tensor_copy(jobs[i][-1], bank[first_bank(s) + i][:, 0:w])
                last.then_inc(evac_dve, 1)

            roots_seen = [0]

            def mean_of(t0, t1):
                nc.vector.tensor_scalar(ms[:, t0:t1], ss[:, t0:t1], 1.0 / D, EPS,
                                        ALU.mult, ALU.add).then_inc(mean_sq, 1)

            def mean_of_squares(t):
                squares_seen[0] += 1
                dve.wait_ge(squares, squares_seen[0])
                mean_of(t, t + 1)

            def inverse_of(t0, t1):
                roots_seen[0] += 1
                dve.wait_ge(rooted, roots_seen[0])
                chained(nc.vector.reciprocal(rstd[:, t0:t1], root[:, t0:t1]))

            def norm_rows(src):
                for t in range(TT):
                    mean_of_squares(t)
                    inverse_of(t, t + 1)
                    nc.vector.tensor_scalar(tok[:, t, :], src[:, t, :], rstd[:, t:t + 1], None,
                                            ALU.mult).then_inc(normed, 1)

            def turn_rows(k, g, blocks=range(KC)):
                for c in blocks:
                    dve.wait_ge(act_hi_done, 8 * k + c - c % 2 + 2)
                    last = nc.vector.scalar_tensor_tensor(
                        out=act_lo[:, c, :], in0=turn_bank(k, c)[:, (c % 2) * T:(c % 2 + 1) * T],
                        scalar=g_col[:, 8 * g + c:8 * g + c + 1], in1=act_hi[:, c, :].bitcast(F32),
                        op0=ALU.mult, op1=ALU.subtract)
                    if c % 2 == 1:
                        last.then_inc(act_done, 1)

            def out_gains(s, i, r):
                dve.wait_ge(g_in[r % 2], 16 * (r // 2 + 1))
                dve.wait_ge(w_used, 2 * s + 2)
                b = first_bank(s)
                cols = slice(512 * i, 512 * i + 512)
                nc.vector.tensor_tensor(tok[:, 1, cols], bank[b + 1][:, :], g_row[:, r % 2, cols],
                                        ALU.mult).then_inc(evac_dve, 1)
                dve.wait_ge(evac_act, TURNS[s] + 1)
                chained(nc.vector.tensor_tensor(tok[:, 0, cols], bank[b][:, :], g_row[:, r % 2, cols], ALU.mult))

            def y_gains(r, t):
                dve.wait_ge(g_in[r % 2], 16 * (r // 2 + 1))
                chained(nc.vector.tensor_tensor(tok[:, t, :], y[:, t, :], g_row[:, r % 2, :], ALU.mult))

            def residual(t):
                nc.vector.scalar_tensor_tensor(out=x_sb[:, t, :], in0=tok[:, t, :], scalar=rstd[:, t:t + 1],
                                               in1=x_sb[:, t, :], op0=ALU.mult,
                                               op1=ALU.add).then_inc(res_done, 1)

            def add_out():
                chained(nc.vector.tensor_tensor(ss, ss4[:, 0, :], ss4[:, 1, :], ALU.add))
                mean_of(0, TT)
                inverse_of(0, TT)
                for t in range(TT):
                    residual(t)

            def add_y(r):
                mean_of_squares(0)
                y_gains(r, 1)
                inverse_of(0, 1)
                residual(0)
                mean_of_squares(1)
                inverse_of(1, 2)
                residual(1)

            def max_of(g):
                kind, h, c = GROUPS[g]
                b = g % PR
                dve.wait_ge(scored, g + 1)
                src = score_bank(g)[:, :].rearrange("p (t k) -> p t k", t=TT)
                if kind != "M":
                    slope = slopes(A_HEADS if kind == "A" else B_HEADS)[h]
                    d = dist_w if kind == "A" else dist
                    chained(nc.vector.scalar_tensor_tensor(
                        out=s_buf[:, g % 2, :, :], in0=d[:, :, :], scalar=-slope / SCALE, in1=src,
                        op0=ALU.mult, op1=ALU.add))
                    src = s_buf[:, g % 2, :, :]
                chained(nc.vector.reduce_max(mx[:, b, :], src, AX))
                if kind == "A":
                    ins = nc.vector.tensor_scalar(neg[:, b, :], mx[:, b, :], sink8[:, h:h + 1], -SCALE,
                                                  ALU.max, ALU.mult)
                else:
                    ins = nc.vector.tensor_scalar(neg[:, b, :], mx[:, b, :], -SCALE, None, ALU.mult)
                ins.then_inc(neg_max, 1)

            def normalise(g):
                kind, h, c = GROUPS[g]
                b = g % PR
                dve.wait_ge(exped, g + 1)
                d = den[:, b, :]
                if kind == "A":
                    chained(nc.vector.tensor_tensor(tot[:, b, :], d, e_sink[:, b, :], ALU.add))
                    d = tot[:, b, :]
                if not combines(g):
                    nc.vector.reciprocal(inv[:, b, :], d).then_inc(inverted, 1)
                    dve.wait_ge(inverted, scaled_upto(g))
                    nc.vector.tensor_scalar(p_buf[:, b, 0, :], p_buf[:, b, 0, :], inv[:, b, 0:1],
                                            None, ALU.mult).then_inc(scaled0, 1)
                    return
                chained(nc.vector.reciprocal(inv[:, b, :], d))
                chained(nc.vector.tensor_scalar(inv_l[:, b, :], inv[:, b, :], neg_lam, None, ALU.mult))
                dve.wait_ge(scaled0, scaled_upto(g))
                dve.wait_ge(scaled1, scaled_upto(g))
                for t in range(TT):
                    last = nc.vector.scalar_tensor_tensor(
                        out=p_buf[:, b, t, :], in0=p_buf[:, b, t, :], scalar=inv_l[:, b, t:t + 1],
                        in1=p_buf[:, (g - 1) % PR, t, :], op0=ALU.mult, op1=ALU.add)
                last.then_inc(combined, 1)

            def finish_block(v):
                u, complete = block_of(GROUP_OF[v])
                if not complete:
                    return
                if GROUPS[GROUP_OF[v]][0] == "B":
                    return
                else:
                    dve.wait_ge(blk_hi, u + 1)
                    nc.vector.tensor_tensor(act_lo[:, u % 8, :], bank[4 + u % 2][:, 0:T],
                                            act_hi[:, u % 8, :].bitcast(F32), ALU.subtract).then_inc(blk_done, 1)

            def second_cut(s):
                cut(2 * s + 3, 0, width_of(2 * s + 3))

            def attention(phase):
                last_slab = (A_PROJ, B_PROJ)[phase][-1]
                g0, g1 = PHASES[phase]
                for g in range(g0, g1):
                    normalise(g)
                    if g + 2 < g1:
                        max_of(g + 2)
                    if phase == 1 and g == g1 - 3:
                        dve.wait_ge(sq_summed, B_HEADS)
                        nc.vector.tensor_scalar(sub_r[:, :], bank[7][0:B_HEADS, 0:T], 1.0 / P, EPS,
                                                ALU.mult, ALU.add).then_inc(sub_ms, 1)
                    if phase == 1 and g == g1 - 1:
                        dve.wait_ge(sub_root, 1)
                        nc.vector.reciprocal(sub_r[:, :], sub_r[:, :]).then_inc(sub_ms, 1)
                    if g in ITEM_OF:
                        v = ITEM_OF[g]
                        if v - 2 >= 0 and GROUP_OF[v - 2] >= g0:
                            finish_block(v - 2)
                second_cut(last_slab)
                if phase == 0:
                    for v in (ITEM_OF[g1 - 1] - 1, ITEM_OF[g1 - 1]):
                        finish_block(v)

            def sub_rows(i):
                dve.wait_ge(sub_spread, i + 1)
                nc.vector.tensor_tensor(o_raw[:, 2 * i:2 * i + 2, :], o_raw[:, 2 * i:2 * i + 2, :],
                                        spread_bank(i)[:, :].rearrange("p (h t) -> p h t", h=2),
                                        ALU.mult).then_inc(sub_y, 1)

            def sub_los(i):
                dve.wait_ge(sub_hi, i + 1)
                dve.wait_ge(sub_y, i + 1)
                nc.vector.scalar_tensor_tensor(out=act_lo[:, 2 * i:2 * i + 2, :], in0=o_raw[:, 2 * i:2 * i + 2, :],
                                               scalar=sub_gs, in1=act_hi[:, 2 * i:2 * i + 2, :].bitcast(F32),
                                               op0=ALU.mult, op1=ALU.subtract).then_inc(sub_lo, 1)

            def hidden(n, tiles, h):
                dve.wait_ge(silu_done, n + 1)
                dve.wait_ge(w_used, h + 4)
                for t in range(tiles):
                    last = nc.vector.tensor_tensor(hid[:, t, :], bank[2 + t][:, :], sil[:, t, :], ALU.mult)
                last.then_inc(hid_done, 1)

            def lo_of_hidden(t, place):
                return nc.vector.tensor_tensor(at_lo[:, :, place * P:(place + 1) * P],
                                               bank[6 + t][:, :].rearrange("p (f t) -> p f t", f=FT),
                                               at_hi[:, :, place * P:(place + 1) * P].bitcast(F32), ALU.subtract)

            def hidden_lo(n, tiles, place=0):
                dve.wait_ge(at_hi_done, n + 1)
                for t in range(tiles):
                    last = lo_of_hidden(t, place + t)
                last.then_inc(at_done, 1)

            def add_down(m, h, after={}):
                for i in range(4):
                    t, f = i // 2, i % 2
                    if i < 3:
                        dve.wait_ge(down_ps, 3 * m + i + 1)
                    else:
                        dve.wait_ge(w_used, h + 1)
                    dst = y[:, t, 512 * f:512 * f + 512]
                    dve.wait_ge(y_added, 4 * m + i + 1)
                    nc.vector.tensor_tensor(dst, bank[4 + f][:, :], dst, ALU.add).then_inc(y_added, 1)
                    if i in after:
                        after[i]()

            def chunk(c, turns, n, tiles, after_turn=None, after_hidden=None, down=None, last_cut=True):
                cut(c + 2, turns)
                cut(c + 3, turns)
                hidden_lo(n - 1, tiles)
                if after_turn:
                    after_turn()
                cut(c + 4, turns)
                cut(c + 5, turns)
                hidden(n, tiles, c + 6 * turns)
                if after_hidden:
                    after_hidden()
                cut(c + 6, turns)
                if down is not None:
                    add_down(down, c + 5 + 6 * turns)
                if last_cut:
                    cut(c + 7, turns)

            def first_chunk(c, n, tiles):
                for i in range(3, 6):
                    cut(c + i)
                hidden(n, tiles, c)

            nc.vector.memset(cell[:, 0:1], 1.0).then_inc(cell_set, 1)
            chained(nc.vector.memset(one_col[:, :], 0.0))
            nc.vector.memset(one_col[:, B_HEADS:B_HEADS + 1], 1.0)
            dve.wait_ge(g_turned, 1)
            nc.vector.tensor_copy(g_col[:, :], bank[0][:, 0:40]).then_inc(g_turned, 1)
            norm_rows(mem_sb)
            cut(0)
            turn_rows(0, MEM_N)
            cut(1)
            dve.wait_ge(turned, 4)
            norm_rows(x_sb)
            cut_next(0)
            turn_rows(1, A_N, range(KC // 2))
            evacuate(0)
            turn_rows(1, A_N, range(KC // 2, KC))
            dve.wait_ge(consts_in, 16 * 4)
            nc.vector.tensor_scalar(sink8[:, :], sink[:, :], 1.0 / SCALE, None, ALU.mult)
            nc.vector.tensor_scalar(sub_gs, sub_g[:, :], 1.0 - LAMBDA_INIT, None, ALU.mult)
            dve.wait_ge(act_step, 1)
            nc.vector.tensor_tensor(router2[:, :, NE:2 * NE], router_sb[:, :, :],
                                    router2[:, :, 0:NE].bitcast(F32), ALU.subtract).then_inc(act_step, 1)
            dve.wait_ge(consts, 6)
            chained(nc.vector.scalar_tensor_tensor(out=dist[:, :, :], in0=dist_w[:, :, :], scalar=-1.0,
                                                   in1=dist_w[:, :, :], op0=ALU.mult, op1=ALU.max))
            chained(nc.vector.tensor_scalar(dist_w[:, :, :], dist[:, :, :], float(WINDOW), FAR, ALU.is_gt, ALU.mult))
            chained(nc.vector.tensor_tensor(dist_w[:, :, :], dist_w[:, :, :], dist[:, :, :], ALU.add))
            lam4 = lam_in[:, :, :].rearrange("p (a b) d -> p a b d", b=2)
            chained(nc.vector.tensor_tensor(lam4[:, :, 0, :], lam4[:, :, 0, :], lam4[:, :, 1, :], ALU.mult))
            nc.vector.reduce_sum(lam_s, lam4[:, :, 0, :], AX).then_inc(lam_red, 1)
            for s in A_PROJ[:-1]:
                cut_next(s)
                evacuate(s)
            dve.wait_ge(lam_exp, 1)
            chained(nc.vector.tensor_tensor(neg_lam, lam_e[:, 1:2], lam_e[:, 0:1], ALU.subtract))
            chained(nc.vector.tensor_scalar(neg_lam, neg_lam, -LAMBDA_INIT, None, ALU.add))

            def last_projection(s, g0):
                cut(2 * s + 2, 0, width_of(2 * s + 2))
                max_of(g0)
                max_of(g0 + 1)
                evacuate(s)

            last_projection(A_PROJ[-1], PHASES[0][0])
            attention(0)
            for i, s in enumerate(A_OUT):
                cut_next(s)
                out_gains(s, i, 0)
            dve.wait_ge(out_sq, 2)
            add_out()
            norm_rows(x_sb)
            turn_rows(2, FFN_N)

            cut(FFN_H + 2)
            first_chunk(FFN_H, 0, TT)
            with dve.Fori(1, NCH - 1) as j:
                chunk(FFN_H - 2, j, j, TT, down=j - 1)
            chunk(FFN_H - 2, NCH - 1, NCH - 1, TT, last_cut=False)

            def last_tile0():
                dve.wait_ge(last_hi, 1)
                lo_of_hidden(0, 0).then_inc(last_at, 1)

            add_down(NCH - 2, FFN_H + 39, {1: last_tile0})
            cut(FFN_H + 41)
            dve.wait_ge(at_hi_done, NCH)
            lo_of_hidden(1, 1).then_inc(at_done, 1)
            cut(FFN_H + 42)
            add_down(NCH - 1, FFN_H + 41, {1: lambda: (dve.wait_ge(y_added, 4 * NCH - 1), y_gains(1, 0))})
            dve.wait_ge(y_added, 4 * NCH + 1)
            add_y(1)
            norm_rows(x_sb)
            cut(FFN_H + 43)
            turn_rows(3, B_N)
            for s in B_PROJ[:-1]:
                cut_next(s)
                evacuate(s)
            last_projection(B_PROJ[-1], PHASES[1][0])
            attention(1)
            sub_rows(0)
            sub_rows(1)
            sub_los(0)
            sub_los(1)
            sub_rows(2)
            finish_block(len(GROUP_OF) - 1)
            sub_los(2)
            for i, s in enumerate(B_OUT):
                cut_next(s)
                out_gains(s, i, 2)
            dve.wait_ge(out_sq, 4)
            add_out()
            norm_rows(x_sb)
            turn_rows(4, MOE_N)

            def per_expert(v):
                return v.unsqueeze(2).broadcast_to([P, TT, NE])

            dve.wait_ge(logits_ps, 1)
            nc.vector.tensor_copy(logitT[:, :], bank[2][0:2 * NE, 0:T]).then_inc(logits_sb, 1)
            dve.wait_ge(logits_ps, 2)
            logit_parts = bank[0][:, 0:TT * 2 * NE].rearrange("p (t x e) -> p x t e", t=TT, x=2)
            chained(nc.vector.tensor_copy(r_tmp, logit_parts[:, 0]))
            chained(nc.vector.tensor_tensor(logit, logit_parts[:, 1], r_tmp, ALU.add))

            def top(src, best, eq, first, mask):
                chained(nc.vector.reduce_max(best, src, AX))
                chained(nc.vector.tensor_tensor(eq, src, per_expert(best), ALU.is_equal))
                chained(nc.vector.tensor_tensor(eq, eq, rev, ALU.mult))
                chained(nc.vector.reduce_max(first, eq, AX))
                chained(nc.vector.tensor_tensor(mask, eq, per_expert(first), ALU.is_equal))

            top(logit, m1, eq1, r1, mask1)
            chained(nc.vector.scalar_tensor_tensor(out=logit2, in0=mask1, scalar=-3e38, in1=logit,
                                                   op0=ALU.mult, op1=ALU.add))
            top(logit2, m2, eq2, r2, mask2)
            nc.vector.tensor_tensor(m_d, m2, m1, ALU.subtract).then_inc(gap, 1)
            nc.vector.tensor_tensor(chosen, mask1, mask2, ALU.add).then_inc(chosen_done, 1)
            dve.wait_ge(pos_ps, 1)
            chained(nc.vector.tensor_copy(pos, bank[1][:, 0:TT * NE].rearrange("p (t e) -> p t e", t=TT)))

            def pick_rows(dst, e, done):
                for t in range(TT):
                    col = NE * t
                    last = nc.vector.tensor_scalar(dst[:, t, :], slot_no[:, :],
                                                   rt[:, 9, :][:, bass.ds(e + col, 1)],
                                                   rt[:, 8, :][:, bass.ds(e + col, 1)], ALU.is_equal, ALU.mult)
                last.then_inc(done, 1)

            def gathered_lo(q):
                for i in range(2):
                    dve.wait_ge(xe_hi, 2 * q + i + 1)
                    nc.vector.tensor_tensor(act_lo[:, 4 * i:4 * i + 4, 0:P],
                                            bank[1 + 2 * i][:, :].rearrange("p (c t) -> p c t", c=4),
                                            act_hi[:, 4 * i:4 * i + 4, 0:P].bitcast(F32),
                                            ALU.subtract).then_inc(xe_done, 1)

            def expert_out(q):
                for f in range(2):
                    dve.wait_ge(ye_hi_done, 2 * q + f + 1)
                    nc.vector.tensor_tensor(ye_lo[:, 4 * f:4 * f + 4, :],
                                            bank[4 + f][:, :].rearrange("p (c t) -> p c t", c=4),
                                            ye_hi[:, 4 * f:4 * f + 4, :].bitcast(F32),
                                            ALU.subtract).then_inc(ye_done, 1)

            def add_scattered(q, e, t, banks=(1, 3)):
                dve.wait_ge(scattered, 2 * q + t + 1)
                dve.wait_ge(y_acc, 2 * q + t + 1)
                for f in range(2):
                    dst = y[:, t, 512 * f:512 * f + 512]
                    last = nc.vector.scalar_tensor_tensor(
                        out=dst, in0=bank[banks[f]][:, :], scalar=rt[:, 7, :][:, bass.ds(e + NE * t, 1)], in1=dst,
                        op0=ALU.mult, op1=ALU.add)
                last.then_inc(y_acc, 1)

            def experts(r):
                c = MOE_H + r * ROUND_H
                n0 = NCH + r * NCH * NE
                q0 = r * NE
                gathered_lo(q0)
                first_chunk(c, n0, 1)
                c -= 2

                def rest(e):
                    prev = not isinstance(e, int) or e >= 1
                    q = q0 + e - 1
                    chunk(c + 6, 7 * e, n0 + 7 * e + 1, 1,
                          (lambda: add_scattered(q, e - 1, 0)) if prev else None,
                          (lambda: add_scattered(q, e - 1, 1)) if prev else None)
                    with dve.Fori(2, NCH - 1) as j:
                        chunk(c, 7 * e + j, n0 + 7 * e + j, 1)
                    last = isinstance(e, int) and e == NE - 1

                    def next_pick(e):
                        dve.wait_ge(pick_ps, q0 + e)
                        pick_rows(pick, e, picked)

                    chunk(c + 36, 7 * e, n0 + 7 * e + 6, 1,
                          None if last else (lambda: next_pick(e + 1)),
                          None if last else (lambda: gathered_lo(q0 + e + 1)), last_cut=not last)

                rest(0)
                with dve.Fori(1, NE - 1) as e:
                    chunk(c, 7 * e, n0 + 7 * e, 1)
                    expert_out(q0 + e - 1)
                    rest(e)
                chunk(c, 7 * (NE - 1), n0 + 7 * (NE - 1), 1)
                expert_out(q0 + NE - 2)
                rest(NE - 1)
                hidden_lo(n0 + NE * NCH - 1, 1, 1)
                cut(c + ROUND_H + 1)
                expert_out(q0 + NE - 1)
                for t in range(TT):
                    add_scattered(q0 + NE - 1, NE - 1, t, LAST_BANKS[t])
                dve.wait_ge(y_acc, 2 * NE * (r + 1) + 1)

            pick_rows(pick, 0, picked)
            dve.wait_ge(gap_exp, 1)
            chained(nc.vector.tensor_scalar(m_den, m_e, 1.0, None, ALU.add))
            chained(nc.vector.reciprocal(g1, m_den))
            chained(nc.vector.tensor_tensor(g2, m_e, g1, ALU.mult))
            chained(nc.vector.tensor_tensor(r_tmp, mask1, per_expert(g1), ALU.mult))
            chained(nc.vector.tensor_tensor(r_tmp2, mask2, per_expert(g2), ALU.mult))
            chained(nc.vector.tensor_tensor(gates, r_tmp, r_tmp2, ALU.add))
            dve.wait_ge(pos_ps, 2)
            chained(nc.vector.tensor_copy(counts, bank[5][:, 0:NE]))
            chained(nc.vector.reduce_max(over_f, counts, AX))
            nc.vector.tensor_copy(over_i[:, :], over_f).then_inc(routed, 1)
            dve.wait_ge(routed, 1)
            cut(MOE_H + 2)
            over = dve.value_load(over_i[0:1, 0:1], min_val=0, max_val=T)
            experts(0)
            with dve.If(over > CAP):
                nc.vector.tensor_scalar(pos, pos, -float(CAP), None, ALU.add).then_inc(moved, 1)
                dve.wait_ge(moved, 1)
                for h in range(3):
                    cut(MOE_H + ROUND_H + h)
                pick_rows(pick, 0, picked)
                experts(1)
            nc.vector.memset(over_f, 0.0).then_inc(y_final, 1)
            y_gains(4, 0)
            add_y(4)

        @block.tensor
        def _(pe):
            def three(o, l_hi, l_lo, r_hi, r_lo, start, stop):
                nc.tensor.matmul(o, l_hi, r_hi, start=start, stop=False)
                nc.tensor.matmul(o, l_hi, r_lo, start=False, stop=False)
                return nc.tensor.matmul(o, l_lo, r_hi, start=False, stop=stop)

            def project(s, k_ready=None, between=None):
                n = TURNS[s]
                if n >= 2:
                    pe.wait_ge(evac_act, n - 1)
                    pe.wait_ge(evac_dve, n - 1)
                jobs = slabs[s][3]
                for i in range(2):
                    h = 2 * s + i
                    ring = h % CUT_SLOTS
                    if k_ready is not None:
                        pe.wait_ge(act_done, 4 * k_ready + 2 * i + 2)
                    pe.wait_ge(cut_lo, h + 1)
                    for b, job in enumerate(jobs):
                        for a in range(4):
                            k = 4 * i + a
                            o = bank[first_bank(s) + b]
                            if job[0] == "T":
                                c0 = job[1]
                                lh, ll = (m[:, ring, a, c0:c0 + P] for m in (w_hi, w_lo))
                                last = three(o[:, 0:T], lh, ll, act_hi[:, k, :], act_lo[:, k, :], k == 0, k == KC - 1)
                            else:
                                _, c0, w, t, _ = job
                                last = three(o[:, 0:w], act_hi[:, k, t * P:(t + 1) * P], act_lo[:, k, t * P:(t + 1) * P],
                                             w_hi[:, ring, a, c0:c0 + w], w_lo[:, ring, a, c0:c0 + w],
                                             k == 0, k == KC - 1)
                    last.then_inc(w_used, 1)
                    if between and i == 0:
                        between()

            def turn_rows(k):
                for t in range(TT):
                    pe.wait_ge(normed, TT * k + t + 1)
                    for c in range(KC):
                        last = nc.tensor.transpose(
                            turn_bank(k, c)[:, (c % 2) * T + t * P:(c % 2) * T + (t + 1) * P],
                            tok[:, t, c * P:(c + 1) * P], ident[:, :])
                        if t == TT - 1 and c % 2 == 1:
                            last.then_inc(turned, 1)

            def scores(g):
                kind, h, c = GROUPS[g]
                if g >= 3:
                    pe.wait_ge(*((exped, g - 2) if GROUPS[g - 3][0] == "M" else (neg_max, g - 2)))
                if kind == "A":
                    kv = h // 3
                    half, q = h % 2, qT[:, h // 2, :]
                    k = kT[:, kv // 2 if kv % 2 == half else 2 + kv // 2, :]
                elif kind == "B":
                    half, q, k = c, qT[:, h, :], kT[:, h, :]
                else:
                    half, q, k = h % 2, qmT[:, h // 2, :], mkT[:, h // 2, :]
                rows = slice(half * HEAD, half * HEAD + HEAD)
                for t in range(TT):
                    last = nc.tensor.matmul(score_bank(g)[:, t * T:(t + 1) * T], q[rows, t * P:(t + 1) * P], k[rows, :],
                                            start=True, stop=True)
                last.then_inc(scored, 1)

            def turn_probs(v):
                g = GROUP_OF[v]
                if combines(g):
                    pe.wait_ge(combined, combined_upto(g))
                else:
                    pe.wait_ge(scaled0, scaled_upto(g))
                    pe.wait_ge(scaled1, scaled_upto(g))
                if v >= 2:
                    pe.wait_ge(probT, v - 1)
                for kt in range(TT):
                    for t in range(TT):
                        last = nc.tensor.transpose(bank[v % 2][:, kt * T + t * P:kt * T + (t + 1) * P],
                                                   p_buf[:, g % PR, t, kt * P:(kt + 1) * P], ident[:, :])
                last.then_inc(prob_turned, 1)

            def values(v):
                g = GROUP_OF[v]
                kind, h, _ = GROUPS[g]
                u, _ = block_of(g)
                pe.wait_ge(probT, v + 1)
                if u >= 2:
                    done, n = (blk_hi, u - 1) if u - 2 >= 8 else (blk_done, u - 1)
                    pe.wait_ge(done, n)
                for kt in range(TT):
                    if kind == "A":
                        val, rows = vv[:, kt, (h // 3) * HEAD:(h // 3 + 1) * HEAD], slice((h % 2) * HEAD, (h % 2 + 1) * HEAD)
                    elif kind == "B":
                        val, rows = vv[:, kt, h * P:(h + 1) * P], slice(0, P)
                    else:
                        val, rows = mv[:, kt, h * HEAD:(h + 1) * HEAD], slice((h % 2) * HEAD, (h % 2 + 1) * HEAD)
                    last = nc.tensor.matmul(bank[4 + u % 2][rows, 0:T], val, pT[:, v % 2, kt, :],
                                            start=(kt == 0), stop=(kt == TT - 1))
                last.then_inc(pv_done, 1)

            def sum_squares(v):
                g = GROUP_OF[v]
                if GROUPS[g][0] != "B":
                    return
                h = GROUPS[g][1]
                pe.wait_ge(blk_hi, 8 + h + 1)
                nc.tensor.matmul(bank[7][0:B_HEADS, 0:T], one_col[:, B_HEADS - h:2 * B_HEADS - h], sq[:, h % 2, :],
                                 start=(h == 0), stop=(h == B_HEADS - 1)).then_inc(sq_summed, 1)

            def first_scores(phase):
                before_last = TURNS[(A_PROJ, B_PROJ)[phase][-2]] + 1
                pe.wait_ge(evac_act, before_last)
                pe.wait_ge(evac_dve, before_last)
                if phase == 0:
                    pe.wait_ge(k_swapped, 32)
                for g in range(PHASES[phase][0], PHASES[phase][0] + 2):
                    scores(g)

            def spread_roots(i):
                for f in range(2):
                    h = 2 * i + f
                    last = nc.tensor.matmul(spread_bank(i)[:, f * T:(f + 1) * T],
                                            ident[0:B_HEADS, h:h + 1].broadcast_to([B_HEADS, P]), sub_r[:, :],
                                            start=True, stop=True)
                last.then_inc(sub_spread, 1)

            def attention(phase):
                g0, g1 = PHASES[phase]
                scores(g0 + 2)
                v0 = min(v for v, g in GROUP_OF.items() if g >= g0)
                for g in range(g0, g1):
                    if g + 3 < g1:
                        scores(g + 3)
                    if g in ITEM_OF:
                        v = ITEM_OF[g]
                        if v - 2 >= v0:
                            sum_squares(v - 2)
                        if v - 1 >= v0:
                            values(v - 1)
                        turn_probs(v)
                if phase == 1:
                    pe.wait_ge(sub_ms, 2)
                    pe.wait_ge(exped, g1 - 1)
                    for i in range(B_HEADS // 2):
                        spread_roots(i)
                values(ITEM_OF[g1 - 1])

            def gate_or_up(h, c, first_bank, tiles, k_ready=None, rows_of=None):
                for i in range(2):
                    ring = (c + i) % CUT_SLOTS
                    if k_ready is not None:
                        pe.wait_ge(act_done, 4 * k_ready + 2 * i + 2)
                    if rows_of is not None:
                        pe.wait_ge(xe_done, 2 * rows_of + i + 1)
                    pe.wait_ge(cut_lo, h + i + 1)
                    for t in range(tiles):
                        for a in range(4):
                            k = 4 * i + a
                            last = three(bank[first_bank + t][:, :], act_hi[:, k, t * P:(t + 1) * P],
                                         act_lo[:, k, t * P:(t + 1) * P], w_hi[:, ring, a, :], w_lo[:, ring, a, :],
                                         k == 0, k == KC - 1)
                    last.then_inc(w_used, 1)
                return last

            def turn_hidden(n, tiles):
                pe.wait_ge(hid_done, n + 1)
                for t in range(tiles):
                    for f in range(FT):
                        last = nc.tensor.transpose(bank[6 + t][:, f * P:(f + 1) * P], hid[:, t, f * P:(f + 1) * P],
                                                   ident[:, :])
                last.then_inc(hid_turned, 1)

            def dense_down(h, c, n, last=False, between=None):
                if last:
                    pe.wait_ge(last_at, 1)
                else:
                    pe.wait_ge(at_done, n + 1)
                for i in range(4):
                    t, f = i // 2, i % 2
                    if last and i == 2:
                        pe.wait_ge(at_done, n + 1)
                    pe.wait_ge(y_added, 4 * n + max(i, 1))
                    for a in range(FT):
                        if i == 0 and a % 2 == 0:
                            pe.wait_ge(cut_lo, h + a // 2 + 1)
                        ring = (c + a // 2) % CUT_SLOTS
                        col = (a % 2) * D + 512 * f
                        r_hi, r_lo = (m[:, ring, :, :].rearrange("p a n -> p (a n)")[:, col:col + 512]
                                      for m in (w_hi, w_lo))
                        ins = three(bank[4 + f][:, :], at_hi[:, a, t * P:(t + 1) * P], at_lo[:, a, t * P:(t + 1) * P],
                                     r_hi, r_lo, a == 0, a == FT - 1)
                        if i == 3 and a % 2 == 1:
                            ins.then_inc(w_used, 1)
                    if i < 3:
                        ins.then_inc(down_ps, 1)
                    if between and i == 1:
                        between()

            def expert_down(h, c, n, first, last_chunk, between=None, place=0):
                pe.wait_ge(at_done, n + 1)
                for i in range(2):
                    ring = (c + i) % CUT_SLOTS
                    pe.wait_ge(cut_lo, h + i + 1)
                    for a in range(2):
                        for f in range(2):
                            col = a * D + 512 * f
                            r_hi, r_lo = (m[:, ring, :, :].rearrange("p a n -> p (a n)")[:, col:col + 512]
                                          for m in (w_hi, w_lo))
                            last = three(bank[4 + f][:, :], at_hi[:, 2 * i + a, place * P:(place + 1) * P],
                                         at_lo[:, 2 * i + a, place * P:(place + 1) * P],
                                         r_hi, r_lo, first and i == 0 and a == 0, last_chunk and i == 1 and a == 1)
                    last.then_inc(w_used, 1)
                    if between and i == 0:
                        between()

            pe.wait_ge(consts, 6)
            pe.wait_ge(gains_in, 16 * 3)
            nc.tensor.transpose(bank[0][:, 0:40], g_rows[:, :], ident[0:40, 0:40]).then_inc(g_turned, 1)
            pe.wait_ge(g_turned, 2)
            turn_rows(0)
            project(0, 0, lambda: (pe.wait_ge(act_done, 4), turn_rows(1)))
            pe.wait_ge(act_done, 8)
            for s in A_PROJ[:-1]:
                project(s)
            project(A_PROJ[-1], None, lambda: first_scores(0))
            pe.wait_ge(evac_act, TURNS[A_PROJ[-1]] + 1)
            pe.wait_ge(evac_dve, TURNS[A_PROJ[-1]] + 1)
            attention(0)
            pe.wait_ge(blk_done, 4)
            project(A_OUT[0], None, lambda: pe.wait_ge(blk_done, 8))
            project(A_OUT[1])
            turn_rows(2)

            gate_or_up(FFN_H, FFN_H, 0, TT, 2)
            gate_or_up(FFN_H + 2, FFN_H + 2, 2, TT)

            def dense_chunk(j, between=None):
                c = FFN_H - 2
                pe.wait_ge(silu_done, j)
                gate_or_up(c + 6 * j, c, 0, TT)
                turn_hidden(j - 1, TT)
                gate_or_up(c + 6 * j + 2, c + 2, 2, TT)
                dense_down(c + 6 * j + 4, c + 4, j - 1, between=between)

            with pe.Fori(1, NCH - 1) as j:
                dense_chunk(j)
            dense_chunk(NCH - 1, lambda: turn_hidden(NCH - 1, TT))
            dense_down(FFN_H + 40, FFN_H + 40, NCH - 1, last=True)

            turn_rows(3)
            for s in B_PROJ[:-1]:
                project(s, 3 if s == B_PROJ[0] else None)
            project(B_PROJ[-1], None, lambda: first_scores(1))
            pe.wait_ge(evac_act, TURNS[B_PROJ[-1]] + 1)
            pe.wait_ge(evac_dve, TURNS[B_PROJ[-1]] + 1)
            attention(1)
            pe.wait_ge(sub_lo, 2)
            project(B_OUT[0], None, lambda: (pe.wait_ge(blk_done, 10), pe.wait_ge(sub_lo, B_HEADS // 2)))
            project(B_OUT[1])
            turn_rows(4)

            pe.wait_ge(act_step, 2)
            for k in range(KC):
                if k % 2 == 0:
                    pe.wait_ge(act_done, 4 * 4 + k // 2 + 1)
                for a in (act_hi, act_lo):
                    last = nc.tensor.matmul(bank[2][0:2 * NE, 0:T], router2[:, k, :], a[:, k, :],
                                            start=(k == 0 and a is act_hi), stop=(k == KC - 1 and a is act_lo))
            last.then_inc(logits_ps, 1)
            pe.wait_ge(logits_sb, 1)
            for t in range(TT):
                last = nc.tensor.transpose(bank[0][:, 2 * NE * t:2 * NE * (t + 1)], logitT[:, t * P:(t + 1) * P],
                                           ident[0:2 * NE, 0:2 * NE])
            last.then_inc(logits_ps, 1)
            pe.wait_ge(chosen_done, 1)
            ch = [rt[:, 8, NE * t:NE * t + NE] for t in range(TT)]
            nc.tensor.matmul(bank[1][:, 0:NE], before[:, :], ch[0], start=True, stop=True)
            nc.tensor.matmul(bank[1][:, NE:2 * NE], ones[:, :], ch[0], start=True, stop=False)
            nc.tensor.matmul(bank[1][:, NE:2 * NE], before[:, :], ch[1], start=False, stop=True).then_inc(pos_ps, 1)
            nc.tensor.matmul(bank[5][:, 0:NE], ones[:, :], ch[0], start=True, stop=False)
            nc.tensor.matmul(bank[5][:, 0:NE], ones[:, :], ch[1], start=False, stop=True).then_inc(pos_ps, 1)
            pe.wait_ge(rows_done, 2)

            def gather(q):
                pe.wait_ge(picked, q + 1)
                for k in range(KC):
                    for t in range(TT):
                        last = nc.tensor.matmul(bank[1 + 2 * (k // 4)][:, (k % 4) * P:(k % 4 + 1) * P],
                                                tok[:, t, k * P:(k + 1) * P], pick[:, t, :],
                                                start=(t == 0), stop=(t == TT - 1))
                    if k % 4 == 3:
                        last.then_inc(gathered, 1)

            def turn_pick(q):
                for t in range(TT):
                    last = nc.tensor.transpose(bank[7][:, t * P:(t + 1) * P], pick[:, t, :], ident[:, :])
                last.then_inc(pick_ps, 1)

            def scatter(q, t, banks=(1, 3)):
                if t == 0:
                    pe.wait_ge(pick_T, q + 1)
                    pe.wait_ge(ye_done, 2 * q + 2)
                elif banks[0] == 1:
                    pe.wait_ge(y_acc, 2 * q + 2)
                for f in range(2):
                    nc.tensor.matmul(bank[banks[f]][:, :], pickT[:, t, :], ye_hi[:, 4 * f:4 * f + 4, :],
                                     start=True, stop=False)
                    last = nc.tensor.matmul(bank[banks[f]][:, :], pickT[:, t, :], ye_lo[:, 4 * f:4 * f + 4, :],
                                            start=False, stop=True)
                last.then_inc(scattered, 1)

            def experts(r):
                c = MOE_H + r * ROUND_H
                n0 = NCH + r * NCH * NE
                q0 = r * NE
                if r >= 1:
                    pe.wait_ge(y_acc, 2 * q0 + 1)
                gather(q0)
                pe.wait_ge(silu_done, n0)
                gate_or_up(c, c, 0, 1, rows_of=q0)
                gate_or_up(c + 2, c + 2, 2, 1)
                c -= 2

                def chunk(h, n, first=False, last=False, mid=None, late=None, rows_of=None, in_down=None):
                    pe.wait_ge(silu_done, n)
                    gate_or_up(h, c, 0, 1, rows_of=rows_of)
                    turn_hidden(n - 1, 1)
                    if mid:
                        mid()
                    gate_or_up(h + 2, c + 2, 2, 1)
                    if late:
                        late()
                    expert_down(h + 4, c + 4, n - 1, first, last, in_down)

                def rest(e):
                    prev = not isinstance(e, int) or e >= 1
                    q = q0 + e - 1
                    chunk(c + 42 * e + 6, n0 + 7 * e + 1, True, False,
                          (lambda: scatter(q, 0)) if prev else None,
                          (lambda: scatter(q, 1)) if prev else None)
                    with pe.Fori(2, NCH - 1) as j:
                        chunk(c + 42 * e + 6 * j, n0 + 7 * e + j)
                    last = isinstance(e, int) and e == NE - 1

                    def next_rows():
                        if prev:
                            pe.wait_ge(y_acc, 2 * q + 3)
                        gather(q0 + e + 1)

                    if last:
                        chunk(c + 42 * e + 36, n0 + 7 * e + 6, mid=lambda: turn_pick(q0 + e),
                              in_down=lambda: turn_hidden(n0 + 7 * e + 6, 1))
                    else:
                        chunk(c + 42 * e + 36, n0 + 7 * e + 6, mid=lambda: turn_pick(q0 + e), late=next_rows)

                rest(0)
                with pe.Fori(1, NE - 1) as e:
                    chunk(c + 42 * e, n0 + 7 * e, last=True, rows_of=q0 + e)
                    rest(e)
                e = NE - 1
                chunk(c + 42 * e, n0 + 7 * e, last=True, rows_of=q0 + e)
                rest(e)
                expert_down(c + ROUND_H, c + ROUND_H, n0 + NE * NCH - 1, False, True, place=1)
                for t in range(TT):
                    scatter(q0 + NE - 1, t, LAST_BANKS[t])

            experts(0)
            pe.wait_ge(routed, 1)
            over = pe.value_load(over_i[0:1, 0:1], min_val=0, max_val=T)
            with pe.If(over > CAP):
                experts(1)


_INS = ['x', 'mem', 'norm_g', 'mem_norm_g', 'w_mem_kv', 'a_w_in', 'a_sink', 'a_w_out', 'b_w_in', 'b_lambda',
        'b_subln_g', 'b_w_out', 'ffn_w_gate', 'ffn_w_up', 'ffn_w_down', 'moe_w_router', 'moe_w_gate', 'moe_w_up',
        'moe_w_down']
_OUTS = [((1, T, D), 'float32')]


def kernel(**inputs):
    import numpy as _np
    import concourse.bacc as _bacc
    from concourse import mybir as _mybir
    from concourse.bass_utils import run_bass_kernel_spmd as _run

    nc = _bacc.Bacc("TRN2", target_bir_lowering=False, num_devices=1)
    arrays, args = {}, []
    for name in _INS:
        a = _np.ascontiguousarray(inputs[name])
        arrays[f"in_{name}_dram"] = a
        args.append(nc.dram_tensor(f"in_{name}_dram", a.shape, _mybir.dt.from_np(a.dtype), kind="ExternalInput").ap())
    for i, (shape, dtype) in enumerate(_OUTS):
        dt = _mybir.dt.from_np(_np.dtype(dtype))
        args.append(nc.dram_tensor(f"out_{i}_dram", shape, dt, kind="ExternalOutput").ap())
    build_encoder(nc, *args)
    r = _run(nc, [arrays], core_ids=[0])
    return r.results[0]["out_0_dram"]
```
